# Optimizing a Trainium2 kernel written in Bass

```python
import math
import jax, jax.numpy as jnp
from jax import lax
import numpy as np

D_MODEL = 1024
BATCH = 1
SEQ = 256
DEPTH = 2

N_META = 16
PREFIX = 128
BLOCK_Q = 128
N_EVEN = (DEPTH + 1) // 2
N_ODD = DEPTH // 2

POOL_WINDOWS = (2, 4, 8, 16)
N_POOL = len(POOL_WINDOWS)
POOL_GROUP = D_MODEL // 8
POOL_WIDTH = N_POOL * POOL_GROUP

DIFF_HEADS = 4
DIFF_QK_DIM = D_MODEL // 16
DIFF_V_DIM = 2 * DIFF_QK_DIM
DIFF_QK_WIDTH = DIFF_HEADS * 2 * DIFF_QK_DIM
DIFF_WIDTH = DIFF_HEADS * DIFF_V_DIM

EVEN_IN = POOL_WIDTH + 2 * DIFF_QK_WIDTH + DIFF_WIDTH
EVEN_MIX = POOL_WIDTH + DIFF_WIDTH

GLA_HEADS = 4
GLA_DK = D_MODEL // 2 // GLA_HEADS
GLA_DV = D_MODEL // GLA_HEADS
GLA_RANK = 16
GLA_TAU = 16.0
GLA_CHUNK = 64
ODD_IN = 2 * GLA_HEADS * GLA_DK + 2 * GLA_HEADS * GLA_DV + GLA_RANK

N_EXPERTS = 16
N_GROUPS = 4
EXPERTS_PER_GROUP = N_EXPERTS // N_GROUPS
TOP_K = 2
D_EXPERT = 512

ALPHA = (2.0 * DEPTH) ** 0.25
BETA = (8.0 * DEPTH) ** -0.25

kernel_name = 'hybrid_pool_diffattn_gla_groupmoe_deepnorm'

def layer_norm(x, g, b, eps=1e-5):
    xf = x.astype(jnp.float32)
    mu = jnp.mean(xf, -1, keepdims=True)
    var = jnp.mean(jnp.square(xf - mu), -1, keepdims=True)
    return ((xf - mu) * lax.rsqrt(var + eps) * g.astype(jnp.float32) + b.astype(jnp.float32)).astype(x.dtype)

def rms_norm(x, w, eps=1e-6):
    xf = x.astype(jnp.float32)
    return (xf * lax.rsqrt(jnp.mean(xf * xf, -1, keepdims=True) + eps) * w.astype(jnp.float32)).astype(x.dtype)

def pooling_mixer(u, valid, w_group, scale):
    B, L, _ = u.shape
    uf = u.astype(jnp.float32) * valid[None, :, None]
    csum = jnp.cumsum(uf, axis=1)
    ccnt = jnp.cumsum(valid)
    outs = []
    for gi, w in enumerate(POOL_WINDOWS):
        c = csum[..., gi * POOL_GROUP:(gi + 1) * POOL_GROUP]
        win_sum = c - jnp.pad(c, ((0, 0), (w, 0), (0, 0)))[:, :L]
        win_cnt = ccnt - jnp.pad(ccnt, (w, 0))[:L]
        mean = win_sum / jnp.maximum(win_cnt, 1.0)[None, :, None]
        outs.append(mean - uf[..., gi * POOL_GROUP:(gi + 1) * POOL_GROUP])
    d = jnp.stack(outs, axis=2)
    y = jnp.einsum('blgc,gcd->blgd', d, w_group.astype(jnp.float32)).reshape(B, L, POOL_WIDTH)
    return (y * scale.astype(jnp.float32)).astype(u.dtype)

def diff_attention(q, k, v, valid, lam, subln_w, lambda_init):
    B, L = q.shape[:2]
    nb = L // BLOCK_Q
    slopes = 2.0 ** (-8.0 * jnp.arange(1, DIFF_HEADS + 1, dtype=jnp.float32) / DIFF_HEADS)
    kpos = jnp.arange(L)
    key_ok = valid > 0
    scale = DIFF_QK_DIM ** -0.5
    qb = q.reshape(B, nb, BLOCK_Q, DIFF_HEADS, 2, DIFF_QK_DIM).swapaxes(0, 1)

    def block(args):
        qblk, bi = args
        qpos = bi * BLOCK_Q + jnp.arange(BLOCK_Q)
        s = jnp.einsum('bqhmd,bkhmd->bhmqk', qblk, k, preferred_element_type=jnp.float32) * scale
        dist = qpos[:, None] - kpos[None, :]
        allowed = (dist >= 0) & (key_ok[None, :] | (dist == 0))
        bias = -slopes[:, None, None] * dist.astype(jnp.float32)[None]
        s = jnp.where(allowed[None, None, None], s + bias[None, :, None], -jnp.inf)
        p = jax.nn.softmax(s, axis=-1)
        pdiff = p[:, :, 0] - lam * p[:, :, 1]
        return jnp.einsum('bhqk,bkhd->bqhd', pdiff.astype(v.dtype), v)

    o = lax.map(block, (qb, jnp.arange(nb)))
    o = o.swapaxes(0, 1).reshape(B, L, DIFF_HEADS, DIFF_V_DIM)
    o = rms_norm(o, subln_w) * (1.0 - lambda_init)
    return o.reshape(B, L, DIFF_WIDTH)

def gla_chunked(q, k, v, log_a):
    B, L, H, Dk = q.shape
    Dv = v.shape[-1]
    nc = L // GLA_CHUNK

    def to_chunks(t):
        return t.reshape(B, nc, GLA_CHUNK, H, t.shape[-1]).transpose(1, 0, 3, 2, 4)

    qc, kc, vc, ac = to_chunks(q), to_chunks(k), to_chunks(v), to_chunks(log_a)
    causal = jnp.tril(jnp.ones((GLA_CHUNK, GLA_CHUNK), dtype=bool))

    def step(S, inp):
        qi, ki, vi, ai = inp
        qf, kf, vf = qi.astype(jnp.float32), ki.astype(jnp.float32), vi.astype(jnp.float32)
        b = jnp.cumsum(ai.astype(jnp.float32), axis=2)
        inter = jnp.einsum('bhtk,bhkv->bhtv', qf * jnp.exp(b), S)
        rel = b[:, :, :, None, :] - b[:, :, None, :, :]
        decay = jnp.exp(jnp.where(causal[None, None, :, :, None], rel, -jnp.inf))
        att = jnp.einsum('bhtk,bhsk,bhtsk->bhts', qf, kf, decay)
        o = inter + jnp.einsum('bhts,bhsv->bhtv', att, vf)
        b_last = b[:, :, -1:, :]
        S = jnp.exp(b_last[:, :, 0, :, None]) * S + jnp.einsum('bhsk,bhsv->bhkv', kf * jnp.exp(b_last - b), vf)
        return S, o.astype(vi.dtype)

    S0 = jnp.zeros((B, H, Dk, Dv), jnp.float32)
    _, o = lax.scan(step, S0, (qc, kc, vc, ac))
    return o.transpose(1, 0, 3, 2, 4).reshape(B, L, H, Dv)

def even_mixer(h, valid, w_in, pool_w, pool_scale, lq1, lk1, lq2, lk2, subln, w_out, lambda_init):
    B, L, _ = h.shape
    z = h @ w_in
    u_pool, q, k, v = jnp.split(z, [POOL_WIDTH, POOL_WIDTH + DIFF_QK_WIDTH, POOL_WIDTH + 2 * DIFF_QK_WIDTH], axis=-1)
    y_pool = pooling_mixer(u_pool, valid, pool_w, pool_scale)
    lam = (jnp.exp(jnp.sum(lq1.astype(jnp.float32) * lk1.astype(jnp.float32)))
           - jnp.exp(jnp.sum(lq2.astype(jnp.float32) * lk2.astype(jnp.float32))) + lambda_init)
    y_attn = diff_attention(q.reshape(B, L, DIFF_HEADS, 2, DIFF_QK_DIM),
                            k.reshape(B, L, DIFF_HEADS, 2, DIFF_QK_DIM),
                            v.reshape(B, L, DIFF_HEADS, DIFF_V_DIM),
                            valid, lam, subln, lambda_init)
    return jnp.concatenate([y_pool, y_attn], axis=-1) @ w_out

def odd_mixer(h, valid, w_in, gate_w2, gate_b, head_norm, w_out):
    B, L, _ = h.shape
    nqk = GLA_HEADS * GLA_DK
    nv = GLA_HEADS * GLA_DV
    z = h @ w_in
    q, k, v, r, g_lr = jnp.split(z, [nqk, 2 * nqk, 2 * nqk + nv, 2 * nqk + 2 * nv], axis=-1)
    g = (g_lr @ gate_w2 + gate_b).astype(jnp.float32)
    log_a = (jax.nn.log_sigmoid(g) / GLA_TAU).reshape(B, L, GLA_HEADS, GLA_DK)
    q = q.reshape(B, L, GLA_HEADS, GLA_DK) * (GLA_DK ** -0.5)
    k = k.reshape(B, L, GLA_HEADS, GLA_DK) * valid.astype(k.dtype)[None, :, None, None]
    o = gla_chunked(q, k, v.reshape(B, L, GLA_HEADS, GLA_DV), log_a)
    o = rms_norm(o, head_norm) * jax.nn.silu(r).reshape(B, L, GLA_HEADS, GLA_DV)
    return o.reshape(B, L, nv) @ w_out

def grouped_moe(h, router_w, router_bias, w_gate, w_up, w_down):
    B, L, D = h.shape
    xt = h.reshape(-1, D)
    probs = jax.nn.softmax(jnp.dot(xt, router_w, preferred_element_type=jnp.float32), axis=-1)
    sel = (probs + router_bias.astype(jnp.float32)).reshape(-1, N_GROUPS, EXPERTS_PER_GROUP)
    group_score = lax.top_k(sel, TOP_K)[0].sum(-1)
    g = jnp.argmax(group_score, axis=-1)
    sel_g = jnp.take_along_axis(sel, g[:, None, None], axis=1)[:, 0]
    _, local = lax.top_k(sel_g, TOP_K)
    idx = g[:, None] * EXPERTS_PER_GROUP + local
    w = jnp.take_along_axis(probs, idx, axis=1)
    w = w / jnp.sum(w, -1, keepdims=True)
    combine = jnp.sum(jax.nn.one_hot(idx, N_EXPERTS, dtype=jnp.float32) * w[..., None], axis=1)
    y = jnp.zeros(xt.shape, jnp.float32)
    for e in range(N_EXPERTS):
        act = jax.nn.silu(xt @ w_gate[e]) * (xt @ w_up[e])
        y = y + combine[:, e:e + 1] * (act @ w_down[e]).astype(jnp.float32)
    return y.astype(h.dtype).reshape(B, L, D)

def setup_inputs(seed: int = 0) -> dict:
    key = jax.random.key(seed)
    ks = jax.random.split(key, 32)

    def nrm(i, shape, scale):
        return jax.random.normal(ks[i], shape, jnp.float32) * scale

    ne, no = N_EVEN, N_ODD
    return {
        'x': nrm(0, (BATCH, SEQ, D_MODEL), 1.0),
        'meta': nrm(1, (N_META, D_MODEL), 1.0),
        'even_w_in': nrm(2, (ne, D_MODEL, EVEN_IN), D_MODEL ** -0.5),
        'pool_w': nrm(3, (ne, N_POOL, POOL_GROUP, POOL_GROUP), POOL_GROUP ** -0.5),
        'pool_scale': 1.0 + nrm(4, (ne, POOL_WIDTH), 0.02),
        'diff_lq1': nrm(5, (ne, DIFF_QK_DIM), 0.1),
        'diff_lk1': nrm(6, (ne, DIFF_QK_DIM), 0.1),
        'diff_lq2': nrm(7, (ne, DIFF_QK_DIM), 0.1),
        'diff_lk2': nrm(8, (ne, DIFF_QK_DIM), 0.1),
        'diff_subln': 1.0 + nrm(9, (ne, DIFF_V_DIM), 0.02),
        'even_w_out': nrm(10, (ne, EVEN_MIX, D_MODEL), EVEN_MIX ** -0.5 * BETA),
        'odd_w_in': nrm(11, (no, D_MODEL, ODD_IN), D_MODEL ** -0.5),
        'gla_gate_w2': nrm(12, (no, GLA_RANK, GLA_HEADS * GLA_DK), GLA_RANK ** -0.5),
        'gla_gate_b': nrm(13, (no, GLA_HEADS * GLA_DK), 0.1),
        'gla_head_norm': 1.0 + nrm(14, (no, GLA_DV), 0.02),
        'odd_w_out': nrm(15, (no, GLA_HEADS * GLA_DV, D_MODEL), (GLA_HEADS * GLA_DV) ** -0.5 * BETA),
        'ln_mix_g': 1.0 + nrm(16, (DEPTH, D_MODEL), 0.02),
        'ln_mix_b': nrm(17, (DEPTH, D_MODEL), 0.02),
        'ln_ffn_g': 1.0 + nrm(18, (DEPTH, D_MODEL), 0.02),
        'ln_ffn_b': nrm(19, (DEPTH, D_MODEL), 0.02),
        'router_w': nrm(20, (D_MODEL, N_EXPERTS), D_MODEL ** -0.5),
        'router_bias': nrm(21, (N_EXPERTS,), 0.01),
        'moe_w_gate': nrm(22, (DEPTH, N_EXPERTS, D_MODEL, D_EXPERT), D_MODEL ** -0.5),
        'moe_w_up': nrm(23, (DEPTH, N_EXPERTS, D_MODEL, D_EXPERT), D_MODEL ** -0.5),
        'moe_w_down': nrm(24, (DEPTH, N_EXPERTS, D_EXPERT, D_MODEL), D_EXPERT ** -0.5 * BETA),
    }

def reference(x, meta, even_w_in, pool_w, pool_scale, diff_lq1, diff_lk1, diff_lq2, diff_lk2,
              diff_subln, even_w_out, odd_w_in, gla_gate_w2, gla_gate_b, gla_head_norm, odd_w_out,
              ln_mix_g, ln_mix_b, ln_ffn_g, ln_ffn_b, router_w, router_bias,
              moe_w_gate, moe_w_up, moe_w_down):
    B = x.shape[0]
    L = PREFIX + x.shape[1]
    pad = jnp.zeros((B, PREFIX - N_META, D_MODEL), x.dtype)
    metas = jnp.broadcast_to(meta.astype(x.dtype)[None], (B, N_META, D_MODEL))
    h = jnp.concatenate([pad, metas, x], axis=1)
    valid = (jnp.arange(L) >= PREFIX - N_META).astype(jnp.float32)
    for i in range(DEPTH):
        j = i // 2
        if i % 2 == 0:
            lambda_init = 0.8 - 0.6 * math.exp(-0.3 * i)
            mix = even_mixer(h, valid, even_w_in[j], pool_w[j], pool_scale[j], diff_lq1[j], diff_lk1[j],
                             diff_lq2[j], diff_lk2[j], diff_subln[j], even_w_out[j], lambda_init)
        else:
            mix = odd_mixer(h, valid, odd_w_in[j], gla_gate_w2[j], gla_gate_b[j], gla_head_norm[j], odd_w_out[j])
        h = layer_norm(ALPHA * h + mix, ln_mix_g[i], ln_mix_b[i])
        ffn = grouped_moe(h, router_w, router_bias, moe_w_gate[i], moe_w_up[i], moe_w_down[i])
        h = layer_norm(ALPHA * h + ffn, ln_ffn_g[i], ln_ffn_b[i])
    return h[:, PREFIX:]


_drawn_inputs = setup_inputs


def setup_inputs(seed=0):
    import zlib

    import numpy as np

    out = dict(_drawn_inputs(seed))
    spreads = {}
    factors = {'pool_scale': 2.916,
     'diff_lq1': 8.0,
     'diff_lq2': 2.821,
     'diff_lk2': 4.288,
     'diff_subln': 3.346,
     'gla_gate_b': 5.823,
     'gla_head_norm': 8.0}
    for name, (base, spread) in spreads.items():
        noise = np.random.default_rng([zlib.crc32(name.encode()), seed]).standard_normal(out[name].shape)
        drawn = base * np.exp(spread * noise) if base else spread * noise
        out[name] = __import__('jax').numpy.asarray(drawn.astype(out[name].dtype))
    for name, factor in factors.items():
        out[name] = (out[name] * factor).astype(out[name].dtype)
    return out
```

```python
import math
from contextlib import ExitStack

import concourse.bass as bass
from concourse import mybir

F32 = mybir.dt.float32
BF16 = mybir.dt.bfloat16
I32 = mybir.dt.int32
ALU = mybir.AluOpType
ACT = mybir.ActivationFunctionType
AX = mybir.AxisListType

P = 128
D = 1024
KC = D // P
SEQ = 256
N_META = 16
T = N_META + SEQ
C0 = (N_META, N_META + P, 0)
ROWS = (P, P, N_META)
HEADS = 4
WINDOWS = (2, 4, 8, 16)
QK_DIM = 64
ATT_SCALE = QK_DIM ** -0.5
SLOPES = [2.0 ** (-8.0 * (h + 1) / HEADS) for h in range(HEADS)]
LAMBDA_INIT = 0.8 - 0.6 * math.exp(0.0)
NEG = -1e30
GLA_DV = D // HEADS
GLA_SCALE = float(P) ** -0.5
GLA_TAU = 16.0
GLA_RANK = 16
LEVELS = (64, 32, 16, 8, 4, 2, 1)
DEPTH = 2
ALPHA = (2.0 * DEPTH) ** 0.25
E = 16
GRP = 4
NG = E // GRP
SLOTS = 64
CAP = SLOTS
NR = 6
UNIT = 4096
GROUP_UNITS = 3 * GRP
BASE_MOE = (6, 6 + NG * GROUP_UNITS + 8)
BASE_ODD = BASE_MOE[0] + NG * GROUP_UNITS


def hybrid_trunk(nc, x, meta, even_w_in, pool_w, pool_scale, diff_lq1, diff_lk1, diff_lq2, diff_lk2,
                 diff_subln, even_w_out, odd_w_in, gla_gate_w2, gla_gate_b, gla_head_norm, odd_w_out,
                 ln_mix_g, ln_mix_b, ln_ffn_g, ln_ffn_b, router_w, router_bias,
                 moe_w_gate, moe_w_up, moe_w_down, out):
    with ExitStack() as ctx:
        def sb(name, shape, dt=F32):
            return ctx.enter_context(nc.sbuf_tensor(name, shape, dt))

        def sem(name):
            return ctx.enter_context(nc.semaphore(name))

        def per_layer(name):
            return [sem(f"{name}{layer}") for layer in range(DEPTH)]

        bank = ctx.enter_context(nc.psum_tensor("bank", [P, 8, 512], F32))

        ring = sb("ring", [P, NR, UNIT])
        htok = sb("htok", [P, 3, D])
        hT = sb("hT", [P, KC, T])
        gain = sb("gain", [P, 2, D])
        ident = sb("ident", [P, P])
        ones_bf = sb("ones_bf", [P, P], BF16)
        before_bf = sb("before_bf", [P, P], BF16)
        dist = sb("dist", [P, 3, T])
        iota_slot = sb("iota_slot", [P, SLOTS])
        iota_e = sb("iota_e", [P, E])
        iota_i = sb("iota_i", [P, T], I32)
        row_i = sb("row_i", [P, P], I32)
        level_mask = sb("level_mask", [P, len(LEVELS) + 1, P], I32)
        small = sb("small", [P, 32])
        rw = sb("rw", [P, KC, E])
        rbias = sb("rbias", [P, E])
        sub_b = sb("sub_b", [P, P])
        stats = sb("stats", [P, 3, 2, 6])
        mv = sb("mv", [P, 3, 2])
        rstd = sb("rstd", [P, 3, 1])
        lgT = sb("lgT", [E, T])
        lg = sb("lg", [P, 3, E])
        pr = sb("pr", [P, 3, E])
        sel = sb("sel", [P, 3, E])
        hi = sb("hi", [P, 3, 4, 2])
        lo = sb("lo", [P, 3, 4, 2])
        gs = sb("gs", [P, 3, 4])
        g2 = sb("g2", [P, 3, 4])
        r1 = sb("r1", [P, 3, 1])
        r2 = sb("r2", [P, 3, 1])
        t1 = sb("t1", [P, 3, E])
        t2 = sb("t2", [P, 3, E])
        picked = sb("picked", [P, 3, E])
        picked_bf = sb("picked_bf", [P, 3, E], BF16)
        weight = sb("weight", [P, 3, E])
        late_w = sb("late_w", [P, 3, E])
        slot_of = sb("slot_of", [P, 3, E])
        over = sb("over", [P, 2])
        over_i = sb("over_i", [P, 1], I32)

        SCR = 16000
        scratch = sb("scratch", [P, SCR])

        class Cut:
            def __init__(self):
                self.at = 0

            def __call__(self, *shape):
                n = 1
                for s in shape:
                    n *= s
                v = scratch[:, self.at:self.at + n]
                self.at += n
                assert self.at <= SCR, self.at
                if len(shape) == 2:
                    v = v.rearrange("p (a b) -> p a b", b=shape[1])
                if len(shape) == 3:
                    v = v.rearrange("p (a b c) -> p a b c", b=shape[1], c=shape[2])
                return v

        cut = Cut()
        PADW = N_META + T
        zpool = cut(4, PADW)
        poolA = cut(4, PADW)
        poolB = cut(4, PADW)
        pcount = cut(4, T)
        zq = cut(4, T)
        zk = cut(4, T)
        v0 = cut(3, 512)
        yT = cut(8, T)
        s_sb = cut(2, 2, T)
        pd = cut(2, T)
        pT = cut(2, 3, P)
        o_tok = cut(3, 512)
        pw_sb = cut(4, P)
        sq0 = cut(P)
        lam_v = cut(4, QK_DIM)
        lam_t = cut(2, QK_DIM)
        ss0 = cut(12)
        mx = cut(12, 2)
        sums = cut(12, 2)
        rs = cut(12, 2)
        rstd0 = cut(12)
        cut = Cut()
        qT = cut(4, SEQ)
        kT = cut(4, T)
        bT = cut(4, T)
        la = cut(4, T)
        vt = cut(3, D)
        rt = cut(2, D)
        dec = cut(4, SEQ)
        ql = cut(4, SEQ)
        kl = cut(4, SEQ)
        att = cut(8, P)
        att01 = cut(4, P)
        ss1 = cut(8)
        rstd1 = cut(8)
        glr = cut(T)
        hn_b = cut(GLA_DV)
        g2w = cut(512)
        gb_sb = cut(4)
        glw = cut(KC, GLA_RANK)
        at = Cut()
        og = at(2, D)
        at.at = 1024 + 1088
        attM = at(4, SEQ)
        at.at = 1024 + 3 * 1088 + 3 * D + 2 * D
        ogT = at(8, SEQ)
        cut = Cut()
        yacc = cut(3, D)
        xg = cut(KC, GRP * SLOTS)
        onehot = cut(3, GRP * SLOTS)
        whot = cut(3, GRP * SLOTS)
        act_sb = cut(2, 512)
        actT = cut(4, P)
        o_sb = cut(D)
        whotT = cut(T)
        late_act = cut(T)
        late_g = cut(KC, P)
        late_u = cut(KC, P)
        late_d = cut(D)

        eps_ln, eps_rms, lam1, lam2, nlam, one = (small[:, i:i + 1] for i in range(6))

        ring_in = [sem(f"ring_in{i}") for i in range(NR)]
        x_in, meta_in, par_in, par1_in, gain_in = (sem(n) for n in ("x_in", "meta_in", "par_in", "par1_in", "gain_in"))
        dve_c, act_c, pool_c = sem("dve_c"), sem("act_c"), sem("pool_c")
        const_ok, lvl_ok = sem("const_ok"), sem("lvl_ok")
        hT_pe, hT_dve, hT_act = sem("hT_pe"), sem("hT_dve"), sem("hT_act")
        h_ready = sem("h_ready")
        pj0_pe, pj0_dve, pj0_act = sem("pj0_pe"), sem("pj0_dve"), sem("pj0_act")
        pj1_pe, pj1_dve, pj1_act = sem("pj1_pe"), sem("pj1_dve"), sem("pj1_act")
        out0, out1 = (pj0_dve, pj0_act), (pj1_dve, pj1_act)
        pooled, poolmm, poolev = sem("pooled"), sem("poolmm"), sem("poolev")
        lam_e, lam_s = sem("lam_e"), sem("lam_s")
        at_s, at_b, at_m, at_e, at_pd = sem("at_s"), sem("at_b"), sem("at_m"), sem("at_e"), sem("at_pd")
        at_t, at_te, at_o, at_oe = sem("at_t"), sem("at_te"), sem("at_o"), sem("at_oe")
        o_ss, o_rs, o_n = sem("o_ss"), sem("o_rs"), sem("o_n")
        yt_pe, yt_ev = sem("yt_pe"), sem("yt_ev")
        mix_pe, mix_dve = sem("mix_pe"), sem("mix_dve")
        var_ok, sd_ok = sem("var_ok"), sem("sd_ok")
        lgt_pe, lgt_ev, lg_pe, lg_ev = sem("lgt_pe"), sem("lgt_ev"), sem("lg_pe"), sem("lg_ev")
        lg_max, lg_exp, pick_ok, pos_pe, route_ok = (sem(n) for n in ("lg_max", "lg_exp", "pick_ok", "pos_pe", "route_ok"))
        slot_ok, flag_ok = sem("slot_ok"), sem("flag_ok")
        yinit = sem("yinit")
        s_ready, sw_ready = per_layer("s_ready"), per_layer("sw_ready")
        gth_pe, gth_ev = per_layer("gth_pe"), per_layer("gth_ev")
        gate_pe, up_pe, silu_ok, act_ok = per_layer("gate_pe"), per_layer("up_pe"), per_layer("silu_ok"), per_layer("act_ok")
        t_pe, t_ev, w_pe, w_ev = per_layer("t_pe"), per_layer("t_ev"), per_layer("w_pe"), per_layer("w_ev")
        d_pe, d_ev, sc_pe, sc_ev = per_layer("d_pe"), per_layer("d_ev"), per_layer("sc_pe"), per_layer("sc_ev")
        gla_ga, gla_ab, gla_e, gla_ln, gla_b = (sem(n) for n in ("gla_ga", "gla_ab", "gla_e", "gla_ln", "gla_b"))
        lv_d, lv_e, lv_q, lv_k, lv_pe, lv_ev = (sem(n) for n in ("lv_d", "lv_e", "lv_q", "lv_k", "lv_pe", "lv_ev"))
        go_pe, go_ev, rg_s, rg_ok, ogt_ok, ogt_pe, ogt_ev = (sem(n) for n in (
            "go_pe", "go_ev", "rg_s", "rg_ok", "ogt_ok", "ogt_pe", "ogt_ev"))
        stored = sem("stored")
        late_in = per_layer("late_in")
        lt_g, lt_u, lt_s, lt_m, lt_pe, lt_ev = (per_layer(n) for n in ("lt_g", "lt_u", "lt_s", "lt_m", "lt_pe", "lt_ev"))

        block = ctx.enter_context(nc.Block())

        def in_unit(w, n):
            return w[0][:, 512 * n:512 * (n + 1)].rearrange("(kc p) n -> p kc n", p=P)

        def unit(n):
            return ring[:, n % NR, :].rearrange("p (kc n) -> p kc n", kc=KC)

        def arrived(eng, n):
            eng.wait_ge(ring_in[n % NR], 16 * (n // NR + 1))


        J0 = [("T", n) for n in range(12)] + [("V", tt) for tt in (2, 0, 1)]
        J1 = ([("G", 0)] + [("A", h) for h in range(4)] + [("Q", h) for h in range(4)] + [("K", h) for h in range(4)]
              + [("V", (n, tt)) for n in range(2) for tt in (2, 0, 1)] + [("R", (n, tt)) for n in range(2) for tt in (0, 1)])

        def job_out(eng, jobs, sems, n):
            if jobs[n][0] == "A":
                eng.wait_ge(gla_ga, jobs[n][1] + 1)
            else:
                eng.wait_ge(sems[n % 2], len([m for m in range(n % 2, n + 1, 2) if jobs[m][0] != "A"]))

        def halves(v, w):
            return v.rearrange("p h (m t) -> p h m t", t=2 * w)

        def key_factors(eng, lv):
            w = LEVELS[lv]
            eng.wait_ge(lv_e, lv + 1)
            if lv == 0:
                job_out(eng, J1, out1, 11)
                job_out(eng, J1, out1, 12)
                eng.wait_ge(lv_k, 1)
            else:
                eng.wait_ge(lv_pe, 2 * lv)
            eng.tensor_tensor(halves(kl, w)[:, :, :, 0:w], halves(kT[:, :, N_META:T], w)[:, :, :, 0:w],
                              halves(dec, w)[:, :, :, 0:w], ALU.mult).then_inc(lv_k, 1)

        def late(eng, layer):
            L = layer
            tiles = ((2, 0, 1), (0, 1))[layer]
            nt = len(tiles)
            c = 0 if layer == 0 else N_META
            eng.wait_ge(flag_ok, layer + 1)
            flag = eng.value_load(over_i[0:1, 0:1], min_val=0, max_val=1)
            with eng.If(flag > 0):
                if eng is nc.vector:
                    dve_prime = nc.vector.memset(small[:, 31:32], 0.0)
                    dve_prime.then_inc(lt_ev[L], 1)
                with eng.Fori(0, E) as e:
                    for fc in range(4):
                        (late_pe if eng is nc.tensor else late_act_part if eng is nc.scalar else late_dve)(eng, L, tiles, nt, c, e, fc)

        def late_pe(pe, L, tiles, nt, c, e, fc):
            pe.wait_ge(late_in[L], e * 192 + 48 * (fc + 1))
            pe.wait_ge(lt_ev[L], e * (8 * nt) + (2 * nt * fc + 1))
            for b, (w, done) in enumerate(((late_g, lt_g), (late_u, lt_u))):
                for kc in range(KC):
                    mm = pe.matmul(bank[:, b, c:T], w[:, kc, :], hT[:, kc, c:T], start=(kc == 0), stop=(kc == KC - 1))
                mm.then_inc(done[L], 1)
            pe.wait_ge(lt_m[L], e * 4 + fc + 1)
            for i, tt in enumerate(tiles):
                for n in range(2):
                    pe.matmul(bank[0:ROWS[tt], 2 + 2 * i + n, :], late_act[:, C0[tt]:C0[tt] + ROWS[tt]],
                              late_d[:, 512 * n:512 * (n + 1)], start=True, stop=True).then_inc(lt_pe[L], 1)

        def late_act_part(act, L, tiles, nt, c, e, fc):
            act.wait_ge(lt_ev[L], e * (8 * nt) + (2 * nt * fc + 1))
            cols = slice(P * fc, P * (fc + 1))
            for dst, w in ((late_g, moe_w_gate), (late_u, moe_w_up)):
                act.dma_start(dst, w[L][bass.ds(e, 1)].rearrange("e (kc p) n -> p (e kc) n", p=P)[:, :, cols]).then_inc(late_in[L], 16)
            act.dma_start(late_d, moe_w_down[L][bass.ds(e, 1)].rearrange("e (fc p) n -> p (e fc) n", p=P)[:, fc, :]).then_inc(late_in[L], 16)
            act.wait_ge(lt_g[L], e * 4 + fc + 1)
            act.activation(late_act[:, c:T], bank[:, 0, c:T], ACT.Silu).then_inc(lt_s[L], 1)

        def late_dve(dve, L, tiles, nt, c, e, fc):
            dve.wait_ge(lt_s[L], e * 4 + fc + 1)
            dve.wait_ge(lt_u[L], e * 4 + fc + 1)
            dve.tensor_tensor(late_act[:, c:T], late_act[:, c:T], bank[:, 1, c:T], ALU.mult).then_inc(lt_m[L], 1)
            for i, tt in enumerate(tiles):
                for n in range(2):
                    r = ROWS[tt]
                    dve.wait_ge(lt_pe[L], e * (8 * nt) + (2 * nt * fc + 2 * i + n + 1))
                    y = yacc[0:r, tt, 512 * n:512 * (n + 1)]
                    dve.scalar_tensor_tensor(y, bank[0:r, 2 + 2 * i + n, :], late_w[0:r, tt, bass.ds(e, 1)], y,
                                             ALU.mult, ALU.add).then_inc(lt_ev[L], 1)

        def exponents(dve, lv, link):
            if lv <= len(LEVELS):
                w = (LEVELS + (P,))[lv] if lv else LEVELS[0]
                if lv == len(LEVELS):
                    w = P
                b = halves(bT[:, :, N_META:T], w)
                m = SEQ // (2 * w)
                end = b[:, :, :, w - 1:w].to_broadcast([P, HEADS, m, w])
                link(dve.tensor_tensor(halves(dec, w)[:, :, :, 0:w], end, b[:, :, :, 0:w], ALU.subtract))
                dve.tensor_tensor(halves(dec, w)[:, :, :, w:2 * w], b[:, :, :, w:2 * w], end, ALU.subtract).then_inc(lv_d, 1)
            else:
                end = bT[:, :, N_META - 1:N_META]
                dve.tensor_tensor(la[:, :, 0:N_META], end.to_broadcast([P, HEADS, N_META]), bT[:, :, 0:N_META],
                                  ALU.subtract).then_inc(gla_b, 1)
                dve.tensor_tensor(dec, bT[:, :, N_META:T], end.to_broadcast([P, HEADS, SEQ]), ALU.subtract).then_inc(lv_d, 1)

        def attend(dve, lv):
            for tt in range(2):
                dve.wait_ge(lv_pe, 2 * lv + tt + 1)
                dve.copy_predicated(att[:, HEADS * tt:HEADS * (tt + 1), :],
                                    level_mask[:, lv, :].unsqueeze(1).to_broadcast([P, HEADS, P]),
                                    bank[:, 2 * (lv % 2) + tt, :].rearrange("p (h t) -> p h t", h=HEADS)).then_inc(lv_ev, 1)

        @block.sync
        def _(sp):
            def used(n):
                if n < 6:
                    return (pj0_pe, 4 * (n + 1)) if n < 3 else ((pj0_pe, len(J0)) if n == 3 else (mix_pe, 6))
                m = n - BASE_ODD
                if m < 0:
                    return used_expert(0, NG - 1, m + GROUP_UNITS)
                return [(pj1_pe, 9), (pj1_pe, 13), (pj1_pe, 16), (pj1_pe, 19), (pj1_pe, 21), (pj1_pe, 23),
                        (mix_pe, 10), (mix_pe, 10)][m]

            def used_expert(layer, g, i):
                if i < 8:
                    return (gate_pe, up_pe)[i // 2 % 2][layer], g * 2 + (i // 4 + 1)
                return d_pe[layer], g * 4 + 2 * (i // 2 - 3)

            def load(n, src):
                if n >= NR:
                    sp.wait_ge(*used(n - NR))
                sp.dma_start(unit(n), src).then_inc(ring_in[n % NR], 16)

            def experts(layer):
                base = BASE_MOE[layer]

                def group(g):
                    order = [(k, e) for pair in (0, 2) for k in "gu" for e in (pair, pair + 1)] + [("d", e) for e in range(GRP)]
                    for i, (kind, e) in enumerate(order):
                        w = {"g": moe_w_gate, "u": moe_w_up, "d": moe_w_down}[kind]
                        kc = 4 if kind == "d" else KC
                        src = w[layer][bass.ds(g * GRP + e, 1)].rearrange("e (kc p) n -> p (e kc) n", p=P)
                        dst = ring[:, (base + i) % NR, :].rearrange("p (kc n) -> p kc n", kc=kc)
                        if i >= NR:
                            sp.wait_ge(*used_expert(layer, g, i - NR))
                        elif isinstance(g, int):
                            sp.wait_ge(*used(base + i - NR))
                        else:
                            sp.wait_ge(*used_expert(layer, g - 1, i - NR + GROUP_UNITS))
                        sp.dma_start(dst, src).then_inc(ring_in[(base + i) % NR], 16)

                group(0)
                with sp.Fori(1, NG) as g:
                    group(g)

            for n in range(4):
                load(n, in_unit(even_w_in, n))
            for n in range(2):
                load(4 + n, in_unit(even_w_out, n))
            experts(0)
            for n in range(6):
                load(BASE_ODD + n, in_unit(odd_w_in, n))
            for n in range(2):
                load(BASE_ODD + 6 + n, in_unit(odd_w_out, n))
            experts(1)
            for tt in range(2):
                sp.wait_ge(h_ready, 3 + 3 + 2 + tt + 1)
                sp.dma_start(out[0, P * tt:P * (tt + 1), :], htok[:, tt, :]).then_inc(stored, 16)
            sp.wait_ge(stored, 32)

        @block.gpsimd
        def _(pool):
            count = [0]

            def link(ins):
                count[0] += 1
                ins.then_inc(pool_c, 1)
                pool.wait_ge(pool_c, count[0])

            def load_gain(k):
                g, b = ((ln_mix_g, ln_mix_b), (ln_ffn_g, ln_ffn_b))[k % 2]
                if k:
                    pool.wait_ge(h_ready, (0, 3, 6, 8)[k])
                pool.dma_start(gain[:, 0, :], g[k // 2].partition_broadcast(P)).then_inc(gain_in, 16)
                pool.dma_start(gain[:, 1, :], b[k // 2].partition_broadcast(P)).then_inc(gain_in, 16)

            pool.dma_start(pw_sb, pool_w[0].rearrange("g c d -> c g d")).then_inc(par_in, 16)
            pool.dma_start(small[:, 8:12], pool_scale[0].rearrange("(g c) -> c g", c=P),
                           allow_slow_non_contiguous=True).then_inc(par_in, 16)
            for i, v in enumerate((diff_lq1, diff_lk1, diff_lq2, diff_lk2)):
                pool.dma_start(lam_v[:, i, :], v[0].partition_broadcast(P)).then_inc(par_in, 16)
            pool.dma_start(sub_b[:, :], diff_subln[0].partition_broadcast(P)).then_inc(par_in, 16)
            pool.dma_start(rw[:, :, :], router_w.rearrange("(kc p) e -> p kc e", p=P)).then_inc(par_in, 16)
            pool.dma_start(rbias[:, :], router_bias.partition_broadcast(P)).then_inc(par_in, 16)
            load_gain(0)
            link(pool.memset(ident[:, :], 0.0))
            pool.affine_select(out=ident[:, :], in_=ident[:, :], compare_op=ALU.not_equal, fill=1.0, base=0,
                               pattern=[[-1, P]], channel_multiplier=1).then_inc(const_ok, 1)
            pool.memset(ones_bf[:, :], 1.0).then_inc(const_ok, 1)
            link(pool.memset(before_bf[:, :], 1.0))
            pool.affine_select(out=before_bf[:, :], in_=before_bf[:, :], compare_op=ALU.is_ge, fill=0.0, base=-1,
                               pattern=[[1, P]], channel_multiplier=-1).then_inc(const_ok, 1)
            pool.iota(iota_slot[:, :], pattern=[[1, SLOTS]], base=0, channel_multiplier=0,
                      allow_small_or_imprecise_dtypes=True).then_inc(const_ok, 1)
            pool.iota(iota_e[:, :], pattern=[[-1, E]], base=E, channel_multiplier=0,
                      allow_small_or_imprecise_dtypes=True).then_inc(const_ok, 1)
            link(pool.memset(zpool[:, :, 0:N_META], 0.0))
            link(pool.memset(poolA[:, :, 0:N_META], 0.0))
            pool.memset(poolB[:, :, 0:N_META], 0.0).then_inc(const_ok, 1)
            for tt in range(3):
                link(pool.iota(dist[:, tt, :], pattern=[[1, T]], base=-C0[tt], channel_multiplier=-1,
                               allow_small_or_imprecise_dtypes=True))
                pool.affine_select(out=dist[:, tt, :], in_=dist[:, tt, :], compare_op=ALU.is_ge, fill=NEG, base=C0[tt],
                                   pattern=[[-1, T]], channel_multiplier=1).then_inc(const_ok, 1)
            for g, w in enumerate(WINDOWS):
                link(pool.iota(pcount[:, g, :], pattern=[[1, T]], base=1, channel_multiplier=0,
                               allow_small_or_imprecise_dtypes=True))
                pool.tensor_scalar(pcount[:, g, :], pcount[:, g, :], float(w), None, ALU.min).then_inc(const_ok, 1)
            pool.iota(iota_i[:, 0:P], pattern=[[1, P]], base=0, channel_multiplier=0).then_inc(const_ok, 1)
            pool.iota(row_i[:, :], pattern=[[0, P]], base=0, channel_multiplier=1).then_inc(const_ok, 1)

            pool.wait_ge(pj0_dve, 2)
            pool.wait_ge(pj0_act, 2)
            src = zpool
            for k in range(4):
                dst = (poolA, poolB)[k % 2]
                link(pool.tensor_tensor(dst[:, k:4, N_META:PADW], src[:, k:4, N_META:PADW],
                                        src[:, k:4, N_META - 2 ** k:PADW - 2 ** k], ALU.add))
                src = dst
            pool.wait_ge(lam_s, 4)
            for g in range(4):
                buf = (poolA, poolB)[g % 2]
                link(pool.tensor_tensor(buf[:, g, N_META:PADW], buf[:, g, N_META:PADW], pcount[:, g, :], ALU.mult))
                pool.tensor_tensor(buf[:, g, N_META:PADW], buf[:, g, N_META:PADW], zpool[:, g, N_META:PADW],
                                   ALU.subtract).then_inc(pooled, 1)
            load_gain(1)
            load_gain(2)
            pool.wait_ge(h_ready, 6)
            pool.dma_start(glw, odd_w_in[0][:, 3072:3072 + GLA_RANK].rearrange("(kc p) n -> p kc n", p=P)).then_inc(par1_in, 16)
            pool.dma_start(g2w[0:GLA_RANK, :], gla_gate_w2[0]).then_inc(par1_in, 16)
            pool.dma_start(gb_sb, gla_gate_b[0].rearrange("(h k) -> k h", k=P),
                           allow_slow_non_contiguous=True).then_inc(par1_in, 16)
            pool.dma_start(hn_b, gla_head_norm[0].partition_broadcast(P)).then_inc(par1_in, 16)
            for lv in range(len(LEVELS)):
                key_factors(pool, lv)
            pool.wait_ge(rg_s, 2)
            for tt in range(2):
                pool.tensor_tensor(rt[:, tt, :].rearrange("p (h v) -> p h v", h=HEADS),
                                   rt[:, tt, :].rearrange("p (h v) -> p h v", h=HEADS),
                                   hn_b.unsqueeze(1).to_broadcast([P, HEADS, GLA_DV]), ALU.mult).then_inc(rg_ok, 1)
            load_gain(3)

        @block.tensor
        def _(pe):
            def turn(k, tiles):
                for i, tt in enumerate(tiles):
                    if k == 0:
                        pe.wait_ge(meta_in if tt == 2 else x_in, 16 if tt == 2 else 32)
                        if i == 0:
                            pe.wait_ge(const_ok, 1)
                    else:
                        pe.wait_ge(h_ready, {1: 0, 2: 3, 3: 6}[k] + i + 1)
                    for kc in range(KC):
                        mm = pe.transpose(bank[:, kc, C0[tt]:C0[tt] + ROWS[tt]],
                                          htok[0:ROWS[tt], tt, P * kc:P * (kc + 1)], ident[0:ROWS[tt], 0:ROWS[tt]])
                        if i == len(tiles) - 1:
                            mm.then_inc(hT_pe, 1)

            def hT_out(k):
                pe.wait_ge(hT_dve, 4 * (k + 1))
                pe.wait_ge(hT_act, 4 * (k + 1))

            def by_token(dst, src, cols, rows, w, used=None):
                for kc in range(KC):
                    mm = pe.matmul(dst, src[:, kc, cols:cols + rows], w[:, kc, :], start=(kc == 0), stop=(kc == KC - 1))
                return mm

            def by_channel(dst, w, src, kcs=KC):
                for kc in range(kcs):
                    mm = pe.matmul(dst, w(kc), src(kc), start=(kc == 0), stop=(kc == kcs - 1))
                return mm

            def mix_out(layer, first_unit, src, tiles, base_col):
                for i, tt in enumerate(tiles):
                    for n in range(2):
                        if i == 0:
                            arrived(pe, first_unit + n)
                        mm = by_token(bank[0:ROWS[tt], 2 * i + n, :], src, C0[tt] - base_col, ROWS[tt], unit(first_unit + n))
                        mm.then_inc(mix_pe, 1)

            def router(layer, tiles):
                hT_out(1 + 2 * layer)
                if layer == 0:
                    pe.wait_ge(par_in, 9 * 16)
                c = 0 if layer == 0 else N_META
                by_channel(bank[0:E, 0, c:T], lambda kc: rw[:, kc, :], lambda kc: hT[:, kc, c:T]).then_inc(lgt_pe, 1)
                pe.wait_ge(lgt_ev, layer + 1)
                for tt in tiles:
                    mm = pe.transpose(bank[0:ROWS[tt], 1, E * tt:E * tt + E], lgT[:, C0[tt]:C0[tt] + ROWS[tt]], ident[0:E, 0:E])
                mm.then_inc(lg_pe, 1)
                pe.wait_ge(pick_ok, layer + 1)
                if layer == 0:
                    pe.wait_ge(const_ok, 3)
                order = sorted(tiles)
                for tt in order + [3]:
                    rows = P if tt == 3 else ROWS[tt]
                    prev = [t for t in order if t < tt]
                    terms = [(ones_bf[0:ROWS[t], 0:rows], t) for t in prev]
                    if tt < 3:
                        terms.append((before_bf[0:ROWS[tt], 0:rows], tt))
                    for i, (lhs, t) in enumerate(terms):
                        mm = pe.matmul(bank[0:rows, 2, E * tt:E * tt + E], lhs, picked_bf[0:ROWS[t], t, :],
                                       start=(i == 0), stop=(i == len(terms) - 1))
                mm.then_inc(pos_pe, 1)

            def experts(layer, tiles):
                base = BASE_MOE[layer]
                nt = len(tiles)
                L = layer

                def gather(g_next):
                    pe.wait_ge(s_ready[L], nt * (g_next + 1))
                    for f in range(4):
                        if f >= 2:
                            pe.wait_ge(gth_ev[L], 4 * g_next + f - 1)
                        for half in range(2):
                            kc = 2 * f + half
                            for i, tt in enumerate(tiles):
                                mm = pe.matmul(bank[:, 4 + f % 2, 256 * half:256 * (half + 1)],
                                               htok[0:ROWS[tt], tt, P * kc:P * (kc + 1)], onehot[0:ROWS[tt], tt, :],
                                               start=(i == 0), stop=(i == nt - 1))
                        mm.then_inc(gth_pe[L], 1)

                def ring_wait(g, i):
                    n = base + i
                    pe.wait_ge(ring_in[n % NR], g * (16 * GROUP_UNITS // NR) + 16 * (n // NR + 1))

                def down_unit(i):
                    return ring[:, (base + i) % NR, :].rearrange("p (fc n) -> p fc n", fc=4)

                def group(g, last):
                    for p in range(2):
                        if p == 0:
                            pe.wait_ge(gth_ev[L], g * 4 + 4)
                        for k in range(2):
                            for e in range(2):
                                ring_wait(g, 4 * p + 2 * k + e)
                            for kc in range(KC):
                                for e in range(2):
                                    s0 = SLOTS * (2 * p + e)
                                    mm = pe.matmul(bank[SLOTS * e:SLOTS * (e + 1), 2 * p + k, :], xg[:, kc, s0:s0 + SLOTS],
                                                   unit(base + 4 * p + 2 * k + e)[:, kc, :],
                                                   start=(kc == 0), stop=(kc == KC - 1))
                            mm.then_inc((gate_pe, up_pe)[k][L], 1)
                    if not last:
                        gather(g + 1)
                    for p in range(2):
                        pe.wait_ge(act_ok[L], g * 2 + p + 1)
                        for fc in range(4):
                            mm = pe.transpose(bank[:, 2 * p, P * fc:P * (fc + 1)], act_sb[:, p, P * fc:P * (fc + 1)], ident[:, :])
                        mm.then_inc(t_pe[L], 1)
                        pe.wait_ge(sw_ready[L], g * nt + nt)
                        for tt in sorted(tiles):
                            mm = pe.transpose(bank[:, 2 * p + 1, C0[tt]:C0[tt] + ROWS[tt]],
                                              whot[0:ROWS[tt], tt, P * p:P * (p + 1)], ident[0:ROWS[tt], 0:ROWS[tt]])
                        mm.then_inc(w_pe[L], 1)
                        pe.wait_ge(t_ev[L], g * 2 + p + 1)
                        for e in range(2):
                            ring_wait(g, 8 + 2 * p + e)
                        for n in range(2):
                            for fc in range(4):
                                for e in range(2):
                                    mm = pe.matmul(bank[SLOTS * e:SLOTS * (e + 1), 6 + n, :], actT[:, fc, SLOTS * e:SLOTS * (e + 1)],
                                                   down_unit(8 + 2 * p + e)[:, fc, 512 * n:512 * (n + 1)],
                                                   start=(fc == 0), stop=(fc == 3))
                            mm.then_inc(d_pe[L], 1)
                        pe.wait_ge(w_ev[L], g * 2 + p + 1)
                        s = 0
                        for n in range(2):
                            pe.wait_ge(d_ev[L], g * 4 + 2 * p + n + 1)
                            for tt in tiles:
                                done = 2 * nt * p + s
                                if done >= 2:
                                    pe.wait_ge(sc_ev[L], g * (4 * nt) + done - 1)
                                elif last:
                                    pe.wait_ge(sc_ev[L], g * (4 * nt))
                                else:
                                    pe.wait_ge(gth_ev[L], g * 4 + 4 + 3 + done)
                                mm = pe.matmul(bank[0:ROWS[tt], 4 + s % 2, :], whotT[:, C0[tt]:C0[tt] + ROWS[tt]],
                                               o_sb[:, 512 * n:512 * (n + 1)], start=True, stop=True)
                                mm.then_inc(sc_pe[L], 1)
                                s += 1

                gather(0)
                with pe.Fori(0, NG - 1) as g:
                    group(g, False)
                group(NG - 1, True)

            turn(0, (2, 0, 1))
            hT_out(0)
            for n, (kind, m) in enumerate(J0):
                if n >= 8:
                    job_out(pe, J0, out0, n - 8)
                if kind == "T":
                    if m % 4 == 0:
                        arrived(pe, m // 4)
                    w = unit(m // 4)
                    mm = by_channel(bank[:, n % 8, 0:T], lambda kc: w[:, kc, P * (m % 4):P * (m % 4 + 1)], lambda kc: hT[:, kc, :])
                else:
                    arrived(pe, 3)
                    mm = by_token(bank[0:ROWS[m], n % 8, :], hT, C0[m], ROWS[m], unit(3))
                mm.then_inc(pj0_pe, 1)

            steps = [(h, tt) for h in range(HEADS) for tt in (2, 0, 1)]

            def keys_of(tt):
                return [2] if tt == 2 else ([2, 0] if tt == 0 else [2, 0, 1])

            def scores(i):
                h, tt = steps[i]
                nk = C0[tt] + ROWS[tt]
                if i == 0:
                    for n in (12, 13, 14):
                        job_out(pe, J0, out0, n)
                if i >= 2:
                    pe.wait_ge(at_b, i - 1)
                for m in range(2):
                    mm = pe.matmul(bank[0:ROWS[tt], 2 * (i % 2) + m, 0:nk], zq[64 * m:64 * (m + 1), h, C0[tt]:C0[tt] + ROWS[tt]],
                                   zk[64 * m:64 * (m + 1), h, 0:nk], start=True, stop=True)
                mm.then_inc(at_s, 1)

            def probs_out(i):
                h, tt = steps[i]
                rows = ROWS[tt]
                pe.wait_ge(at_pd, i + 1)
                if i >= 2:
                    pe.wait_ge(at_te, i - 1)
                for kt in keys_of(tt):
                    mm = pe.transpose(bank[0:ROWS[kt], 4 + i % 2, P * kt:P * kt + rows],
                                      pd[0:rows, i % 2, C0[kt]:C0[kt] + ROWS[kt]], ident[0:rows, 0:rows])
                mm.then_inc(at_t, 1)
                pe.wait_ge(at_te, i + 1)
                if i >= 2:
                    pe.wait_ge(at_oe, i - 1)
                ks = keys_of(tt)
                for j, kt in enumerate(ks):
                    mm = pe.matmul(bank[0:rows, 6 + i % 2, 0:P], pT[0:ROWS[kt], i % 2, kt, 0:rows],
                                   v0[0:ROWS[kt], kt, P * h:P * (h + 1)], start=(j == 0), stop=(j == len(ks) - 1))
                mm.then_inc(at_o, 1)

            for i in range(len(steps) + 1):
                if i < len(steps):
                    scores(i)
                if i == 1:
                    for g in range(4):
                        pe.wait_ge(pooled, g + 1)
                        pe.matmul(bank[:, 4 + g, 0:T], pw_sb[:, g, :], (poolA, poolB)[g % 2][:, g, N_META:PADW],
                                  start=True, stop=True).then_inc(poolmm, 1)
                    pe.wait_ge(poolev, 4)
                if i >= 1:
                    probs_out(i - 1)
            for h in range(HEADS):
                pe.wait_ge(o_n, 3)
                for tt in (2, 0, 1):
                    mm = pe.transpose(bank[:, h, C0[tt]:C0[tt] + ROWS[tt]], o_tok[0:ROWS[tt], tt, P * h:P * (h + 1)],
                                      ident[0:ROWS[tt], 0:ROWS[tt]])
                mm.then_inc(yt_pe, 1)
            pe.wait_ge(yt_ev, 4)
            mix_out(0, 4, yT, (2, 0, 1), 0)
            pe.wait_ge(mix_dve, 6)
            turn(1, (2, 0, 1))
            router(0, (2, 0, 1))
            experts(0, (2, 0, 1))
            late(pe, 0)

            turn(2, (2, 0, 1))
            hT_out(2)
            pe.wait_ge(par1_in, 4 * 16)
            for n, (kind, m) in enumerate(J1):
                if n >= 8:
                    job_out(pe, J1, out1, n - 8)
                b = n % 8
                if kind == "G":
                    mm = by_channel(bank[0:GLA_RANK, b, 0:T], lambda kc: glw[:, kc, :], lambda kc: hT[:, kc, :])
                if kind == "A":
                    pe.wait_ge(pj1_dve, 1)
                    mm = pe.matmul(bank[:, b, 0:T], g2w[0:GLA_RANK, P * m:P * (m + 1)], glr[0:GLA_RANK, :], start=True, stop=True)
                if kind in "QK":
                    u = BASE_ODD + (kind == "K")
                    arrived(pe, u)
                    c = N_META if kind == "Q" else 0
                    mm = by_channel(bank[:, b, 0:T - c], lambda kc: unit(u)[:, kc, P * m:P * (m + 1)], lambda kc: hT[:, kc, c:T])
                if kind in "VR":
                    half, tt = m
                    u = BASE_ODD + (2 if kind == "V" else 4) + half
                    arrived(pe, u)
                    mm = by_token(bank[0:ROWS[tt], b, :], hT, C0[tt], ROWS[tt], unit(u))
                mm.then_inc(pj1_pe, 1)
            nj = len(J1)
            for n in range(nj - 8, nj):
                job_out(pe, J1, out1, n)
            for lv in range(len(LEVELS) + 1):
                if lv < len(LEVELS):
                    pe.wait_ge(lv_q, lv + 1)
                    pe.wait_ge(lv_k, lv + 2)
                if lv >= 2:
                    pe.wait_ge(lv_ev, 2 * (lv - 1))
                for tt in range(2):
                    for h in range(HEADS):
                        if lv < len(LEVELS):
                            a, c = kl[:, h, P * tt:P * (tt + 1)], ql[:, h, P * tt:P * (tt + 1)]
                        else:
                            a, c = kT[:, h, C0[tt]:C0[tt] + P], qT[:, h, P * tt:P * (tt + 1)]
                        mm = pe.matmul(bank[:, 2 * (lv % 2) + tt, P * h:P * (h + 1)], a, c, start=True, stop=True)
                    mm.then_inc(lv_pe, 1)
            pe.wait_ge(lv_q, len(LEVELS) + 1)
            for h in range(HEADS):
                mm = pe.matmul(bank[:, 4, P * h:P * (h + 1)], kl[:, h, 0:P], ql[:, h, P:SEQ], start=True, stop=True)
            mm.then_inc(lv_pe, 1)
            pe.wait_ge(lv_q, len(LEVELS) + 2)
            for h in range(HEADS):
                mm = pe.matmul(bank[0:N_META, 5 + h // 2, SEQ * (h % 2):SEQ * (h % 2 + 1)], kl[:, h, 0:N_META], ql[:, h, :],
                               start=True, stop=True)
            mm.then_inc(lv_pe, 1)
            pe.wait_ge(lv_ev, 2 * (len(LEVELS) + 1) + 3)
            for tt in range(2):
                for c in range(2):
                    for h in (2 * c, 2 * c + 1):
                        dst = bank[:, 2 * tt + c, GLA_DV * (h % 2):GLA_DV * (h % 2 + 1)]
                        vh = vt[:, :, GLA_DV * h:GLA_DV * (h + 1)]
                        pe.matmul(dst, attM[0:N_META, h, P * tt:P * (tt + 1)], vh[0:N_META, 2, :], start=True, stop=False)
                        if tt == 1:
                            pe.matmul(dst, att01[:, h, :], vh[:, 0, :], start=False, stop=False)
                        mm = pe.matmul(dst, att[:, HEADS * tt + h, :], vh[:, tt, :], start=False, stop=True)
                    mm.then_inc(go_pe, 1)
            for tt in range(2):
                pe.wait_ge(ogt_ok, HEADS * (tt + 1))
                if tt == 0:
                    pe.wait_ge(go_ev, 4)
                for c in range(KC):
                    mm = pe.transpose(bank[:, c, P * tt:P * (tt + 1)], og[:, tt, P * c:P * (c + 1)], ident[:, :])
                    if tt == 1:
                        mm.then_inc(ogt_pe, 1)
            pe.wait_ge(ogt_ev, 8)
            mix_out(1, BASE_ODD + 6, ogT, (0, 1), N_META)
            pe.wait_ge(mix_dve, 10)
            turn(3, (0, 1))
            router(1, (0, 1))
            experts(1, (0, 1))
            late(pe, 1)

        @block.scalar
        def _(act):
            count = [0]

            def link(ins):
                count[0] += 1
                ins.then_inc(act_c, 1)
                act.wait_ge(act_c, count[0])

            act.dma_start(htok[0:N_META, 2, :], meta[:, :]).then_inc(meta_in, 16)
            for tt in range(2):
                act.dma_start(htok[:, tt, :], x[0, P * tt:P * (tt + 1), :]).then_inc(x_in, 16)

            def turn(k, c=0):
                for kc in range(1, KC, 2):
                    act.wait_ge(hT_pe, KC * k + kc + 1)
                    act.copy(hT[:, kc, c:T], bank[:, kc, c:T]).then_inc(hT_act, 1)

            def norm_sd(k, tiles):
                for i, tt in enumerate(tiles):
                    done = {0: 0, 1: 3, 2: 6, 3: 8}[k] + i
                    act.wait_ge(var_ok, done + 1)
                    act.activation(rstd[0:ROWS[tt], tt, :], mv[0:ROWS[tt], tt, 1:2], ACT.Sqrt,
                                   bias=eps_ln[0:ROWS[tt], :]).then_inc(sd_ok, 1)

            def router(layer, tiles):
                act.wait_ge(lgt_pe, layer + 1)
                c = 0 if layer == 0 else N_META
                act.copy(lgT[:, c:T], bank[0:E, 0, c:T]).then_inc(lgt_ev, 1)
                act.wait_ge(hT_pe, KC * (2 + 2 * layer))
                if layer == 0:
                    act.wait_ge(h_ready, 3)
                for tt in tiles:
                    act.mul(yacc[0:ROWS[tt], tt, :], htok[0:ROWS[tt], tt, :], ALPHA).then_inc(yinit, 1)
                act.wait_ge(lg_max, layer + 1)
                act.activation(pr[:, 0:len(tiles), :], lg[:, 0:len(tiles), :], ACT.Exp).then_inc(lg_exp, 1)

            def experts(layer, tiles):
                L = layer

                def gather_out(g):
                    for f in range(4):
                        act.wait_ge(gth_pe[L], g * 4 + f + 1)
                        act.copy(xg[:, 2 * f:2 * f + 2, :],
                                 bank[:, 4 + f % 2, :].rearrange("p (a b) -> p a b", a=2)).then_inc(gth_ev[L], 1)

                def group(g, last):
                    for p in range(2):
                        act.wait_ge(gate_pe[L], g * 2 + p + 1)
                        act.activation(act_sb[:, p, :], bank[:, 2 * p, :], ACT.Silu).then_inc(silu_ok[L], 1)
                    if not last:
                        gather_out(g + 1)
                    for p in range(2):
                        act.wait_ge(t_pe[L], g * 2 + p + 1)
                        act.copy(actT, bank[:, 2 * p, :].rearrange("p (a b) -> p a b", a=4)).then_inc(t_ev[L], 1)
                        for n in range(2):
                            act.wait_ge(d_pe[L], g * 4 + 2 * p + n + 1)
                            act.copy(o_sb[:, 512 * n:512 * (n + 1)], bank[:, 6 + n, :]).then_inc(d_ev[L], 1)

                gather_out(0)
                with act.Fori(0, NG - 1) as g:
                    group(g, False)
                group(NG - 1, True)

            turn(0)
            for n, (kind, m) in enumerate(J0):
                if n % 2 == 0:
                    continue
                act.wait_ge(pj0_pe, n + 1)
                if kind == "T":
                    dst = zpool[:, m, N_META:PADW] if m < 4 else (zq, zk)[m // 4 - 1][:, m % 4, :]
                    act.copy(dst, bank[:, n % 8, 0:T]).then_inc(pj0_act, 1)
                else:
                    act.copy(v0[0:ROWS[m], m, :], bank[0:ROWS[m], n % 8, :]).then_inc(pj0_act, 1)
            act.wait_ge(lam_e, 2)
            act.activation(lam1, lam1, ACT.Exp).then_inc(act_c, 1)
            act.activation(lam2, lam2, ACT.Exp).then_inc(act_c, 1)
            count[0] += 2
            steps = [(h, tt) for h in range(HEADS) for tt in (2, 0, 1)]

            def probs_copy(i):
                h, tt = steps[i]
                rows = ROWS[tt]
                act.wait_ge(at_t, i + 1)
                if i >= 2:
                    act.wait_ge(at_o, i - 1)
                if tt != 2:
                    n = 1 if tt == 0 else 2
                    link(act.copy(pT[:, i % 2, 0:n, :], bank[:, 4 + i % 2, 0:P * n].rearrange("p (a b) -> p a b", b=P)))
                act.copy(pT[0:N_META, i % 2, 2, 0:rows], bank[0:N_META, 4 + i % 2, 2 * P:2 * P + rows]).then_inc(at_te, 1)

            for i, (h, tt) in enumerate(steps):
                nk = C0[tt] + ROWS[tt]
                r = ROWS[tt]
                act.wait_ge(at_m, i + 1)
                for m in range(2):
                    sv = s_sb[0:r, i % 2, m, 0:nk]
                    act.activation(sv, sv, ACT.Exp, bias=mx[0:r, i, m:m + 1], scale=ATT_SCALE,
                                   accum_out=sums[0:r, i, m:m + 1]).then_inc(at_e, 1)
                if i == 0:
                    for g in range(4):
                        act.wait_ge(poolmm, g + 1)
                        act.mul(yT[:, g, :], bank[:, 4 + g, 0:T], small[:, 8 + g:9 + g]).then_inc(poolev, 1)
                if i >= 1:
                    probs_copy(i - 1)
            probs_copy(len(steps) - 1)
            act.wait_ge(o_ss, 12)
            act.activation(rstd0, ss0, ACT.Sqrt, bias=eps_rms, scale=1.0 / P).then_inc(o_rs, 1)
            for h in (1, 3):
                act.wait_ge(yt_pe, h + 1)
                act.copy(yT[:, 4 + h, :], bank[:, h, 0:T]).then_inc(yt_ev, 1)
            norm_sd(0, (2, 0, 1))
            turn(1)
            router(0, (2, 0, 1))
            experts(0, (2, 0, 1))
            late(act, 0)
            norm_sd(1, (2, 0, 1))

            turn(2)
            for h in range(HEADS):
                act.wait_ge(gla_ab, h + 1)
                act.activation(la[:, h, :], la[:, h, :], ACT.Exp, scale=-1.0).then_inc(gla_e, 1)
            act.wait_ge(gla_e, 4)
            for h in range(HEADS):
                act.activation(la[:, h, :], la[:, h, :], ACT.Ln, bias=one).then_inc(gla_ln, 1)
            for n, (kind, m) in enumerate(J1):
                if n % 2 == 0 or kind in "GA":
                    continue
                act.wait_ge(pj1_pe, n + 1)
                b = n % 8
                if kind == "Q":
                    act.mul(qT[:, m, :], bank[:, b, 0:SEQ], GLA_SCALE).then_inc(pj1_act, 1)
                if kind == "K":
                    act.copy(kT[:, m, :], bank[:, b, 0:T]).then_inc(pj1_act, 1)
                if kind in "VR":
                    half, tt = m
                    dst = (vt if kind == "V" else rt)[0:ROWS[tt], tt, 512 * half:512 * (half + 1)]
                    act.copy(dst, bank[0:ROWS[tt], b, :]).then_inc(pj1_act, 1)
            for lv in range(len(LEVELS) + 2):
                act.wait_ge(lv_d, lv + 1)
                act.activation(dec, dec, ACT.Exp).then_inc(lv_e, 1)
                if lv == len(LEVELS) + 1:
                    act.wait_ge(gla_b, 5)
                    act.activation(la[:, :, 0:N_META], la[:, :, 0:N_META], ACT.Exp).then_inc(lv_e, 1)
            act.wait_ge(lv_pe, 2 * (len(LEVELS) + 1) + 1)
            act.copy(att01, bank[:, 4, :].rearrange("p (h t) -> p h t", h=HEADS)).then_inc(lv_ev, 1)
            act.wait_ge(lv_pe, 2 * (len(LEVELS) + 1) + 2)
            for c in range(2):
                act.copy(attM[0:N_META, 2 * c:2 * c + 2, :],
                         bank[0:N_META, 5 + c, :].rearrange("p (h t) -> p h t", h=2)).then_inc(lv_ev, 1)
            job_out(act, J1, out1, len(J1) - 1)
            job_out(act, J1, out1, len(J1) - 2)
            for tt in range(2):
                act.activation(rt[:, tt, :], rt[:, tt, :], ACT.Silu).then_inc(rg_s, 1)
            act.wait_ge(o_ss, 20)
            act.activation(rstd1, ss1, ACT.Sqrt, bias=eps_rms, scale=1.0 / GLA_DV).then_inc(o_rs, 1)
            for c in range(1, KC, 2):
                act.wait_ge(ogt_pe, c + 1)
                act.copy(ogT[:, c, :], bank[:, c, 0:SEQ]).then_inc(ogt_ev, 1)
            norm_sd(2, (0, 1))
            turn(3, N_META)
            router(1, (0, 1))
            experts(1, (0, 1))
            late(act, 1)
            norm_sd(3, (0, 1))

        @block.vector
        def _(dve):
            count = [0]

            def link(ins):
                count[0] += 1
                ins.then_inc(dve_c, 1)
                dve.wait_ge(dve_c, count[0])

            def turn(k, c=0):
                for kc in range(0, KC, 2):
                    dve.wait_ge(hT_pe, KC * k + kc + 1)
                    dve.tensor_copy(hT[:, kc, c:T], bank[:, kc, c:T]).then_inc(hT_dve, 1)

            def norm(k, tiles, src):
                sd0 = {0: 0, 1: 3, 2: 6, 3: 8}[k]
                for i, tt in enumerate(tiles):
                    r = ROWS[tt]
                    for n in range(2):
                        link(dve.bn_stats(stats[0:r, tt, n, :], src(tt)[:, 512 * n:512 * (n + 1)]))
                    dve.bn_aggr(mv[0:r, tt, :], stats[0:r, tt, :, :]).then_inc(var_ok, 1)
                dve.wait_ge(gain_in, 32 * (k + 1))
                for i, tt in enumerate(tiles):
                    r = ROWS[tt]
                    dve.wait_ge(sd_ok, sd0 + i + 1)
                    link(dve.reciprocal(rstd[0:r, tt, :], rstd[0:r, tt, :]))
                    link(dve.tensor_scalar(htok[0:r, tt, :], src(tt), mv[0:r, tt, 0:1], rstd[0:r, tt, :], ALU.subtract, ALU.mult))
                    link(dve.tensor_tensor(htok[0:r, tt, :], htok[0:r, tt, :], gain[0:r, 0, :], ALU.mult))
                    dve.tensor_tensor(htok[0:r, tt, :], htok[0:r, tt, :], gain[0:r, 1, :], ALU.add).then_inc(h_ready, 1)

            def mix_in(done, tiles):
                k = done
                for i, tt in enumerate(tiles):
                    for n in range(2):
                        dve.wait_ge(mix_pe, k + 1)
                        c = slice(512 * n, 512 * (n + 1))
                        dve.scalar_tensor_tensor(htok[0:ROWS[tt], tt, c], htok[0:ROWS[tt], tt, c], ALPHA,
                                                 bank[0:ROWS[tt], 2 * i + n, :], ALU.mult, ALU.add).then_inc(mix_dve, 1)
                        k += 1
                dve.wait_ge(mix_dve, k)

            def router(layer, tiles):
                nt = len(tiles)
                a = slice(0, nt)
                dve.wait_ge(lg_pe, layer + 1)
                if nt == 3:
                    link(dve.tensor_copy(lg[0:N_META, 2, :], bank[0:N_META, 1, 2 * E:3 * E]))
                link(dve.tensor_copy(lg[:, 0:2, :], bank[:, 1, 0:2 * E].rearrange("p (t e) -> p t e", t=2)))
                link(dve.tensor_reduce(r1[:, a, :], lg[:, a, :], AX.X, ALU.max))
                dve.tensor_tensor(lg[:, a, :], lg[:, a, :], r1[:, a, :].to_broadcast([P, nt, E]), ALU.subtract).then_inc(lg_max, 1)
                dve.wait_ge(lg_exp, layer + 1)
                link(dve.tensor_reduce(r1[:, a, :], pr[:, a, :], AX.X, ALU.add))
                link(dve.reciprocal(r1[:, a, :], r1[:, a, :]))
                link(dve.tensor_tensor(pr[:, a, :], pr[:, a, :], r1[:, a, :].to_broadcast([P, nt, E]), ALU.mult))
                link(dve.tensor_tensor(sel[:, a, :], pr[:, a, :], rbias[:, :].unsqueeze(1).to_broadcast([P, nt, E]), ALU.add))
                s4 = sel[:, a, :].rearrange("p t (g c b) -> p (t g) c b", c=2, b=2)
                hv = hi[:, a, :, :].rearrange("p t g c -> p (t g) c")
                lv = lo[:, a, :, :].rearrange("p t g c -> p (t g) c")
                link(dve.tensor_tensor(hv, s4[:, :, :, 0], s4[:, :, :, 1], ALU.max))
                link(dve.tensor_tensor(lv, s4[:, :, :, 0], s4[:, :, :, 1], ALU.min))
                gv = gs[:, a, :].rearrange("p t g -> p (t g)")
                uv = g2[:, a, :].rearrange("p t g -> p (t g)")
                link(dve.tensor_tensor(gv, hv[:, :, 0], hv[:, :, 1], ALU.max))
                link(dve.tensor_tensor(uv, hv[:, :, 0], hv[:, :, 1], ALU.min))
                link(dve.tensor_tensor(hv[:, :, 0], lv[:, :, 0], lv[:, :, 1], ALU.max))
                link(dve.tensor_tensor(uv, uv, hv[:, :, 0], ALU.max))
                link(dve.tensor_tensor(gv, gv, uv, ALU.add))

                def first_max(scores, n, hot, tmp):
                    link(dve.tensor_reduce(r1[:, a, :], scores, AX.X, ALU.max))
                    link(dve.tensor_tensor(tmp, scores, r1[:, a, :].to_broadcast([P, nt, n]), ALU.is_equal))
                    link(dve.tensor_tensor(tmp, tmp, iota_e[:, 0:n].unsqueeze(1).to_broadcast([P, nt, n]), ALU.mult))
                    link(dve.tensor_reduce(r2[:, a, :], tmp, AX.X, ALU.max))
                    link(dve.tensor_tensor(hot, tmp, r2[:, a, :].to_broadcast([P, nt, n]), ALU.is_equal))

                first_max(gs[:, a, :], 4, g2[:, a, :], gs[:, a, :])
                link(dve.tensor_scalar(g2[:, a, :], g2[:, a, :], 1.0, -NEG, ALU.subtract, ALU.mult))
                sg = sel[:, a, :].rearrange("p t (g c) -> p t g c", g=4)
                link(dve.tensor_tensor(sg, sg, g2[:, a, :].unsqueeze(3).to_broadcast([P, nt, 4, 4]), ALU.add))
                first_max(sel[:, a, :], E, picked[:, a, :], t1[:, a, :])
                link(dve.tensor_scalar(t2[:, a, :], picked[:, a, :], 2 * NEG, None, ALU.mult))
                link(dve.tensor_tensor(sel[:, a, :], sel[:, a, :], t2[:, a, :], ALU.add))
                first_max(sel[:, a, :], E, t2[:, a, :], t1[:, a, :])
                link(dve.tensor_tensor(picked[:, a, :], picked[:, a, :], t2[:, a, :], ALU.add))
                dve.tensor_copy(picked_bf[:, a, :], picked[:, a, :]).then_inc(pick_ok, 1)
                link(dve.tensor_tensor(weight[:, a, :], pr[:, a, :], picked[:, a, :], ALU.mult))
                link(dve.tensor_reduce(r1[:, a, :], weight[:, a, :], AX.X, ALU.add))
                link(dve.reciprocal(r1[:, a, :], r1[:, a, :]))
                link(dve.tensor_tensor(weight[:, a, :], weight[:, a, :], r1[:, a, :].to_broadcast([P, nt, E]), ALU.mult))
                dve.wait_ge(pos_pe, layer + 1)
                for tt in tiles:
                    r = ROWS[tt]
                    link(dve.tensor_copy(t1[0:r, tt, :], bank[0:r, 2, E * tt:E * tt + E]))
                link(dve.tensor_reduce(over[:, 0:1], bank[:, 2, 3 * E:4 * E], AX.X, ALU.max))
                link(dve.tensor_scalar(over[:, 1:2], over[:, 0:1], float(CAP), None, ALU.is_gt))
                dve.tensor_copy(over_i[:, :], over[:, 1:2]).then_inc(flag_ok, 1)
                link(dve.tensor_scalar(t2[:, a, :], t1[:, a, :], float(CAP), None, ALU.is_lt))
                link(dve.tensor_tensor(t2[:, a, :], t2[:, a, :], picked[:, a, :], ALU.mult))
                link(dve.tensor_scalar(t1[:, a, :], t1[:, a, :], 1.0, None, ALU.add))
                link(dve.tensor_tensor(t1[:, a, :], t1[:, a, :], t2[:, a, :], ALU.mult))
                link(dve.tensor_scalar(slot_of[:, a, :], t1[:, a, :], -1.0, None, ALU.add))
                link(dve.tensor_scalar(t2[:, a, :], t2[:, a, :], -1.0, 1.0, ALU.mult, ALU.add))
                dve.tensor_tensor(late_w[:, a, :], weight[:, a, :], t2[:, a, :], ALU.mult).then_inc(slot_ok, 1)
                dve.wait_ge(slot_ok, layer + 1)

            def experts(layer, tiles):
                L = layer
                nt = len(tiles)

                def build(g):
                    for tt in tiles:
                        r = ROWS[tt]
                        at = slot_of[0:r, tt, bass.ds(g * GRP, GRP)] if not isinstance(g, int) else slot_of[0:r, tt, g * GRP:(g + 1) * GRP]
                        dve.tensor_tensor(onehot[0:r, tt, :].rearrange("p (e s) -> p e s", e=GRP),
                                          iota_slot[0:r, :].unsqueeze(1).to_broadcast([r, GRP, SLOTS]),
                                          at.unsqueeze(2).to_broadcast([r, GRP, SLOTS]), ALU.is_equal).then_inc(s_ready[L], 1)

                def group(g, last):
                    dve.wait_ge(s_ready[L], g * nt + nt)
                    for tt in tiles:
                        r = ROWS[tt]
                        wt = weight[0:r, tt, bass.ds(g * GRP, GRP)] if not isinstance(g, int) else weight[0:r, tt, g * GRP:(g + 1) * GRP]
                        dve.tensor_tensor(whot[0:r, tt, :].rearrange("p (e s) -> p e s", e=GRP),
                                          onehot[0:r, tt, :].rearrange("p (e s) -> p e s", e=GRP),
                                          wt.unsqueeze(2).to_broadcast([r, GRP, SLOTS]), ALU.mult).then_inc(sw_ready[L], 1)
                    if not last:
                        dve.wait_ge(sw_ready[L], g * nt + nt)
                        dve.wait_ge(gth_pe[L], g * 4 + 4)
                        build(g + 1)
                    for p in range(2):
                        dve.wait_ge(silu_ok[L], g * 2 + p + 1)
                        dve.wait_ge(up_pe[L], g * 2 + p + 1)
                        dve.tensor_tensor(act_sb[:, p, :], act_sb[:, p, :], bank[:, 2 * p + 1, :], ALU.mult).then_inc(act_ok[L], 1)
                    for p in range(2):
                        dve.wait_ge(w_pe[L], g * 2 + p + 1)
                        c = 0 if nt == 3 else N_META
                        dve.tensor_copy(whotT[:, c:T], bank[:, 2 * p + 1, c:T]).then_inc(w_ev[L], 1)
                        s = 0
                        for n in range(2):
                            for tt in tiles:
                                dve.wait_ge(sc_pe[L], g * (4 * nt) + 2 * nt * p + s + 1)
                                y = yacc[0:ROWS[tt], tt, 512 * n:512 * (n + 1)]
                                dve.tensor_tensor(y, y, bank[0:ROWS[tt], 4 + s % 2, :], ALU.add).then_inc(sc_ev[L], 1)
                                s += 1

                build(0)
                dve.wait_ge(yinit, (3, 5)[layer])
                with dve.Fori(0, NG - 1) as g:
                    group(g, False)
                group(NG - 1, True)
                dve.wait_ge(sc_ev[L], 4 * nt * NG)

            dve.memset(eps_ln, 1e-5)
            dve.memset(eps_rms, 1e-6)
            dve.memset(one, 1.0)
            dve.memset(lg[:, :, :], 0.0)
            link(dve.memset(ss0, 1.0))
            dve.wait_ge(const_ok, 6 + 3 + 4 + 2)
            for g in range(4):
                dve.reciprocal(pcount[:, g, :], pcount[:, g, :]).then_inc(lam_s, 1)
            dve.wait_ge(par_in, 9 * 16)
            for k in range(2):
                link(dve.tensor_tensor(lam_t[:, k, :], lam_v[:, 2 * k, :], lam_v[:, 2 * k + 1, :], ALU.mult))
                dve.tensor_reduce((lam1, lam2)[k], lam_t[:, k, :], AX.X, ALU.add).then_inc(lam_e, 1)
            dve.tensor_scalar(sub_b[:, :], sub_b[:, :], 1.0 - LAMBDA_INIT, None, ALU.mult)
            ge, xf = rt[:, 0, 0:P], rt[:, 0, P:2 * P]
            link(dve.tensor_tensor(ge, iota_i[:, 0:P], row_i[:, :], ALU.is_ge))
            link(dve.tensor_tensor(row_i[:, :], row_i[:, :], iota_i[:, 0:P], ALU.bitwise_xor))
            link(dve.tensor_scalar(xf, row_i[:, :], -4096.0, None, ALU.add))
            link(dve.tensor_tensor(xf, xf, ge, ALU.mult))
            link(dve.tensor_scalar(row_i[:, :], xf, 4096.0, None, ALU.add))
            for lv, w in enumerate(LEVELS):
                link(dve.tensor_scalar(level_mask[:, lv, :], row_i[:, :], w.bit_length() - 1, None, ALU.logical_shift_right))
                link(dve.tensor_scalar(level_mask[:, lv, :], level_mask[:, lv, :], 1.0, None, ALU.is_equal))
            link(dve.tensor_scalar(level_mask[:, len(LEVELS), :], row_i[:, :], 0.0, None, ALU.is_equal))

            turn(0)
            for n, (kind, m) in enumerate(J0):
                if n % 2:
                    continue
                dve.wait_ge(pj0_pe, n + 1)
                if kind == "T":
                    dst = zpool[:, m, N_META:PADW] if m < 4 else (zq, zk)[m // 4 - 1][:, m % 4, :]
                    dve.tensor_copy(dst, bank[:, n % 8, 0:T]).then_inc(pj0_dve, 1)
                else:
                    dve.tensor_copy(v0[0:ROWS[m], m, :], bank[0:ROWS[m], n % 8, :]).then_inc(pj0_dve, 1)
            dve.wait_ge(act_c, 2)
            link(dve.tensor_tensor(nlam, lam2, lam1, ALU.subtract))
            link(dve.tensor_scalar(nlam, nlam, -LAMBDA_INIT, None, ALU.add))
            steps = [(h, tt) for h in range(HEADS) for tt in (2, 0, 1)]

            def biased(i):
                h, tt = steps[i]
                r, nk = ROWS[tt], C0[tt] + ROWS[tt]
                dve.wait_ge(at_s, i + 1)
                if i >= 2:
                    dve.wait_ge(at_pd, i - 1)
                sv = s_sb[0:r, i % 2, :, 0:nk]
                dve.scalar_tensor_tensor(sv, dist[0:r, tt, 0:nk].unsqueeze(1).to_broadcast([r, 2, nk]), SLOPES[h] / ATT_SCALE,
                                         bank[0:r, 2 * (i % 2):2 * (i % 2) + 2, 0:nk], ALU.mult, ALU.add).then_inc(at_b, 1)
                dve.wait_ge(at_b, i + 1)
                link(dve.tensor_reduce(mx[0:r, i, :], sv, AX.X, ALU.max))
                dve.tensor_scalar(mx[0:r, i, :], mx[0:r, i, :], -ATT_SCALE, None, ALU.mult).then_inc(at_m, 1)

            def difference(i):
                h, tt = steps[i]
                r, nk = ROWS[tt], C0[tt] + ROWS[tt]
                dve.wait_ge(at_e, 2 * i + 2)
                link(dve.reciprocal(rs[0:r, i, :], sums[0:r, i, :]))
                link(dve.tensor_tensor(rs[0:r, i, 1:2], rs[0:r, i, 1:2], nlam[0:r, :], ALU.mult))
                p0, p1 = s_sb[0:r, i % 2, 0, 0:nk], s_sb[0:r, i % 2, 1, 0:nk]
                link(dve.tensor_scalar(p1, p1, rs[0:r, i, 1:2], None, ALU.mult))
                if i >= 2:
                    dve.wait_ge(at_t, i - 1)
                dve.scalar_tensor_tensor(pd[0:r, i % 2, 0:nk], p0, rs[0:r, i, 0:1], p1, ALU.mult, ALU.add).then_inc(at_pd, 1)

            def head_out(i):
                h, tt = steps[i]
                r = ROWS[tt]
                dve.wait_ge(at_o, i + 1)
                o = o_tok[0:r, tt, P * h:P * (h + 1)]
                dve.tensor_copy(o, bank[0:r, 6 + i % 2, 0:P]).then_inc(at_oe, 1)
                dve.wait_ge(at_oe, i + 1)
                j = HEADS * tt + h
                dve.tensor_tensor_reduce(out=sq0[0:r, :], in0=o, in1=o, scale=1.0, scalar=0.0, op0=ALU.mult,
                                         op1=ALU.add, accum_out=ss0[0:r, j:j + 1]).then_inc(o_ss, 1)
                dve.wait_ge(o_ss, i + 1)

            for i in range(len(steps) + 2):
                if i < len(steps):
                    biased(i)
                if 1 <= i <= len(steps):
                    difference(i - 1)
                if i >= 2:
                    head_out(i - 2)
            dve.wait_ge(o_rs, 1)
            link(dve.reciprocal(rstd0, rstd0))
            for tt in (2, 0, 1):
                r = ROWS[tt]
                o = o_tok[0:r, tt, :].rearrange("p (h v) -> p h v", h=HEADS)
                link(dve.tensor_tensor(o, o, rstd0[0:r, HEADS * tt:HEADS * (tt + 1)].unsqueeze(2).to_broadcast([r, HEADS, P]), ALU.mult))
                dve.tensor_tensor(o, o, sub_b[0:r, :].unsqueeze(1).to_broadcast([r, HEADS, P]), ALU.mult).then_inc(o_n, 1)
            for h in (0, 2):
                dve.wait_ge(yt_pe, h + 1)
                dve.tensor_copy(yT[:, 4 + h, :], bank[:, h, 0:T]).then_inc(yt_ev, 1)
            mix_in(0, (2, 0, 1))
            norm(0, (2, 0, 1), lambda tt: htok[0:ROWS[tt], tt, :])
            turn(1)
            router(0, (2, 0, 1))
            experts(0, (2, 0, 1))
            late(dve, 0)
            norm(1, (2, 0, 1), lambda tt: yacc[0:ROWS[tt], tt, :])

            turn(2)
            dve.wait_ge(par1_in, 64)
            for n, (kind, m) in enumerate(J1):
                if n % 2 and kind != "A":
                    continue
                dve.wait_ge(pj1_pe, n + 1)
                b = n % 8
                if kind == "G":
                    dve.tensor_copy(glr[0:GLA_RANK, :], bank[0:GLA_RANK, b, 0:T]).then_inc(pj1_dve, 1)
                if kind == "A":
                    dve.tensor_scalar(bT[:, m, :], bank[:, b, 0:T], gb_sb[:, m:m + 1], None, ALU.add).then_inc(gla_ga, 1)
                    dve.wait_ge(gla_ga, m + 1)
                    dve.scalar_tensor_tensor(la[:, m, :], bT[:, m, :], -1.0, bT[:, m, :], ALU.mult, ALU.max).then_inc(gla_ab, 1)
                if kind == "Q":
                    dve.tensor_scalar(qT[:, m, :], bank[:, b, 0:SEQ], GLA_SCALE, None, ALU.mult).then_inc(pj1_dve, 1)
                if kind == "K":
                    dve.tensor_copy(kT[:, m, :], bank[:, b, 0:T]).then_inc(pj1_dve, 1)
                if kind in "VR":
                    half, tt = m
                    dst = (vt if kind == "V" else rt)[0:ROWS[tt], tt, 512 * half:512 * (half + 1)]
                    dve.tensor_copy(dst, bank[0:ROWS[tt], b, :]).then_inc(pj1_dve, 1)
                if kind == "K" and m == 3:
                    dve.wait_ge(gla_ln, 4)
                    link(dve.tensor_scalar(bT, bT, 0.0, None, ALU.min))
                    link(dve.tensor_tensor(la, bT, la, ALU.subtract))
                    link(dve.tensor_scalar(la, la, 1.0 / GLA_TAU, None, ALU.mult))
                    link(dve.memset(ogT[:, 0:2, :], 1.0))
                    for h in range(HEADS):
                        dve.tensor_tensor_scan(bT[:, h, :], ogT[:, 0:2, :].rearrange("p a b -> p (a b)")[:, 0:T], la[:, h, :], 0.0,
                                               ALU.mult, ALU.add).then_inc(gla_b, 1)
                    dve.wait_ge(gla_b, 4)
                    link(dve.memset(ql, 0.0))
                    link(dve.memset(att, 0.0))
                    dve.memset(kl, 0.0).then_inc(lv_k, 1)
                    exponents(dve, 0, link)
            for lv in range(len(LEVELS)):
                w = LEVELS[lv]
                dve.wait_ge(lv_e, lv + 1)
                if lv:
                    dve.wait_ge(lv_pe, 2 * lv)
                dve.tensor_tensor(halves(ql, w)[:, :, :, w:2 * w], halves(qT, w)[:, :, :, w:2 * w],
                                  halves(dec, w)[:, :, :, w:2 * w], ALU.mult).then_inc(lv_q, 1)
                dve.wait_ge(lv_q, lv + 1)
                dve.wait_ge(lv_k, lv + 2)
                exponents(dve, lv + 1, link)
                attend(dve, lv)
            nl = len(LEVELS)
            dve.wait_ge(lv_e, nl + 1)
            dve.wait_ge(lv_pe, 2 * nl)
            link(dve.tensor_tensor(kl[:, :, 0:P], kT[:, :, N_META:N_META + P], dec[:, :, 0:P], ALU.mult))
            dve.tensor_tensor(ql[:, :, P:SEQ], qT[:, :, P:SEQ], dec[:, :, P:SEQ], ALU.mult).then_inc(lv_q, 1)
            dve.wait_ge(lv_q, nl + 1)
            exponents(dve, nl + 1, link)
            attend(dve, nl)
            dve.wait_ge(lv_e, nl + 3)
            dve.wait_ge(lv_pe, 2 * (nl + 1) + 1)
            link(dve.tensor_tensor(kl[:, :, 0:N_META], kT[:, :, 0:N_META], la[:, :, 0:N_META], ALU.mult))
            dve.tensor_tensor(ql, qT, dec, ALU.mult).then_inc(lv_q, 1)
            for tt in range(2):
                for c in range(2):
                    dve.wait_ge(go_pe, 2 * tt + c + 1)
                    o = og[:, tt, 512 * c:512 * (c + 1)]
                    dve.tensor_copy(o, bank[:, 2 * tt + c, :]).then_inc(go_ev, 1)
                    dve.wait_ge(go_ev, 2 * tt + c + 1)
                    for h in (2 * c, 2 * c + 1):
                        oh = og[:, tt, GLA_DV * h:GLA_DV * (h + 1)]
                        j = HEADS * tt + h
                        dve.tensor_tensor_reduce(out=ogT[:, 0, :], in0=oh, in1=oh, scale=1.0, scalar=0.0,
                                                 op0=ALU.mult, op1=ALU.add, accum_out=ss1[:, j:j + 1]).then_inc(o_ss, 1)
                        dve.wait_ge(o_ss, 12 + j + 1)
            dve.wait_ge(o_rs, 2)
            link(dve.reciprocal(rstd1, rstd1))
            for tt in range(2):
                dve.wait_ge(rg_ok, tt + 1)
                for h in range(HEADS):
                    c = slice(GLA_DV * h, GLA_DV * (h + 1))
                    j = HEADS * tt + h
                    dve.scalar_tensor_tensor(og[:, tt, c], og[:, tt, c], rstd1[:, j:j + 1], rt[:, tt, c],
                                             ALU.mult, ALU.mult).then_inc(ogt_ok, 1)
            for c in range(0, KC, 2):
                dve.wait_ge(ogt_pe, c + 1)
                dve.tensor_copy(ogT[:, c, :], bank[:, c, 0:SEQ]).then_inc(ogt_ev, 1)
            mix_in(6, (0, 1))
            norm(2, (0, 1), lambda tt: htok[0:ROWS[tt], tt, :])
            turn(3, N_META)
            router(1, (0, 1))
            experts(1, (0, 1))
            late(dve, 1)
            norm(3, (0, 1), lambda tt: yacc[0:ROWS[tt], tt, :])


_INS = ['x', 'meta', 'even_w_in', 'pool_w', 'pool_scale', 'diff_lq1', 'diff_lk1', 'diff_lq2', 'diff_lk2',
        'diff_subln', 'even_w_out', 'odd_w_in', 'gla_gate_w2', 'gla_gate_b', 'gla_head_norm', 'odd_w_out',
        'ln_mix_g', 'ln_mix_b', 'ln_ffn_g', 'ln_ffn_b', 'router_w', 'router_bias',
        'moe_w_gate', 'moe_w_up', 'moe_w_down']


def kernel(**inputs):
    import numpy as _np
    import concourse.bacc as _bacc
    from concourse import mybir as _mybir
    from concourse.bass_utils import run_bass_kernel_spmd as _run

    nc = _bacc.Bacc("TRN2", target_bir_lowering=False, num_devices=1)
    arrays, args = {}, []
    for name in _INS:
        a = _np.ascontiguousarray(inputs[name])
        arrays[f"in_{name}_dram"] = a
        args.append(nc.dram_tensor(f"in_{name}_dram", a.shape, _mybir.dt.from_np(a.dtype), kind="ExternalInput").ap())
    out = nc.dram_tensor("out_0_dram", (1, SEQ, D), _mybir.dt.float32, kind="ExternalOutput").ap()
    hybrid_trunk(nc, *args, out)
    r = _run(nc, [arrays], core_ids=[0])
    return r.results[0]["out_0_dram"]
```

```python
import math
from contextlib import ExitStack

import concourse.bass as bass
from concourse import mybir

F32 = mybir.dt.float32
BF16 = mybir.dt.bfloat16
I32 = mybir.dt.int32
ALU = mybir.AluOpType
ACT = mybir.ActivationFunctionType
AX = mybir.AxisListType

P = 128
D = 1024
KC = D // P
SEQ = 256
N_META = 16
T = N_META + SEQ
C0 = (N_META, N_META + P, 0)
ROWS = (P, P, N_META)
HEADS = 4
WINDOWS = (2, 4, 8, 16)
QK_DIM = 64
ATT_SCALE = QK_DIM ** -0.5
SLOPES = [2.0 ** (-8.0 * (h + 1) / HEADS) for h in range(HEADS)]
LAMBDA_INIT = 0.8 - 0.6 * math.exp(0.0)
NEG = -1e30
GLA_DV = D // HEADS
GLA_SCALE = float(P) ** -0.5
GLA_TAU = 16.0
GLA_RANK = 16
LEVELS = (64, 32, 16, 8, 4, 2, 1)
DEPTH = 2
ALPHA = (2.0 * DEPTH) ** 0.25
E = 16
GRP = 4
NG = E // GRP
SLOTS = 64
CAP = SLOTS
NR = 6
UNIT = 4096
GROUP_UNITS = 3 * GRP
BASE_MOE = (6, 6 + NG * GROUP_UNITS + 8)
BASE_ODD = BASE_MOE[0] + NG * GROUP_UNITS


def hybrid_trunk(nc, x, meta, even_w_in, pool_w, pool_scale, diff_lq1, diff_lk1, diff_lq2, diff_lk2,
                 diff_subln, even_w_out, odd_w_in, gla_gate_w2, gla_gate_b, gla_head_norm, odd_w_out,
                 ln_mix_g, ln_mix_b, ln_ffn_g, ln_ffn_b, router_w, router_bias,
                 moe_w_gate, moe_w_up, moe_w_down, out):
    with ExitStack() as ctx:
        def sb(name, shape, dt=F32):
            return ctx.enter_context(nc.sbuf_tensor(name, shape, dt))

        def sem(name):
            return ctx.enter_context(nc.semaphore(name))

        def per_layer(name):
            return [sem(f"{name}{layer}") for layer in range(DEPTH)]

        bank = ctx.enter_context(nc.psum_tensor("bank", [P, 8, 512], F32))

        ring = sb("ring", [P, NR, UNIT])
        htok = sb("htok", [P, 3, D])
        hT = sb("hT", [P, KC, T])
        gain = sb("gain", [P, 2, D])
        ident = sb("ident", [P, P])
        ones_bf = sb("ones_bf", [P, P], BF16)
        before_bf = sb("before_bf", [P, P], BF16)
        dist = sb("dist", [P, 3, T])
        iota_slot = sb("iota_slot", [P, SLOTS])
        iota_g = sb("iota_g", [P, NG])
        earlier = sb("earlier", [P, GRP, GRP])
        iota_i = sb("iota_i", [P, T], I32)
        row_i = sb("row_i", [P, P], I32)
        level_mask = sb("level_mask", [P, len(LEVELS) + 1, P], I32)
        small = sb("small", [P, 32])
        rw = sb("rw", [P, KC, E])
        rbias = sb("rbias", [P, E])
        sub_b = sb("sub_b", [P, P])
        stats = sb("stats", [P, 3, 2, 6])
        mv = sb("mv", [P, 3, 2])
        rstd = sb("rstd", [P, 3, 1])
        nbias = sb("nbias", [P, 3, 1])
        lgT = sb("lgT", [E, T])
        lg = sb("lg", [P, 3, E])
        pr = sb("pr", [P, 3, E])
        sel = sb("sel", [P, 3, E])
        above = sb("above", [P, 3 * NG, GRP, GRP])
        equal = sb("equal", [P, 3 * NG, GRP, GRP])
        rank = sb("rank", [P, 3 * NG, GRP])
        gs = sb("gs", [P, 3, NG])
        ghot = sb("ghot", [P, 3, NG])
        r1 = sb("r1", [P, 3, 1])
        r2 = sb("r2", [P, 3, 1])
        t1 = sb("t1", [P, 3, E])
        picked = sb("picked", [P, 3, E])
        picked_bf = sb("picked_bf", [P, 3, E], BF16)
        weight = sb("weight", [P, 3, E])
        late_w = sb("late_w", [P, 3, E])
        slot_of = sb("slot_of", [P, 3, E])
        over = sb("over", [P, 2])
        over_i = sb("over_i", [P, 1], I32)

        SCR = 16000
        scratch = sb("scratch", [P, SCR])

        class Cut:
            def __init__(self):
                self.at = 0

            def __call__(self, *shape):
                n = 1
                for s in shape:
                    n *= s
                v = scratch[:, self.at:self.at + n]
                self.at += n
                assert self.at <= SCR, self.at
                if len(shape) == 2:
                    v = v.rearrange("p (a b) -> p a b", b=shape[1])
                if len(shape) == 3:
                    v = v.rearrange("p (a b c) -> p a b c", b=shape[1], c=shape[2])
                return v

        cut = Cut()
        PADW = N_META + T
        zpool = cut(4, PADW)
        poolA = cut(4, PADW)
        poolB = cut(4, PADW)
        pcount = cut(4, N_META)
        zq = cut(4, T)
        zk = cut(4, T)
        v0 = cut(3, 512)
        yT = cut(8, T)
        s_sb = cut(8, T).rearrange("p (b m) k -> p b m k", b=2)
        pd = cut(2, T)
        pT = cut(2, 3, P)
        o_tok = cut(3, 512)
        pw_sb = cut(4, P)
        sq0 = cut(P)
        lam_v = cut(4, QK_DIM)
        lam_t = cut(2, QK_DIM)
        ss0 = cut(12)
        mx = cut(6, 4)
        sums = cut(6, 4)
        rs = cut(6, 4)
        rstd0 = cut(12)
        cut = Cut()
        qT = cut(4, SEQ)
        kT = cut(4, T)
        bT = cut(4, T)
        la = cut(4, T)
        vt = cut(3, D)
        rt = cut(2, D)
        dec = cut(4, SEQ)
        ql = cut(4, SEQ)
        kl = cut(4, SEQ)
        att = cut(8, P)
        att01 = cut(4, P)
        ss1 = cut(8)
        rstd1 = cut(8)
        glr = cut(T)
        hn_b = cut(GLA_DV)
        g2w = cut(512)
        gb_sb = cut(4)
        glw = cut(KC, GLA_RANK)
        at = Cut()
        og = at(2, D)
        at.at = 1024 + 1088
        attM = at(4, SEQ)
        at.at = 1024 + 3 * 1088 + 3 * D + 2 * D
        ogT = at(8, SEQ)
        cut = Cut()
        yacc = cut(3, D)
        xg = cut(KC, GRP * SLOTS)
        onehot = cut(3, GRP * SLOTS)
        whot = cut(3, GRP * SLOTS)
        act_sb = cut(2, 512)
        actT = cut(4, P)
        o_sb = cut(D)
        whotT = cut(2, T)
        ymeta = cut(SEQ)
        late_act = cut(T)
        meta_row = scratch[:, cut.at:cut.at + D]
        late_g = cut(KC, P)
        late_u = cut(KC, P)
        late_d = cut(D)

        eps_ln, eps_rms, lam1, lam2, nlam, one = (small[:, i:i + 1] for i in range(6))

        ring_in = [sem(f"ring_in{i}") for i in range(NR)]
        x_in, meta_in, par_in, par1_in, gain_in = (sem(n) for n in ("x_in", "meta_in", "par_in", "par1_in", "gain_in"))
        dve_c, act_c, pool_c = sem("dve_c"), sem("act_c"), sem("pool_c")
        const_ok, lvl_ok = sem("const_ok"), sem("lvl_ok")
        hT_pe, hT_act = sem("hT_pe"), sem("hT_act")
        h_left, h_right = sem("h_left"), sem("h_right")
        pj0_pe, pj0_dve, pj0_act = sem("pj0_pe"), sem("pj0_dve"), sem("pj0_act")
        pj1_pe, pj1_dve, pj1_act = sem("pj1_pe"), sem("pj1_dve"), sem("pj1_act")
        out0, out1 = (pj0_dve, pj0_act), (pj1_dve, pj1_act)
        pooled, poolmm, poolev = sem("pooled"), sem("poolmm"), sem("poolev")
        lam_e, lam_s = sem("lam_e"), sem("lam_s")
        at_s, at_b, at_m, at_e, at_pd = sem("at_s"), sem("at_b"), sem("at_m"), sem("at_e"), sem("at_pd")
        at_t, at_te, at_o, at_oe = sem("at_t"), sem("at_te"), sem("at_o"), sem("at_oe")
        o_ss, o_rs, o_n = sem("o_ss"), sem("o_rs"), sem("o_n")
        yt_pe, yt_dve, yt_act = sem("yt_pe"), sem("yt_dve"), sem("yt_act")
        mix_pe, mix_dve = sem("mix_pe"), sem("mix_dve")
        var_ok, sd_ok, nb_ok, xn_ok, xg_ok = (sem(n) for n in ("var_ok", "sd_ok", "nb_ok", "xn_ok", "xg_ok"))
        ym_zero, ym_out = sem("ym_zero"), sem("ym_out")
        lgt_pe, lgt_ev, lg_pe, lg_ev = sem("lgt_pe"), sem("lgt_ev"), sem("lg_pe"), sem("lg_ev")
        lg_max, lg_exp, pick_ok, pos_pe, route_ok = (sem(n) for n in ("lg_max", "lg_exp", "pick_ok", "pos_pe", "route_ok"))
        eq_ok, slot_ok, flag_ok = sem("eq_ok"), sem("slot_ok"), sem("flag_ok")
        yinit = sem("yinit")
        s_ready, sw_ready = per_layer("s_ready"), per_layer("sw_ready")
        gth_pe, gth_ev = per_layer("gth_pe"), per_layer("gth_ev")
        gate_pe, up_pe, silu_ok, act_ok = per_layer("gate_pe"), per_layer("up_pe"), per_layer("silu_ok"), per_layer("act_ok")
        t_pe, t_ev, w_pe, w_ev = per_layer("t_pe"), per_layer("t_ev"), per_layer("w_pe"), per_layer("w_ev")
        d_pe, d_ev, sc_pe, sc_ev = per_layer("d_pe"), per_layer("d_ev"), per_layer("sc_pe"), per_layer("sc_ev")
        gla_ga, gla_ab, gla_e, gla_ln, gla_b = (sem(n) for n in ("gla_ga", "gla_ab", "gla_e", "gla_ln", "gla_b"))
        lv_d, lv_e, lv_q, lv_k, lv_pe, lv_ev, lv_act = (sem(n) for n in ("lv_d", "lv_e", "lv_q", "lv_k", "lv_pe", "lv_ev", "lv_act"))
        go_pe, go_ev, rg_s, rg_ok, ogt_ok, ogt_pe, ogt_ev = (sem(n) for n in (
            "go_pe", "go_ev", "rg_s", "rg_ok", "ogt_ok", "ogt_pe", "ogt_ev"))
        stored = sem("stored")
        first_half = sem("first_half")
        late_in = per_layer("late_in")
        lt_g, lt_u, lt_s, lt_m, lt_pe, lt_ev = (per_layer(n) for n in ("lt_g", "lt_u", "lt_s", "lt_m", "lt_pe", "lt_ev"))

        block = ctx.enter_context(nc.Block())

        def in_unit(w, n):
            return w[0][:, 512 * n:512 * (n + 1)].rearrange("(kc p) n -> p kc n", p=P)

        def unit(n):
            return ring[:, n % NR, :].rearrange("p (kc n) -> p kc n", kc=KC)

        def normed(eng, n):
            eng.wait_ge(h_left, n)
            eng.wait_ge(h_right, n)

        def arrived(eng, n):
            eng.wait_ge(ring_in[n % NR], 16 * (n // NR + 1))


        J0 = ([("Q", h, "da"[h % 2]) for h in range(4)] + [("K", h, "da"[h % 2]) for h in range(4)]
              + [("V", tt, "a") for tt in (2, 0, 1)] + [("U", g, "a") for g in (3, 2, 1, 0)])
        def bank0(n):
            return n if n < 8 else (4, 5)[n - 8] if n < 10 else 7

        J1 = ([("V", (n, 0), "a", 4 + n) for n in range(2)] + [("M", 0, "a", 6), ("G", 0, "d", 7)]
              + [("A", h, "g", h) for h in range(4)] + [("Q", h, "da"[h % 2], 4 + h) for h in range(4)]
              + [("K", h, "da"[h % 2], h) for h in range(4)] + [("V", (n, 1), "da"[n], 4 + n) for n in range(2)]
              + [("R", (n, tt), "da"[tt], (6, 7, 4, 5)[2 * n + tt]) for n in range(2) for tt in range(2)])
        NLV = 16

        def job_out(eng, jobs, sems, n):
            by = jobs[n][2]
            sem_of = {"d": sems[0], "a": sems[1], "g": gla_ga}[by]
            eng.wait_ge(sem_of, len([m for m in range(n + 1) if jobs[m][2] == by]))

        def meta_quarters(pe, dst, src, w):
            for kc in range(KC):
                for q in range(4):
                    wq = w(kc, q)
                    mm = pe.matmul(dst[32 * q:32 * q + N_META, 0:wq.shape[-1]], src[:, kc, 0:N_META], wq,
                                   start=(kc == 0), stop=(kc == KC - 1), skip_group_check=True)
            return mm

        def halves(v, w):
            return v.rearrange("p h (m t) -> p h m t", t=2 * w)

        def key_factors(eng, lv):
            w = LEVELS[lv]
            eng.wait_ge(lv_e, lv + 1)
            if lv == 0:
                job_out(eng, J1, out1, NLV - 2)
                job_out(eng, J1, out1, NLV - 1)
                eng.wait_ge(lv_k, 1)
            else:
                eng.wait_ge(lv_pe, 2 * lv)
            eng.tensor_tensor(halves(kl, w)[:, :, :, 0:w], halves(kT[:, :, N_META:T], w)[:, :, :, 0:w],
                              halves(dec, w)[:, :, :, 0:w], ALU.mult).then_inc(lv_k, 1)

        STEPS = [(0, 0), (0, 1), (1, 0), (1, 1), (2, 0), (2, 1)]
        KEYS = ([2, 0], [2, 0, 1], [2])

        FFN_ORDER = (0, 2, 1)
        TURN_BANK = (6, 0, 2)

        def scatter_order(layer, last):
            if last:
                return [(0, 0), (0, 1)] + [(2, 2)] * (layer == 0) + [(1, 0), (1, 1)]
            return [(0, 0), (1, 0), (0, 1), (1, 1)] + [(2, 2)] * (layer == 0)

        def late(eng, layer):
            L = layer
            tiles = ((2, 0, 1), (0, 1))[layer]
            nt = len(tiles)
            c = 0 if layer == 0 else N_META
            eng.wait_ge(flag_ok, layer + 1)
            flag = eng.value_load(over_i[0:1, 0:1], min_val=0, max_val=1)
            with eng.If(flag > 0):
                if eng is nc.vector:
                    dve_prime = nc.vector.memset(small[:, 31:32], 0.0)
                    dve_prime.then_inc(lt_ev[L], 1)
                with eng.Fori(0, E) as e:
                    for fc in range(4):
                        (late_pe if eng is nc.tensor else late_act_part if eng is nc.scalar else late_dve)(eng, L, tiles, nt, c, e, fc)
                if eng is not nc.scalar:
                    eng.wait_ge(lt_ev[L], 1 + 8 * nt * E)

        def late_pe(pe, L, tiles, nt, c, e, fc):
            pe.wait_ge(gth_ev[L], 4)
            pe.wait_ge(late_in[L], e * 192 + 48 * (fc + 1))
            pe.wait_ge(lt_ev[L], e * (8 * nt) + (2 * nt * fc + 1))
            for b, (w, done) in enumerate(((late_g, lt_g), (late_u, lt_u))):
                for kc in range(KC):
                    mm = pe.matmul(bank[:, b, c:T], w[:, kc, :], hT[:, kc, c:T], start=(kc == 0), stop=(kc == KC - 1))
                mm.then_inc(done[L], 1)
            pe.wait_ge(lt_m[L], e * 4 + fc + 1)
            for i, tt in enumerate(tiles):
                for n in range(2):
                    pe.matmul(bank[0:ROWS[tt], 2 + 2 * i + n, :], late_act[:, C0[tt]:C0[tt] + ROWS[tt]],
                              late_d[:, 512 * n:512 * (n + 1)], start=True, stop=True).then_inc(lt_pe[L], 1)

        def late_act_part(act, L, tiles, nt, c, e, fc):
            act.wait_ge(lt_ev[L], e * (8 * nt) + (2 * nt * fc + 1))
            cols = slice(P * fc, P * (fc + 1))
            for dst, w in ((late_g, moe_w_gate), (late_u, moe_w_up)):
                act.dma_start(dst, w[L][bass.ds(e, 1)].rearrange("e (kc p) n -> p (e kc) n", p=P)[:, :, cols]).then_inc(late_in[L], 16)
            act.dma_start(late_d, moe_w_down[L][bass.ds(e, 1)].rearrange("e (fc p) n -> p (e fc) n", p=P)[:, fc, :]).then_inc(late_in[L], 16)
            act.wait_ge(lt_g[L], e * 4 + fc + 1)
            act.activation(late_act[:, c:T], bank[:, 0, c:T], ACT.Silu).then_inc(lt_s[L], 1)

        def late_dve(dve, L, tiles, nt, c, e, fc):
            dve.wait_ge(lt_s[L], e * 4 + fc + 1)
            dve.wait_ge(lt_u[L], e * 4 + fc + 1)
            dve.tensor_tensor(late_act[:, c:T], late_act[:, c:T], bank[:, 1, c:T], ALU.mult).then_inc(lt_m[L], 1)
            for i, tt in enumerate(tiles):
                for n in range(2):
                    r = ROWS[tt]
                    dve.wait_ge(lt_pe[L], e * (8 * nt) + (2 * nt * fc + 2 * i + n + 1))
                    y = yacc[0:r, tt, 512 * n:512 * (n + 1)]
                    dve.scalar_tensor_tensor(y, bank[0:r, 2 + 2 * i + n, :], late_w[0:r, tt, bass.ds(e, 1)], y,
                                             ALU.mult, ALU.add).then_inc(lt_ev[L], 1)

        def exponents(dve, lv, link):
            if lv <= len(LEVELS):
                w = (LEVELS + (P,))[lv] if lv else LEVELS[0]
                if lv == len(LEVELS):
                    w = P
                b = halves(bT[:, :, N_META:T], w)
                m = SEQ // (2 * w)
                end = b[:, :, :, w - 1:w].to_broadcast([P, HEADS, m, w])
                link(dve.tensor_tensor(halves(dec, w)[:, :, :, 0:w], end, b[:, :, :, 0:w], ALU.subtract))
                dve.tensor_tensor(halves(dec, w)[:, :, :, w:2 * w], b[:, :, :, w:2 * w], end, ALU.subtract).then_inc(lv_d, 1)
            else:
                end = bT[:, :, N_META - 1:N_META]
                dve.tensor_tensor(la[:, :, 0:N_META], end.to_broadcast([P, HEADS, N_META]), bT[:, :, 0:N_META],
                                  ALU.subtract).then_inc(gla_b, 1)
                dve.tensor_tensor(dec, bT[:, :, N_META:T], end.to_broadcast([P, HEADS, SEQ]), ALU.subtract).then_inc(lv_d, 1)

        def attend(dve, lv):
            for tt in range(2):
                dve.wait_ge(lv_pe, 2 * lv + tt + 1)
                if lv:
                    dve.wait_ge(lv_ev, 2 * lv + tt - 1)
                dve.copy_predicated(att[:, HEADS * tt:HEADS * (tt + 1), :],
                                    level_mask[:, lv, :].unsqueeze(1).to_broadcast([P, HEADS, P]),
                                    bank[:, 2 * (lv % 2) + tt, :].rearrange("p (h t) -> p h t", h=HEADS)).then_inc(lv_ev, 1)

        @block.sync
        def _(sp):
            def used(n):
                if n < 6:
                    return [(pj0_pe, 4), (pj0_pe, 8), (pj0_pe, 11), (pj0_pe, 15), (mix_pe, 5), (mix_pe, 5)][n]
                m = n - BASE_ODD
                if m < 0:
                    return used_expert(0, NG - 1, m + GROUP_UNITS)
                return [(pj1_pe, 12), (pj1_pe, 16), (pj1_pe, 17), (pj1_pe, 18), (pj1_pe, 20), (pj1_pe, 22),
                        (mix_pe, 9), (mix_pe, 9)][m]

            def used_expert(layer, g, i):
                if i < 8:
                    return (gate_pe, up_pe)[i // 2 % 2][layer], g * 2 + (i // 4 + 1)
                return d_pe[layer], g * 4 + 2 * (i // 2 - 3)

            def load(n, src):
                if n >= NR:
                    sp.wait_ge(*used(n - NR))
                sp.dma_start(unit(n), src).then_inc(ring_in[n % NR], 16)

            def experts(layer):
                base = BASE_MOE[layer]

                def group(g):
                    order = [(k, e) for pair in (0, 2) for k in "gu" for e in (pair, pair + 1)] + [("d", e) for e in range(GRP)]
                    for i, (kind, e) in enumerate(order):
                        w = {"g": moe_w_gate, "u": moe_w_up, "d": moe_w_down}[kind]
                        kc = 4 if kind == "d" else KC
                        src = w[layer][bass.ds(g * GRP + e, 1)].rearrange("e (kc p) n -> p (e kc) n", p=P)
                        dst = ring[:, (base + i) % NR, :].rearrange("p (kc n) -> p kc n", kc=kc)
                        if i >= NR:
                            sp.wait_ge(*used_expert(layer, g, i - NR))
                        elif isinstance(g, int):
                            sp.wait_ge(*used(base + i - NR))
                        else:
                            sp.wait_ge(*used_expert(layer, g - 1, i - NR + GROUP_UNITS))
                        sp.dma_start(dst, src).then_inc(ring_in[(base + i) % NR], 16)

                group(0)
                with sp.Fori(1, NG) as g:
                    group(g)

            sp.dma_start(htok[0:N_META, 2, :], meta[:, :]).then_inc(meta_in, 16)
            for tt in range(2):
                sp.dma_start(htok[:, tt, :], x[0, P * tt:P * (tt + 1), :]).then_inc(x_in, 16)
            sp.dma_start(unit(0)[:, :, 0:256], in_unit(even_w_in, 1)[:, :, 0:256]).then_inc(first_half, 16)
            sp.dma_start(unit(0)[:, :, 256:512], in_unit(even_w_in, 1)[:, :, 256:512]).then_inc(ring_in[0], 16)
            for n, block_of_w in ((1, 2), (2, 3), (3, 0)):
                load(n, in_unit(even_w_in, block_of_w))
            for n in range(2):
                load(4 + n, in_unit(even_w_out, n))
            experts(0)
            for n in range(6):
                load(BASE_ODD + n, in_unit(odd_w_in, n))
            for n in range(2):
                load(BASE_ODD + 6 + n, in_unit(odd_w_out, n))
            experts(1)
            for tt in range(2):
                normed(sp, 3 + 3 + 2 + tt + 1)
                sp.dma_start(out[0, P * tt:P * (tt + 1), :], htok[:, tt, :]).then_inc(stored, 16)
            sp.wait_ge(stored, 32)

        @block.gpsimd
        def _(pool):
            count = [0]

            def link(ins):
                count[0] += 1
                ins.then_inc(pool_c, 1)
                pool.wait_ge(pool_c, count[0])

            def load_gain(k):
                g, b = ((ln_mix_g, ln_mix_b), (ln_ffn_g, ln_ffn_b))[k % 2]
                if k:
                    normed(pool, (0, 3, 6, 8)[k])
                pool.dma_start(gain[:, 0, :], g[k // 2].partition_broadcast(P)).then_inc(gain_in, 16)
                pool.dma_start(gain[:, 1, :], b[k // 2].partition_broadcast(P)).then_inc(gain_in, 16)

            def norm_shift(k, tiles):
                for i, tt in enumerate(tiles):
                    r = ROWS[tt]
                    pool.wait_ge(xg_ok, (0, 3, 6, 8)[k] + i + 1)
                    pool.tensor_tensor(htok[0:r, tt, 0:512], htok[0:r, tt, 0:512], gain[0:r, 1, 0:512], ALU.add).then_inc(h_left, 1)

            link(pool.memset(ident[:, :], 0.0))
            pool.affine_select(out=ident[:, :], in_=ident[:, :], compare_op=ALU.not_equal, fill=1.0, base=0,
                               pattern=[[-1, P]], channel_multiplier=1).then_inc(const_ok, 1)
            pool.memset(ones_bf[:, :], 1.0).then_inc(const_ok, 1)
            link(pool.memset(before_bf[:, :], 1.0))
            pool.affine_select(out=before_bf[:, :], in_=before_bf[:, :], compare_op=ALU.is_ge, fill=0.0, base=-1,
                               pattern=[[1, P]], channel_multiplier=-1).then_inc(const_ok, 1)
            pool.iota(iota_slot[:, :], pattern=[[1, SLOTS]], base=1 + CAP - SLOTS, channel_multiplier=0,
                      allow_small_or_imprecise_dtypes=True).then_inc(const_ok, 1)
            pool.iota(iota_g[:, :], pattern=[[-1, NG]], base=NG, channel_multiplier=0,
                      allow_small_or_imprecise_dtypes=True).then_inc(const_ok, 1)
            link(pool.memset(earlier[:, :, :], 1.0))
            link(pool.affine_select(out=earlier[:, :, :], in_=earlier[:, :, :], compare_op=ALU.is_ge, fill=0.0, base=-1,
                                    pattern=[[1, GRP], [-1, GRP]], channel_multiplier=0))
            link(pool.memset(zpool[:, :, 0:N_META], 0.0))
            link(pool.memset(poolA[:, :, 0:N_META], 0.0))
            pool.memset(poolB[:, :, 0:N_META], 0.0).then_inc(const_ok, 1)
            for tt in range(3):
                link(pool.iota(dist[:, tt, :], pattern=[[1, T]], base=-C0[tt], channel_multiplier=-1,
                               allow_small_or_imprecise_dtypes=True))
                pool.affine_select(out=dist[:, tt, :], in_=dist[:, tt, :], compare_op=ALU.is_ge, fill=NEG, base=C0[tt],
                                   pattern=[[-1, T]], channel_multiplier=1).then_inc(const_ok, 1)
                if tt == 1:
                    load_gain(0)
            for g, w in enumerate(WINDOWS):
                link(pool.iota(pcount[:, g, :], pattern=[[1, N_META]], base=1, channel_multiplier=0,
                               allow_small_or_imprecise_dtypes=True))
                pool.tensor_scalar(pcount[:, g, :], pcount[:, g, :], float(w), None, ALU.min).then_inc(const_ok, 1)
            pool.iota(iota_i[:, 0:P], pattern=[[1, P]], base=0, channel_multiplier=0).then_inc(const_ok, 1)
            pool.iota(row_i[:, :], pattern=[[0, P]], base=0, channel_multiplier=1).then_inc(const_ok, 1)

            pool.wait_ge(lam_s, 4)
            for i, g in enumerate((3, 2, 1, 0)):
                job_out(pool, J0, out0, 11 + i)
                src = zpool
                for k in range(g + 1):
                    dst = (poolA, poolB)[k % 2]
                    link(pool.tensor_tensor(dst[:, g, N_META:PADW], src[:, g, N_META:PADW],
                                            src[:, g, N_META - 2 ** k:PADW - 2 ** k], ALU.add))
                    src = dst
                link(pool.tensor_scalar(src[:, g, 2 * N_META:PADW], src[:, g, 2 * N_META:PADW], 1.0 / WINDOWS[g], None, ALU.mult))
                link(pool.tensor_tensor(src[:, g, N_META:2 * N_META], src[:, g, N_META:2 * N_META], pcount[:, g, :], ALU.mult))
                pool.tensor_tensor(src[:, g, N_META:PADW], src[:, g, N_META:PADW], zpool[:, g, N_META:PADW],
                                   ALU.subtract).then_inc(pooled, 1)
            norm_shift(0, (2, 0, 1))
            load_gain(1)
            normed(pool, 3)
            pool.dma_start(glw, odd_w_in[0][:, 3072:3072 + GLA_RANK].rearrange("(kc p) n -> p kc n", p=P)).then_inc(par1_in, 16)
            pool.dma_start(g2w[0:GLA_RANK, :], gla_gate_w2[0]).then_inc(par1_in, 16)
            pool.dma_start(gb_sb, gla_gate_b[0].rearrange("(h k) -> k h", k=P),
                           allow_slow_non_contiguous=True).then_inc(par1_in, 16)
            pool.dma_start(hn_b, gla_head_norm[0].partition_broadcast(P)).then_inc(par1_in, 16)
            norm_shift(1, (0, 2, 1))
            load_gain(2)
            for lv in range(len(LEVELS)):
                key_factors(pool, lv)
            pool.wait_ge(rg_s, 2)
            for tt in range(2):
                pool.tensor_tensor(rt[:, tt, :].rearrange("p (h v) -> p h v", h=HEADS),
                                   rt[:, tt, :].rearrange("p (h v) -> p h v", h=HEADS),
                                   hn_b.unsqueeze(1).to_broadcast([P, HEADS, GLA_DV]), ALU.mult).then_inc(rg_ok, 1)
            norm_shift(2, (0, 1))
            load_gain(3)
            norm_shift(3, (0, 1))

        @block.tensor
        def _(pe):
            def turn_tile(k, i, tt):
                if k == 0:
                    pe.wait_ge(meta_in if tt == 2 else x_in, 16 if tt == 2 else 32)
                    if i == 0:
                        pe.wait_ge(const_ok, 1)
                else:
                    normed(pe, {1: 0, 2: 3, 3: 6}[k] + i + 1)
                for kc in range(KC):
                    c = P * (kc % 4)
                    mm = pe.transpose(bank[:, TURN_BANK[i] + kc // 4, c:c + ROWS[tt]],
                                      htok[0:ROWS[tt], tt, P * kc:P * (kc + 1)], ident[0:ROWS[tt], 0:ROWS[tt]])
                mm.then_inc(hT_pe, 1)

            def hT_out(k, i):
                pe.wait_ge(hT_act, 3 * k + i + 1)

            def by_token(dst, src, cols, rows, w, used=None):
                for kc in range(KC):
                    mm = pe.matmul(dst, src[:, kc, cols:cols + rows], w[:, kc, :], start=(kc == 0), stop=(kc == KC - 1))
                return mm

            def by_channel(dst, w, src, kcs=KC):
                for kc in range(kcs):
                    mm = pe.matmul(dst, w(kc), src(kc), start=(kc == 0), stop=(kc == kcs - 1))
                return mm

            def mix_out(src, first_unit, tiles, base_col, kcs):
                for tt in tiles:
                    for n in range(2):
                        u = unit(first_unit + n)
                        for kc in kcs:
                            mm = pe.matmul(bank[:, 2 * tt + n, :], src[:, kc, C0[tt] - base_col:C0[tt] - base_col + P], u[:, kc, :],
                                           start=(kc == 0), stop=(kc == KC - 1), skip_group_check=True)
                        if kcs[-1] == KC - 1:
                            mm.then_inc(mix_pe, 1)

            def router(layer, tiles):
                k = 1 + 2 * layer
                if layer == 0:
                    pe.wait_ge(par_in, 9 * 16)
                for i, tt in enumerate(tiles):
                    turn_tile(k, i, tt)
                    hT_out(k, i)
                    c = slice(C0[tt], C0[tt] + ROWS[tt])
                    mm = by_channel(bank[0:E, 6, c], lambda kc: rw[:, kc, :], lambda kc: hT[:, kc, c])
                mm.then_inc(lgt_pe, 1)
                pe.wait_ge(lgt_ev, layer + 1)
                for tt in tiles:
                    mm = pe.transpose(bank[0:ROWS[tt], 7, E * tt:E * tt + E], lgT[:, C0[tt]:C0[tt] + ROWS[tt]], ident[0:E, 0:E])
                mm.then_inc(lg_pe, 1)
                pe.wait_ge(pick_ok, layer + 1)
                if layer == 0:
                    pe.wait_ge(const_ok, 3)
                order = sorted(tiles)
                for tt in order + [3]:
                    rows = P if tt == 3 else ROWS[tt]
                    prev = [t for t in order if t < tt]
                    terms = [(ones_bf[0:ROWS[t], 0:rows], t) for t in prev]
                    if tt < 3:
                        terms.append((before_bf[0:ROWS[tt], 0:rows], tt))
                    for i, (lhs, t) in enumerate(terms):
                        mm = pe.matmul(bank[0:rows, 7 if tt == 3 else 5, E * tt:E * tt + E], lhs, picked_bf[0:ROWS[t], t, :],
                                       start=(i == 0), stop=(i == len(terms) - 1))
                mm.then_inc(pos_pe, 1)

            def experts(layer, tiles):
                base = BASE_MOE[layer]
                nt = len(tiles)
                ns = len(scatter_order(layer, False))
                L = layer

                def gather(g_next):
                    pe.wait_ge(s_ready[L], nt * (g_next + 1))
                    for f in range(4):
                        if f >= 2:
                            pe.wait_ge(gth_ev[L], 4 * g_next + f - 1)
                        for half in range(2):
                            kc = 2 * f + half
                            for i, tt in enumerate(tiles):
                                mm = pe.matmul(bank[:, 4 + f % 2, 256 * half:256 * (half + 1)],
                                               htok[0:ROWS[tt], tt, P * kc:P * (kc + 1)], onehot[0:ROWS[tt], tt, :],
                                               start=(i == 0), stop=(i == nt - 1))
                        mm.then_inc(gth_pe[L], 1)

                def ring_wait(g, i):
                    n = base + i
                    pe.wait_ge(ring_in[n % NR], g * (16 * GROUP_UNITS // NR) + 16 * (n // NR + 1))

                def down_unit(i):
                    return ring[:, (base + i) % NR, :].rearrange("p (fc n) -> p fc n", fc=4)

                def group(g, last):
                    for p in range(2):
                        if p == 0:
                            pe.wait_ge(gth_ev[L], g * 4 + 4)
                        for k in range(2):
                            for e in range(2):
                                ring_wait(g, 4 * p + 2 * k + e)
                            for kc in range(KC):
                                for e in range(2):
                                    s0 = SLOTS * (2 * p + e)
                                    mm = pe.matmul(bank[SLOTS * e:SLOTS * (e + 1), 2 * p + k, :], xg[:, kc, s0:s0 + SLOTS],
                                                   unit(base + 4 * p + 2 * k + e)[:, kc, :],
                                                   start=(kc == 0), stop=(kc == KC - 1))
                            mm.then_inc((gate_pe, up_pe)[k][L], 1)

                    def turn_pair(p):
                        pe.wait_ge(act_ok[L], g * 2 + p + 1)
                        for fc in range(4):
                            mm = pe.transpose(bank[:, 2 * p, P * fc:P * (fc + 1)], act_sb[:, p, P * fc:P * (fc + 1)], ident[:, :])
                        mm.then_inc(t_pe[L], 1)
                        pe.wait_ge(sw_ready[L], g * nt + nt)
                        for tt in sorted(tiles):
                            mm = pe.transpose(bank[:, 2 * p + 1, C0[tt]:C0[tt] + ROWS[tt]],
                                              whot[0:ROWS[tt], tt, P * p:P * (p + 1)], ident[0:ROWS[tt], 0:ROWS[tt]])
                        mm.then_inc(w_pe[L], 1)

                    def down(p):
                        pe.wait_ge(t_ev[L], g * 2 + p + 1)
                        for e in range(2):
                            ring_wait(g, 8 + 2 * p + e)
                        for n in range(2):
                            for fc in range(4):
                                for e in range(2):
                                    mm = pe.matmul(bank[SLOTS * e:SLOTS * (e + 1), 6 + n, :], actT[:, fc, SLOTS * e:SLOTS * (e + 1)],
                                                   down_unit(8 + 2 * p + e)[:, fc, 512 * n:512 * (n + 1)],
                                                   start=(fc == 0), stop=(fc == 3))
                            mm.then_inc(d_pe[L], 1)

                    def scatter(p):
                        pe.wait_ge(w_ev[L], g * 2 + p + 1)
                        for i, (tt, n) in enumerate(scatter_order(L, last and p == 1)):
                            s = ns * p + i
                            if s >= 2:
                                pe.wait_ge(sc_ev[L], g * (2 * ns) + s - 1)
                            elif last:
                                pe.wait_ge(sc_ev[L], g * (2 * ns))
                            else:
                                pe.wait_ge(gth_ev[L], g * 4 + 4 + 3 + s)
                            pe.wait_ge(d_ev[L], g * 4 + 2 * p + min(n, 1) + 1)
                            if tt == 2:
                                for q in range(4):
                                    mm = pe.matmul(bank[32 * q:32 * (q + 1), 4 + s % 2, 0:SEQ], whotT[:, p, 0:32],
                                                   o_sb[:, SEQ * q:SEQ * (q + 1)], start=True, stop=True, skip_group_check=True)
                            else:
                                mm = pe.matmul(bank[:, 4 + s % 2, :], whotT[:, p, C0[tt]:C0[tt] + P],
                                               o_sb[:, 512 * n:512 * (n + 1)], start=True, stop=True)
                            mm.then_inc(sc_pe[L], 1)

                    turn_pair(0)
                    if not last:
                        gather(g + 1)
                    down(0)
                    turn_pair(1)
                    scatter(0)
                    down(1)
                    scatter(1)

                gather(0)
                late(pe, L)
                with pe.Fori(0, NG - 1) as g:
                    group(g, False)
                group(NG - 1, True)

            for i, tt in enumerate((2, 0, 1)):
                turn_tile(0, i, tt)
            hT_out(0, 2)

            def job0(n):
                kind, m, _ = J0[n]
                if n >= 8:
                    job_out(pe, J0, out0, (4, 5, 7)[n - 8] if n < 11 else n - 1)
                u = unit("QKVU".index(kind))
                if n < 2:
                    pe.wait_ge(first_half, 16)
                else:
                    arrived(pe, "QKVU".index(kind))
                b = bank0(n)
                if kind != "V":
                    mm = by_channel(bank[:, b, 0:T], lambda kc: u[:, kc, P * m:P * (m + 1)], lambda kc: hT[:, kc, :])
                elif m == 2:
                    mm = meta_quarters(pe, bank[:, b, :], hT, lambda kc, q: u[:, kc, P * q:P * (q + 1)])
                else:
                    mm = by_token(bank[:, b, :], hT, C0[m], P, u)
                mm.then_inc(pj0_pe, 1)

            def scores(i):
                tt, hp = STEPS[i]
                nk = C0[tt] + ROWS[tt]
                if i == 0:
                    job_out(pe, J0, out0, 6)
                    job_out(pe, J0, out0, 7)
                else:
                    pe.wait_ge(at_b, 2 * i)
                for j in range(4):
                    h, m = 2 * hp + j // 2, j % 2
                    mm = pe.matmul(bank[0:ROWS[tt], j, 0:nk], zq[64 * m:64 * (m + 1), h, C0[tt]:C0[tt] + ROWS[tt]],
                                   zk[64 * m:64 * (m + 1), h, 0:nk], start=True, stop=True)
                mm.then_inc(at_s, 1)

            def probs_out(i):
                tt, hp = STEPS[i]
                rows = ROWS[tt]
                ks = KEYS[tt]
                if i == 0:
                    job_out(pe, J0, out0, 10)
                pe.wait_ge(at_pd, 2 * i + 2)
                for j in range(2):
                    for kt in ks:
                        mm = pe.transpose(bank[0:ROWS[kt], 4 + j, P * kt:P * kt + rows],
                                          pd[0:rows, j, C0[kt]:C0[kt] + ROWS[kt]], ident[0:rows, 0:rows])
                mm.then_inc(at_t, 1)
                pe.wait_ge(at_te, i + 1)
                if i >= 1:
                    pe.wait_ge(at_oe, i)
                for j in range(2):
                    h = 2 * hp + j
                    for a, kt in enumerate(ks):
                        mm = pe.matmul(bank[0:rows, 6, P * j:P * (j + 1)], pT[0:ROWS[kt], j, kt, 0:rows],
                                       v0[0:ROWS[kt], kt, P * h:P * (h + 1)], start=(a == 0), stop=(a == len(ks) - 1))
                mm.then_inc(at_o, 1)

            for n in range(8):
                job0(n)
            scores(0)
            job0(8)
            job0(9)
            scores(1)
            job0(10)
            probs_out(0)
            for i in range(2, 6):
                scores(i)
                job0(9 + i)
                probs_out(i - 1)
            for i, g in enumerate((3, 2, 1, 0)):
                pe.wait_ge(pooled, i + 1)
                if i == 0:
                    job_out(pe, J0, out0, 14)
                else:
                    pe.wait_ge(poolev, i)
                pe.matmul(bank[:, 7, 0:T], pw_sb[:, g, :], (poolA, poolB)[g % 2][:, g, N_META:PADW],
                          start=True, stop=True).then_inc(poolmm, 1)
                if i == 1:
                    probs_out(5)
            pe.wait_ge(poolev, 4)
            for n in range(2):
                arrived(pe, 4 + n)
            mix_out(yT, 4, (0, 1), 0, range(4))
            for i, tt in enumerate((2, 0, 1)):
                pe.wait_ge(o_n, i + 1)
                for h in range(HEADS):
                    mm = pe.transpose(bank[:, 5 + i, P * h:P * h + ROWS[tt]], o_tok[0:ROWS[tt], tt, P * h:P * (h + 1)],
                                      ident[0:ROWS[tt], 0:ROWS[tt]])
                mm.then_inc(yt_pe, 1)
            pe.wait_ge(yt_act, 2)
            meta_quarters(pe, bank[:, 4, :], yT, lambda kc, q: unit(4 + q // 2)[:, kc, SEQ * (q % 2):SEQ * (q % 2 + 1)]).then_inc(mix_pe, 1)
            mix_out(yT, 4, (0,), 0, range(4, KC))
            pe.wait_ge(yt_dve, 1)
            mix_out(yT, 4, (1,), 0, range(4, KC))
            router(0, (2, 0, 1))
            experts(0, (2, 0, 1))

            def job1(n):
                kind, m, _, b = J1[n]
                before = [i for i in range(n) if J1[i][3] == b]
                if before:
                    job_out(pe, J1, out1, before[-1])
                if kind == "G":
                    mm = by_channel(bank[0:GLA_RANK, b, 0:T], lambda kc: glw[:, kc, :], lambda kc: hT[:, kc, :])
                if kind == "A":
                    job_out(pe, J1, out1, 3)
                    mm = pe.matmul(bank[:, b, 0:T], g2w[0:GLA_RANK, P * m:P * (m + 1)], glr[0:GLA_RANK, :], start=True, stop=True)
                if kind in "QK":
                    u = BASE_ODD + (kind == "K")
                    arrived(pe, u)
                    c = N_META if kind == "Q" else 0
                    mm = by_channel(bank[:, b, 0:T - c], lambda kc: unit(u)[:, kc, P * m:P * (m + 1)], lambda kc: hT[:, kc, c:T])
                if kind in "VR":
                    half, tt = m
                    u = BASE_ODD + (2 if kind == "V" else 4) + half
                    arrived(pe, u)
                    mm = by_token(bank[:, b, :], hT, C0[tt], P, unit(u))
                if kind == "M":
                    mm = meta_quarters(pe, bank[:, b, :], hT,
                                       lambda kc, q: unit(BASE_ODD + 2 + q // 2)[:, kc, SEQ * (q % 2):SEQ * (q % 2 + 1)])
                mm.then_inc(pj1_pe, 1)

            nl = len(LEVELS)

            def level(st):
                b = 2 * (st % 2)
                if st >= 2:
                    pe.wait_ge(lv_ev, 2 * min(st - 1, nl + 1))
                if st < nl:
                    pe.wait_ge(lv_q, st + 1)
                    pe.wait_ge(lv_k, st + 2)
                if st <= nl:
                    for tt in range(2):
                        for h in range(HEADS):
                            if st < nl:
                                a, c = kl[:, h, P * tt:P * (tt + 1)], ql[:, h, P * tt:P * (tt + 1)]
                            else:
                                a, c = kT[:, h, C0[tt]:C0[tt] + P], qT[:, h, P * tt:P * (tt + 1)]
                            mm = pe.matmul(bank[:, b + tt, P * h:P * (h + 1)], a, c, start=True, stop=True)
                        mm.then_inc(lv_pe, 1)
                if st == nl + 1:
                    pe.wait_ge(lv_q, nl + 1)
                    for h in range(HEADS):
                        mm = pe.matmul(bank[:, b, P * h:P * (h + 1)], kl[:, h, 0:P], ql[:, h, P:SEQ], start=True, stop=True)
                    mm.then_inc(lv_pe, 1)
                if st == nl + 2:
                    pe.wait_ge(lv_q, nl + 2)
                    for h in range(HEADS):
                        mm = pe.matmul(bank[0:N_META, b + h // 2, SEQ * (h % 2):SEQ * (h % 2 + 1)], kl[:, h, 0:N_META],
                                       ql[:, h, :], start=True, stop=True)
                    mm.then_inc(lv_pe, 1)

            turn_tile(2, 0, FFN_ORDER[0])
            hT_out(2, 0)
            job1(0)
            job1(1)
            turn_tile(2, 1, FFN_ORDER[1])
            hT_out(2, 1)
            job1(2)
            turn_tile(2, 2, FFN_ORDER[2])
            hT_out(2, 2)
            pe.wait_ge(par1_in, 4 * 16)
            for n in range(3, NLV):
                job1(n)
            for st in range(nl + 3):
                if NLV + st < len(J1):
                    job1(NLV + st)
                level(st)
            pe.wait_ge(lv_ev, 2 * (nl + 1))
            pe.wait_ge(lv_act, 3)
            for n in (2, NLV, NLV + 1):
                job_out(pe, J1, out1, n)
            for tt in range(2):
                for c in range(2):
                    for h in (2 * c, 2 * c + 1):
                        dst = bank[:, 2 * tt + c, GLA_DV * (h % 2):GLA_DV * (h % 2 + 1)]
                        vh = vt[:, :, GLA_DV * h:GLA_DV * (h + 1)]
                        pe.matmul(dst, attM[0:N_META, h, P * tt:P * (tt + 1)], vh[0:N_META, 2, :], start=True, stop=False)
                        if tt == 1:
                            pe.matmul(dst, att01[:, h, :], vh[:, 0, :], start=False, stop=False)
                        mm = pe.matmul(dst, att[:, HEADS * tt + h, :], vh[:, tt, :], start=False, stop=True)
                    mm.then_inc(go_pe, 1)
            for tt in range(2):
                pe.wait_ge(ogt_ok, HEADS * (tt + 1))
                if tt == 0:
                    pe.wait_ge(go_ev, 4)
                    for n in range(len(J1) - 2, len(J1)):
                        job_out(pe, J1, out1, n)
                for c in range(KC):
                    mm = pe.transpose(bank[:, c, P * tt:P * (tt + 1)], og[:, tt, P * c:P * (c + 1)], ident[:, :])
                    if tt == 1:
                        mm.then_inc(ogt_pe, 1)
            pe.wait_ge(ogt_ev, 8)
            for n in range(2):
                arrived(pe, BASE_ODD + 6 + n)
            mix_out(ogT, BASE_ODD + 6, (0, 1), N_META, range(KC))
            router(1, (0, 1))
            experts(1, (0, 1))

        @block.scalar
        def _(act):
            count = [0]

            def link(ins):
                count[0] += 1
                ins.then_inc(act_c, 1)
                act.wait_ge(act_c, count[0])

            act.dma_start(pw_sb, pool_w[0].rearrange("g c d -> c g d")).then_inc(par_in, 16)
            act.dma_start(small[:, 8:12], pool_scale[0].rearrange("(g c) -> c g", c=P),
                          allow_slow_non_contiguous=True).then_inc(par_in, 16)
            for i, v in enumerate((diff_lq1, diff_lk1, diff_lq2, diff_lk2)):
                act.dma_start(lam_v[:, i, :], v[0].partition_broadcast(P)).then_inc(par_in, 16)
            act.dma_start(sub_b[:, :], diff_subln[0].partition_broadcast(P)).then_inc(par_in, 16)
            act.dma_start(rw[:, :, :], router_w.rearrange("(kc p) e -> p kc e", p=P)).then_inc(par_in, 16)
            act.dma_start(rbias[:, :], router_bias.partition_broadcast(P)).then_inc(par_in, 16)

            def turn_tile(k, i, tt):
                act.wait_ge(hT_pe, 3 * k + i + 1)
                b = TURN_BANK[i]
                act.copy(hT[:, :, C0[tt]:C0[tt] + ROWS[tt]],
                         bank[:, b:b + 2, :].rearrange("p b (c t) -> p (b c) t", c=4)[:, :, 0:ROWS[tt]]).then_inc(hT_act, 1)

            def norm_tile(k, i, tt):
                n = (0, 3, 6, 8)[k] + i + 1
                r = ROWS[tt]
                act.wait_ge(var_ok, n)
                act.activation(rstd[0:r, tt, :], mv[0:r, tt, 1:2], ACT.Sqrt, bias=eps_ln[0:r, :]).then_inc(sd_ok, 1)
                act.wait_ge(nb_ok, n)
                for half in range(2):
                    c = slice(512 * half, 512 * (half + 1))
                    act.activation(htok[0:r, tt, c], (htok if k % 2 == 0 else yacc)[0:r, tt, c], ACT.Identity,
                                   bias=nbias[0:r, tt, :], scale=rstd[0:r, tt, :]).then_inc(xn_ok, 1)

            def router(layer, tiles):
                k = 1 + 2 * layer
                for i, tt in enumerate(tiles):
                    if i == len(tiles) - 1:
                        norm_tile(k - 1, i, tt)
                    turn_tile(k, i, tt)
                act.activation(small[:, 30:31], one, ACT.Exp)
                c = 0 if layer == 0 else N_META
                act.wait_ge(lgt_pe, layer + 1)
                act.copy(lgT[:, c:T], bank[0:E, 6, c:T]).then_inc(lgt_ev, 1)
                act.wait_ge(lg_max, layer + 1)
                act.activation(pr[:, 0:len(tiles), :], lg[:, 0:len(tiles), :], ACT.Exp).then_inc(lg_exp, 1)
                for tt in range(2):
                    act.mul(yacc[:, tt, :], htok[:, tt, :], ALPHA).then_inc(yinit, 1)
                if layer == 0:
                    act.wait_ge(ym_zero, 1)
                    for q in range(4):
                        act.mul(ymeta[32 * q:32 * q + N_META, :], htok[0:N_META, 2, SEQ * q:SEQ * (q + 1)], ALPHA).then_inc(yinit, 1)
            def experts(layer, tiles):
                L = layer

                def gather_out(g):
                    for f in range(4):
                        act.wait_ge(gth_pe[L], g * 4 + f + 1)
                        act.copy(xg[:, 2 * f:2 * f + 2, :],
                                 bank[:, 4 + f % 2, :].rearrange("p (a b) -> p a b", a=2)).then_inc(gth_ev[L], 1)

                def group(g, last):
                    for p in range(2):
                        act.wait_ge(gate_pe[L], g * 2 + p + 1)
                        act.activation(act_sb[:, p, :], bank[:, 2 * p, :], ACT.Silu).then_inc(silu_ok[L], 1)
                    for p in range(2):
                        act.wait_ge(t_pe[L], g * 2 + p + 1)
                        act.copy(actT, bank[:, 2 * p, :].rearrange("p (a b) -> p a b", a=4)).then_inc(t_ev[L], 1)
                        if p == 0 and not last:
                            gather_out(g + 1)
                        for n in range(2):
                            act.wait_ge(d_pe[L], g * 4 + 2 * p + n + 1)
                            act.copy(o_sb[:, 512 * n:512 * (n + 1)], bank[:, 6 + n, :]).then_inc(d_ev[L], 1)

                gather_out(0)
                late(act, L)
                with act.Fori(0, NG - 1) as g:
                    group(g, False)
                group(NG - 1, True)

            for i, tt in enumerate((2, 0, 1)):
                turn_tile(0, i, tt)

            def job0(n):
                kind, m, _ = J0[n]
                act.wait_ge(pj0_pe, n + 1)
                b = bank0(n)
                if kind in "QK":
                    act.copy((zq, zk)[kind == "K"][:, m, :], bank[:, b, 0:T]).then_inc(pj0_act, 1)
                elif kind == "U":
                    act.copy(zpool[:, m, N_META:PADW], bank[:, b, 0:T]).then_inc(pj0_act, 1)
                elif m == 2:
                    for q in range(4):
                        cp = act.copy(v0[0:N_META, 2, P * q:P * (q + 1)], bank[32 * q:32 * q + N_META, b, 0:P])
                        if q < 3:
                            link(cp)
                    cp.then_inc(pj0_act, 1)
                else:
                    act.copy(v0[:, m, :], bank[:, b, :]).then_inc(pj0_act, 1)

            def exps(i):
                tt, hp = STEPS[i]
                r, nk = ROWS[tt], C0[tt] + ROWS[tt]
                act.wait_ge(at_m, i + 1)
                for j in range(4):
                    sv = s_sb[0:r, i % 2, j, 0:nk]
                    act.activation(sv, sv, ACT.Exp, bias=mx[0:r, i, j:j + 1], scale=ATT_SCALE,
                                   accum_out=sums[0:r, i, j:j + 1]).then_inc(at_e, 1)

            def probs_copy(i):
                tt, hp = STEPS[i]
                rows = ROWS[tt]
                act.wait_ge(at_t, i + 1)
                n = (1, 2, 0)[tt]
                if n:
                    link(act.copy(pT[:, :, 0:n, :], bank[:, 4:6, 0:P * n].rearrange("p b (a c) -> p b a c", c=P)))
                act.copy(pT[0:N_META, :, 2, 0:rows], bank[0:N_META, 4:6, 2 * P:2 * P + rows]).then_inc(at_te, 1)

            for n in range(1, 8, 2):
                job0(n)
            act.wait_ge(lam_e, 2)
            link(act.activation(lam1, lam1, ACT.Exp))
            link(act.activation(lam2, lam2, ACT.Exp))
            exps(0)
            job0(8)
            job0(9)
            exps(1)
            job0(10)
            probs_copy(0)
            for i in range(2, 6):
                exps(i)
                job0(9 + i)
                probs_copy(i - 1)
            for i, g in enumerate((3, 2, 1, 0)):
                act.wait_ge(poolmm, i + 1)
                act.mul(yT[:, g, :], bank[:, 7, 0:T], small[:, 8 + g:9 + g]).then_inc(poolev, 1)
                if i == 1:
                    probs_copy(5)
            act.wait_ge(o_ss, 12)
            act.activation(rstd0, ss0, ACT.Sqrt, bias=eps_rms, scale=1.0 / P).then_inc(o_rs, 1)
            for i, tt in enumerate((2, 0)):
                act.wait_ge(yt_pe, i + 1)
                act.copy(yT[:, 4:8, C0[tt]:C0[tt] + ROWS[tt]],
                         bank[:, 5 + i, :].rearrange("p (h t) -> p h t", h=HEADS)[:, :, 0:ROWS[tt]]).then_inc(yt_act, 1)
            norm_tile(0, 0, 2)
            norm_tile(0, 1, 0)
            router(0, (2, 0, 1))
            experts(0, (2, 0, 1))

            def job1(n):
                kind, m, by, b = J1[n]
                if by != "a":
                    return
                act.wait_ge(pj1_pe, n + 1)
                if kind == "Q":
                    act.mul(qT[:, m, :], bank[:, b, 0:SEQ], GLA_SCALE).then_inc(pj1_act, 1)
                if kind == "K":
                    act.copy(kT[:, m, :], bank[:, b, 0:T]).then_inc(pj1_act, 1)
                if kind in "VR":
                    half, tt = m
                    act.copy((vt if kind == "V" else rt)[:, tt, 512 * half:512 * (half + 1)], bank[:, b, :]).then_inc(pj1_act, 1)
                if kind == "M":
                    for q in range(4):
                        cp = act.copy(vt[0:N_META, 2, SEQ * q:SEQ * (q + 1)], bank[32 * q:32 * q + N_META, b, 0:SEQ])
                        if q < 3:
                            link(cp)
                    cp.then_inc(pj1_act, 1)

            norm_tile(1, 0, FFN_ORDER[0])
            turn_tile(2, 0, FFN_ORDER[0])
            act.wait_ge(sc_ev[0], 10 * NG - 2)
            for q in range(4):
                act.copy(meta_row[0:N_META, SEQ * q:SEQ * (q + 1)], ymeta[32 * q:32 * q + N_META, :]).then_inc(ym_out, 1)
            norm_tile(1, 1, FFN_ORDER[1])
            norm_tile(1, 2, FFN_ORDER[2])
            job1(0)
            job1(1)
            turn_tile(2, 1, FFN_ORDER[1])
            job1(2)
            turn_tile(2, 2, FFN_ORDER[2])
            for h in range(HEADS):
                act.wait_ge(gla_ab, h + 1)
                act.activation(la[:, h, :], la[:, h, :], ACT.Exp, scale=-1.0).then_inc(gla_e, 1)
            act.wait_ge(gla_e, 4)
            for h in range(HEADS):
                act.activation(la[:, h, :], la[:, h, :], ACT.Ln, bias=one).then_inc(gla_ln, 1)

            for n in range(3, NLV):
                job1(n)
            nl = len(LEVELS)
            for st in range(nl + 3):
                if st != nl:
                    d = st if st < nl else st - 1
                    act.wait_ge(lv_d, d + 1)
                    act.activation(dec, dec, ACT.Exp).then_inc(lv_e, 1)
                if st == nl + 2:
                    act.wait_ge(gla_b, 5)
                    act.activation(la[:, :, 0:N_META], la[:, :, 0:N_META], ACT.Exp).then_inc(lv_e, 1)
                if NLV + st < len(J1):
                    job1(NLV + st)
                if st == nl + 2:
                    act.wait_ge(lv_pe, 2 * (nl + 1) + 1)
                    act.copy(att01, bank[:, 2 * ((nl + 1) % 2), :].rearrange("p (h t) -> p h t", h=HEADS)).then_inc(lv_act, 1)
            job_out(act, J1, out1, len(J1) - 1)
            job_out(act, J1, out1, len(J1) - 2)
            act.wait_ge(lv_pe, 2 * (nl + 1) + 2)
            for c in range(2):
                act.copy(attM[0:N_META, 2 * c:2 * c + 2, :],
                         bank[0:N_META, 2 * (nl % 2) + c, :].rearrange("p (h t) -> p h t", h=2)).then_inc(lv_act, 1)
            for tt in range(2):
                act.activation(rt[:, tt, :], rt[:, tt, :], ACT.Silu).then_inc(rg_s, 1)
            act.wait_ge(o_ss, 20)
            act.activation(rstd1, ss1, ACT.Sqrt, bias=eps_rms, scale=1.0 / GLA_DV).then_inc(o_rs, 1)
            for c in range(1, KC, 2):
                act.wait_ge(ogt_pe, c + 1)
                act.copy(ogT[:, c, :], bank[:, c, 0:SEQ]).then_inc(ogt_ev, 1)
            norm_tile(2, 0, 0)
            router(1, (0, 1))
            experts(1, (0, 1))
            norm_tile(3, 0, 0)
            norm_tile(3, 1, 1)

        @block.vector
        def _(dve):
            count = [0]

            def link(ins):
                count[0] += 1
                ins.then_inc(dve_c, 1)
                dve.wait_ge(dve_c, count[0])

            def norm_stats(k, i, tt):
                r = ROWS[tt]
                src = (htok if k % 2 == 0 else yacc)[0:r, tt, :]
                for half in range(2):
                    link(dve.bn_stats(stats[0:r, tt, half, :], src[:, 512 * half:512 * (half + 1)]))
                dve.bn_aggr(mv[0:r, tt, :], stats[0:r, tt, :, :]).then_inc(var_ok, 1)

            def norm_scale(k, i, tt):
                r = ROWS[tt]
                dve.wait_ge(sd_ok, (0, 3, 6, 8)[k] + i + 1)
                link(dve.reciprocal(rstd[0:r, tt, :], rstd[0:r, tt, :]))
                dve.scalar_tensor_tensor(nbias[0:r, tt, :], mv[0:r, tt, 0:1], -1.0, rstd[0:r, tt, :], ALU.mult, ALU.mult).then_inc(nb_ok, 1)

            def norm_gain(k, i, tt):
                r = ROWS[tt]
                n = (0, 3, 6, 8)[k] + i + 1
                if i == 0:
                    dve.wait_ge(gain_in, 32 * (k + 1))
                left, right = (htok[0:r, tt, 512 * half:512 * (half + 1)] for half in range(2))
                dve.wait_ge(xn_ok, 2 * n - 1)
                dve.tensor_tensor(left, left, gain[0:r, 0, 0:512], ALU.mult).then_inc(xg_ok, 1)
                dve.wait_ge(xn_ok, 2 * n)
                link(dve.tensor_tensor(right, right, gain[0:r, 0, 512:D], ALU.mult))
                dve.tensor_tensor(right, right, gain[0:r, 1, 512:D], ALU.add).then_inc(h_right, 1)

            def norm_tile(k, i, tt):
                norm_stats(k, i, tt)
                norm_scale(k, i, tt)
                norm_gain(k, i, tt)

            def mix_tile(done, tt):
                if tt == 2:
                    dve.wait_ge(mix_pe, done + 1)
                    for q in range(4):
                        c = slice(SEQ * q, SEQ * (q + 1))
                        link(dve.scalar_tensor_tensor(htok[0:N_META, 2, c], htok[0:N_META, 2, c], ALPHA,
                                                      bank[32 * q:32 * q + N_META, 4, 0:SEQ], ALU.mult, ALU.add))
                    return
                for n in range(2):
                    dve.wait_ge(mix_pe, done + n + 1)
                    c = slice(512 * n, 512 * (n + 1))
                    link(dve.scalar_tensor_tensor(htok[:, tt, c], htok[:, tt, c], ALPHA, bank[:, 2 * tt + n, :], ALU.mult, ALU.add))

            def router(layer, tiles):
                nt = len(tiles)
                a = slice(0, nt)
                dve.wait_ge(lg_pe, layer + 1)
                if nt == 3:
                    link(dve.tensor_copy(lg[0:N_META, 2, :], bank[0:N_META, 7, 2 * E:3 * E]))
                link(dve.tensor_copy(lg[:, 0:2, :], bank[:, 7, 0:2 * E].rearrange("p (t e) -> p t e", t=2)))
                link(dve.tensor_reduce(r1[:, a, :], lg[:, a, :], AX.X, ALU.max))
                dve.tensor_tensor(lg[:, a, :], lg[:, a, :], r1[:, a, :].to_broadcast([P, nt, E]), ALU.subtract).then_inc(lg_max, 1)
                dve.wait_ge(lg_exp, layer + 1)
                link(dve.tensor_reduce(r1[:, a, :], pr[:, a, :], AX.X, ALU.add))
                link(dve.reciprocal(r1[:, a, :], r1[:, a, :]))
                link(dve.tensor_tensor(pr[:, a, :], pr[:, a, :], r1[:, a, :].to_broadcast([P, nt, E]), ALU.mult))
                link(dve.tensor_tensor(sel[:, a, :], pr[:, a, :], rbias[:, :].unsqueeze(1).to_broadcast([P, nt, E]), ALU.add))
                n = nt * NG
                s4 = sel[:, a, :].rearrange("p t (g c) -> p (t g) c", c=GRP)
                shape = [P, n, GRP, GRP]
                ab, eq, rk = above[:, 0:n, :, :], equal[:, 0:n, :, :], rank[:, 0:n, :]
                j_side, i_side = s4.unsqueeze(2).to_broadcast(shape), s4.unsqueeze(3).to_broadcast(shape)
                dve.tensor_tensor(eq, j_side, i_side, ALU.is_equal).then_inc(eq_ok, 1)
                link(dve.tensor_tensor(ab, j_side, i_side, ALU.is_gt))
                dve.wait_ge(eq_ok, layer + 1)
                link(dve.tensor_tensor(eq, eq, earlier[:, :, :].unsqueeze(1).to_broadcast(shape), ALU.mult))
                link(dve.tensor_tensor(ab, ab, eq, ALU.add))
                link(dve.tensor_reduce(rk, ab, AX.X, ALU.add))
                t4 = t1[:, a, :].rearrange("p t (g c) -> p (t g) c", c=GRP)
                link(dve.scalar_tensor_tensor(t4, rk, 1.5, s4, ALU.is_lt, ALU.mult))
                gv = gs[:, a, :].rearrange("p t g -> p (t g)")
                link(dve.tensor_reduce(gv, t4, AX.X, ALU.add))
                g3 = gs[:, a, :]
                link(dve.tensor_reduce(r1[:, a, :], g3, AX.X, ALU.max))
                link(dve.tensor_tensor(g3, g3, r1[:, a, :].to_broadcast([P, nt, NG]), ALU.is_equal))
                link(dve.tensor_tensor(g3, g3, iota_g[:, :].unsqueeze(1).to_broadcast([P, nt, NG]), ALU.mult))
                link(dve.tensor_reduce(r2[:, a, :], g3, AX.X, ALU.max))
                link(dve.tensor_tensor(ghot[:, a, :], g3, r2[:, a, :].to_broadcast([P, nt, NG]), ALU.is_equal))
                hot = ghot[:, a, :].rearrange("p t g -> p (t g)").unsqueeze(2).to_broadcast([P, n, GRP])
                dve.scalar_tensor_tensor(picked_bf[:, a, :].rearrange("p t (g c) -> p (t g) c", c=GRP), rk, 1.5, hot,
                                         ALU.is_lt, ALU.mult).then_inc(pick_ok, 1)
                dve.wait_ge(pick_ok, layer + 1)
                link(dve.tensor_tensor(weight[:, a, :], pr[:, a, :], picked_bf[:, a, :], ALU.mult))
                link(dve.tensor_reduce(r1[:, a, :], weight[:, a, :], AX.X, ALU.add))
                link(dve.reciprocal(r1[:, a, :], r1[:, a, :]))
                link(dve.tensor_tensor(weight[:, a, :], weight[:, a, :], r1[:, a, :].to_broadcast([P, nt, E]), ALU.mult))
                dve.wait_ge(pos_pe, layer + 1)
                if nt == 3:
                    dve.scalar_tensor_tensor(slot_of[0:N_META, 2, :], bank[0:N_META, 5, 2 * E:3 * E], 1.0,
                                             picked_bf[0:N_META, 2, :], ALU.add, ALU.mult).then_inc(slot_ok, 1)
                dve.scalar_tensor_tensor(slot_of[:, 0:2, :], bank[:, 5, 0:2 * E].rearrange("p (t e) -> p t e", t=2), 1.0,
                                         picked_bf[:, 0:2, :], ALU.add, ALU.mult).then_inc(slot_ok, 1)
                dve.wait_ge(slot_ok, (2, 3)[layer])

            def overflow(layer, nt):
                a = slice(0, nt)
                link(dve.tensor_reduce(over[:, 0:1], bank[:, 7, 3 * E:4 * E], AX.X, ALU.max))
                link(dve.tensor_scalar(over[:, 1:2], over[:, 0:1], float(CAP), None, ALU.is_gt))
                dve.tensor_copy(over_i[:, :], over[:, 1:2]).then_inc(flag_ok, 1)
                link(dve.scalar_tensor_tensor(late_w[:, a, :], slot_of[:, a, :], float(CAP), weight[:, a, :], ALU.is_gt, ALU.mult))

            def experts(layer, tiles):
                L = layer
                nt = len(tiles)
                ns = len(scatter_order(L, False))

                def build(g):
                    for tt in tiles:
                        r = ROWS[tt]
                        at = slot_of[0:r, tt, bass.ds(g * GRP, GRP)] if not isinstance(g, int) else slot_of[0:r, tt, g * GRP:(g + 1) * GRP]
                        dve.tensor_tensor(onehot[0:r, tt, :].rearrange("p (e s) -> p e s", e=GRP),
                                          iota_slot[0:r, :].unsqueeze(1).to_broadcast([r, GRP, SLOTS]),
                                          at.unsqueeze(2).to_broadcast([r, GRP, SLOTS]), ALU.is_equal).then_inc(s_ready[L], 1)

                def group(g, last):
                    dve.wait_ge(s_ready[L], g * nt + nt)
                    for tt in tiles:
                        r = ROWS[tt]
                        wt = weight[0:r, tt, bass.ds(g * GRP, GRP)] if not isinstance(g, int) else weight[0:r, tt, g * GRP:(g + 1) * GRP]
                        dve.tensor_tensor(whot[0:r, tt, :].rearrange("p (e s) -> p e s", e=GRP),
                                          onehot[0:r, tt, :].rearrange("p (e s) -> p e s", e=GRP),
                                          wt.unsqueeze(2).to_broadcast([r, GRP, SLOTS]), ALU.mult).then_inc(sw_ready[L], 1)
                    if not last:
                        dve.wait_ge(sw_ready[L], g * nt + nt)
                        dve.wait_ge(gth_pe[L], g * 4 + 4)
                        build(g + 1)
                    for p in range(2):
                        dve.wait_ge(silu_ok[L], g * 2 + p + 1)
                        dve.wait_ge(up_pe[L], g * 2 + p + 1)
                        dve.tensor_tensor(act_sb[:, p, :], act_sb[:, p, :], bank[:, 2 * p + 1, :], ALU.mult).then_inc(act_ok[L], 1)
                    for p in range(2):
                        dve.wait_ge(w_pe[L], g * 2 + p + 1)
                        c = 0 if nt == 3 else N_META
                        dve.tensor_copy(whotT[:, p, c:T], bank[:, 2 * p + 1, c:T]).then_inc(w_ev[L], 1)
                    for p in range(2):
                        for i, (tt, n) in enumerate(scatter_order(L, last and p == 1)):
                            s = ns * p + i
                            dve.wait_ge(sc_pe[L], g * (2 * ns) + s + 1)
                            if tt == 2:
                                dve.tensor_tensor(ymeta, ymeta, bank[:, 4 + s % 2, 0:SEQ], ALU.add).then_inc(sc_ev[L], 1)
                            else:
                                y = yacc[:, tt, 512 * n:512 * (n + 1)]
                                dve.tensor_tensor(y, y, bank[:, 4 + s % 2, :], ALU.add).then_inc(sc_ev[L], 1)

                build(0)
                overflow(L, nt)
                dve.wait_ge(yinit, (6, 8)[layer])
                late(dve, L)
                with dve.Fori(0, NG - 1) as g:
                    group(g, False)
                group(NG - 1, True)

            dve.memset(eps_ln, 1e-5)
            dve.memset(eps_rms, 1e-6)
            dve.memset(one, 1.0)
            dve.memset(lg[:, :, :], 0.0)
            dve.memset(slot_of[:, :, :], 0.0)
            link(dve.memset(ss0, 1.0))

            def level_masks():
                ge, xf = rt[:, 0, 0:P], rt[:, 0, P:2 * P]
                link(dve.tensor_tensor(ge, iota_i[:, 0:P], row_i[:, :], ALU.is_ge))
                link(dve.tensor_tensor(row_i[:, :], row_i[:, :], iota_i[:, 0:P], ALU.bitwise_xor))
                link(dve.tensor_scalar(xf, row_i[:, :], -4096.0, None, ALU.add))
                link(dve.tensor_tensor(xf, xf, ge, ALU.mult))
                link(dve.tensor_scalar(row_i[:, :], xf, 4096.0, None, ALU.add))
                for lv, w in enumerate(LEVELS):
                    link(dve.tensor_scalar(level_mask[:, lv, :], row_i[:, :], w.bit_length() - 1, None, ALU.logical_shift_right))
                    link(dve.tensor_scalar(level_mask[:, lv, :], level_mask[:, lv, :], 1.0, None, ALU.is_equal))
                link(dve.tensor_scalar(level_mask[:, len(LEVELS), :], row_i[:, :], 0.0, None, ALU.is_equal))

            for n in range(0, 8, 2):
                kind, m, _ = J0[n]
                if n == 4:
                    dve.wait_ge(const_ok, 6 + 3 + 4 + 2)
                    level_masks()
                dve.wait_ge(pj0_pe, n + 1)
                dve.tensor_copy((zq, zk)[kind == "K"][:, m, :], bank[:, n, 0:T]).then_inc(pj0_dve, 1)
            for g in range(4):
                dve.reciprocal(pcount[:, g, :], pcount[:, g, :]).then_inc(lam_s, 1)
            dve.wait_ge(par_in, 9 * 16)
            for k in range(2):
                link(dve.tensor_tensor(lam_t[:, k, :], lam_v[:, 2 * k, :], lam_v[:, 2 * k + 1, :], ALU.mult))
                dve.tensor_reduce((lam1, lam2)[k], lam_t[:, k, :], AX.X, ALU.add).then_inc(lam_e, 1)
            link(dve.tensor_scalar(sub_b[:, :], sub_b[:, :], 1.0 - LAMBDA_INIT, None, ALU.mult))

            def biased(i):
                tt, hp = STEPS[i]
                r, nk = ROWS[tt], C0[tt] + ROWS[tt]
                dve.wait_ge(at_s, i + 1)
                for j in range(2):
                    dve.scalar_tensor_tensor(s_sb[0:r, i % 2, 2 * j:2 * j + 2, 0:nk],
                                             dist[0:r, tt, 0:nk].unsqueeze(1).to_broadcast([r, 2, nk]),
                                             SLOPES[2 * hp + j] / ATT_SCALE,
                                             bank[0:r, 2 * j:2 * j + 2, 0:nk], ALU.mult, ALU.add).then_inc(at_b, 1)
                dve.wait_ge(at_b, 2 * i + 2)
                link(dve.tensor_reduce(mx[0:r, i, :], s_sb[0:r, i % 2, :, 0:nk], AX.X, ALU.max))
                dve.tensor_scalar(mx[0:r, i, :], mx[0:r, i, :], -ATT_SCALE, None, ALU.mult).then_inc(at_m, 1)

            def difference(i):
                tt, hp = STEPS[i]
                r, nk = ROWS[tt], C0[tt] + ROWS[tt]
                dve.wait_ge(at_e, 4 * i + 4)
                link(dve.reciprocal(rs[0:r, i, :], sums[0:r, i, :]))
                odd = rs[0:r, i, :].rearrange("p (j m) -> p j m", m=2)[:, :, 1]
                link(dve.tensor_scalar(odd, odd, nlam[0:r, :], None, ALU.mult))
                for j in range(2):
                    p1 = s_sb[0:r, i % 2, 2 * j + 1, 0:nk]
                    link(dve.tensor_scalar(p1, p1, rs[0:r, i, 2 * j + 1:2 * j + 2], None, ALU.mult))
                if i >= 1:
                    dve.wait_ge(at_t, i)
                for j in range(2):
                    dve.scalar_tensor_tensor(pd[0:r, j, 0:nk], s_sb[0:r, i % 2, 2 * j, 0:nk], rs[0:r, i, 2 * j:2 * j + 1],
                                             s_sb[0:r, i % 2, 2 * j + 1, 0:nk], ALU.mult, ALU.add).then_inc(at_pd, 1)

            def heads_out(i):
                tt, hp = STEPS[i]
                r = ROWS[tt]
                dve.wait_ge(at_o, i + 1)
                dve.tensor_copy(o_tok[0:r, tt, 2 * P * hp:2 * P * (hp + 1)], bank[0:r, 6, 0:2 * P]).then_inc(at_oe, 1)
                dve.wait_ge(at_oe, i + 1)
                for j in range(2):
                    h = 2 * hp + j
                    o = o_tok[0:r, tt, P * h:P * (h + 1)]
                    c = HEADS * tt + h
                    dve.tensor_tensor_reduce(out=sq0[0:r, :], in0=o, in1=o, scale=1.0, scalar=0.0, op0=ALU.mult,
                                             op1=ALU.add, accum_out=ss0[0:r, c:c + 1]).then_inc(o_ss, 1)
                    dve.wait_ge(o_ss, 2 * i + j + 1)

            biased(0)
            dve.wait_ge(act_c, 2)
            link(dve.tensor_tensor(nlam, lam2, lam1, ALU.subtract))
            link(dve.tensor_scalar(nlam, nlam, -LAMBDA_INIT, None, ALU.add))
            difference(0)
            biased(1)
            for i in range(2, 6):
                biased(i)
                difference(i - 1)
                heads_out(i - 2)
            difference(5)
            heads_out(4)
            heads_out(5)
            dve.wait_ge(o_rs, 1)
            link(dve.reciprocal(rstd0, rstd0))
            for tt in (2, 0, 1):
                r = ROWS[tt]
                o = o_tok[0:r, tt, :].rearrange("p (h v) -> p h v", h=HEADS)
                link(dve.tensor_tensor(o, o, rstd0[0:r, HEADS * tt:HEADS * (tt + 1)].unsqueeze(2).to_broadcast([r, HEADS, P]), ALU.mult))
                dve.tensor_tensor(o, o, sub_b[0:r, :].unsqueeze(1).to_broadcast([r, HEADS, P]), ALU.mult).then_inc(o_n, 1)
            dve.wait_ge(yt_pe, 3)
            dve.tensor_copy(yT[:, 4:8, C0[1]:T], bank[:, 7, :].rearrange("p (h t) -> p h t", h=HEADS)).then_inc(yt_dve, 1)
            for i, tt in enumerate((2, 0, 1)):
                mix_tile((0, 1, 3)[i], tt)
                norm_tile(0, i, tt)
            dve.memset(ymeta, 0.0).then_inc(ym_zero, 1)
            link(dve.memset(yacc[0:N_META, 2, :], 0.0))
            router(0, (2, 0, 1))
            experts(0, (2, 0, 1))
            norm_tile(1, 0, 0)
            dve.wait_ge(ym_out, 4)
            link(dve.tensor_tensor(yacc[0:N_META, 2, :], yacc[0:N_META, 2, :], meta_row[0:N_META, :], ALU.add))
            norm_stats(1, 1, 2)
            norm_scale(1, 1, 2)
            norm_stats(1, 2, 1)
            norm_gain(1, 1, 2)
            norm_scale(1, 2, 1)
            norm_gain(1, 2, 1)

            dve.wait_ge(par1_in, 64)

            def job1(n):
                kind, m, by, b = J1[n]
                if by == "a":
                    return
                dve.wait_ge(pj1_pe, n + 1)
                if kind == "G":
                    dve.tensor_copy(glr[0:GLA_RANK, :], bank[0:GLA_RANK, b, 0:T]).then_inc(pj1_dve, 1)
                if kind == "A":
                    dve.tensor_scalar(bT[:, m, :], bank[:, b, 0:T], gb_sb[:, m:m + 1], None, ALU.add).then_inc(gla_ga, 1)
                    dve.wait_ge(gla_ga, m + 1)
                    dve.scalar_tensor_tensor(la[:, m, :], bT[:, m, :], -1.0, bT[:, m, :], ALU.mult, ALU.max).then_inc(gla_ab, 1)
                if kind == "Q":
                    dve.tensor_scalar(qT[:, m, :], bank[:, b, 0:SEQ], GLA_SCALE, None, ALU.mult).then_inc(pj1_dve, 1)
                if kind == "K":
                    dve.tensor_copy(kT[:, m, :], bank[:, b, 0:T]).then_inc(pj1_dve, 1)
                if kind in "VR":
                    half, tt = m
                    dve.tensor_copy((vt if kind == "V" else rt)[:, tt, 512 * half:512 * (half + 1)], bank[:, b, :]).then_inc(pj1_dve, 1)

            nl = len(LEVELS)
            for n in range(3, NLV):
                job1(n)
                if n == 11:
                    dve.wait_ge(gla_ln, 4)
                    link(dve.tensor_scalar(bT, bT, 0.0, None, ALU.min))
                    link(dve.tensor_tensor(la, bT, la, ALU.subtract))
                    link(dve.tensor_scalar(la, la, 1.0 / GLA_TAU, None, ALU.mult))
                    link(dve.memset(ql, 1.0))
                    for h in range(HEADS):
                        dve.tensor_tensor_scan(bT[:, h, :], ql.rearrange("p a b -> p (a b)")[:, 0:T], la[:, h, :], 0.0,
                                               ALU.mult, ALU.add).then_inc(gla_b, 1)
                    dve.wait_ge(gla_b, 4)
                    exponents(dve, 0, link)
                    link(dve.memset(att, 0.0))
                    dve.memset(kl, 0.0).then_inc(lv_k, 1)
            for st in range(nl + 3):
                if st < nl:
                    w = LEVELS[st]
                    dve.wait_ge(lv_e, st + 1)
                    if st:
                        dve.wait_ge(lv_pe, 2 * st)
                    dve.tensor_tensor(halves(ql, w)[:, :, :, w:2 * w], halves(qT, w)[:, :, :, w:2 * w],
                                      halves(dec, w)[:, :, :, w:2 * w], ALU.mult).then_inc(lv_q, 1)
                    dve.wait_ge(lv_q, st + 1)
                    dve.wait_ge(lv_k, st + 2)
                    exponents(dve, st + 1, link)
                if st == nl + 1:
                    dve.wait_ge(lv_e, nl + 1)
                    dve.wait_ge(lv_pe, 2 * nl)
                    link(dve.tensor_tensor(kl[:, :, 0:P], kT[:, :, N_META:N_META + P], dec[:, :, 0:P], ALU.mult))
                    dve.tensor_tensor(ql[:, :, P:SEQ], qT[:, :, P:SEQ], dec[:, :, P:SEQ], ALU.mult).then_inc(lv_q, 1)
                    dve.wait_ge(lv_q, nl + 1)
                    exponents(dve, nl + 1, link)
                if NLV + st < len(J1):
                    job1(NLV + st)
                if st <= nl:
                    attend(dve, st)
                if st == nl + 2:
                    dve.wait_ge(lv_e, nl + 3)
                    dve.wait_ge(lv_pe, 2 * (nl + 1) + 1)
                    link(dve.tensor_tensor(kl[:, :, 0:N_META], kT[:, :, 0:N_META], la[:, :, 0:N_META], ALU.mult))
                    dve.tensor_tensor(ql, qT, dec, ALU.mult).then_inc(lv_q, 1)
            for tt in range(2):
                for c in range(2):
                    dve.wait_ge(go_pe, 2 * tt + c + 1)
                    o = og[:, tt, 512 * c:512 * (c + 1)]
                    dve.tensor_copy(o, bank[:, 2 * tt + c, :]).then_inc(go_ev, 1)
                    dve.wait_ge(go_ev, 2 * tt + c + 1)
                    for h in (2 * c, 2 * c + 1):
                        oh = og[:, tt, GLA_DV * h:GLA_DV * (h + 1)]
                        j = HEADS * tt + h
                        dve.tensor_tensor_reduce(out=ogT[:, 0, :], in0=oh, in1=oh, scale=1.0, scalar=0.0,
                                                 op0=ALU.mult, op1=ALU.add, accum_out=ss1[:, j:j + 1]).then_inc(o_ss, 1)
                        dve.wait_ge(o_ss, 12 + j + 1)
            dve.wait_ge(o_rs, 2)
            link(dve.reciprocal(rstd1, rstd1))
            for tt in range(2):
                dve.wait_ge(rg_ok, tt + 1)
                for h in range(HEADS):
                    c = slice(GLA_DV * h, GLA_DV * (h + 1))
                    j = HEADS * tt + h
                    dve.scalar_tensor_tensor(og[:, tt, c], og[:, tt, c], rstd1[:, j:j + 1], rt[:, tt, c],
                                             ALU.mult, ALU.mult).then_inc(ogt_ok, 1)
            for c in range(0, KC, 2):
                dve.wait_ge(ogt_pe, c + 1)
                dve.tensor_copy(ogT[:, c, :], bank[:, c, 0:SEQ]).then_inc(ogt_ev, 1)
            for i in range(2):
                mix_tile(5 + 2 * i, i)
                norm_tile(2, i, i)
            router(1, (0, 1))
            experts(1, (0, 1))
            norm_stats(3, 0, 0)
            norm_scale(3, 0, 0)
            norm_stats(3, 1, 1)
            norm_gain(3, 0, 0)
            norm_scale(3, 1, 1)
            norm_gain(3, 1, 1)


_INS = ['x', 'meta', 'even_w_in', 'pool_w', 'pool_scale', 'diff_lq1', 'diff_lk1', 'diff_lq2', 'diff_lk2',
        'diff_subln', 'even_w_out', 'odd_w_in', 'gla_gate_w2', 'gla_gate_b', 'gla_head_norm', 'odd_w_out',
        'ln_mix_g', 'ln_mix_b', 'ln_ffn_g', 'ln_ffn_b', 'router_w', 'router_bias',
        'moe_w_gate', 'moe_w_up', 'moe_w_down']


def kernel(**inputs):
    import numpy as _np
    import concourse.bacc as _bacc
    from concourse import mybir as _mybir
    from concourse.bass_utils import run_bass_kernel_spmd as _run

    nc = _bacc.Bacc("TRN2", target_bir_lowering=False, num_devices=1)
    arrays, args = {}, []
    for name in _INS:
        a = _np.ascontiguousarray(inputs[name])
        arrays[f"in_{name}_dram"] = a
        args.append(nc.dram_tensor(f"in_{name}_dram", a.shape, _mybir.dt.from_np(a.dtype), kind="ExternalInput").ap())
    out = nc.dram_tensor("out_0_dram", (1, SEQ, D), _mybir.dt.float32, kind="ExternalOutput").ap()
    hybrid_trunk(nc, *args, out)
    r = _run(nc, [arrays], core_ids=[0])
    return r.results[0]["out_0_dram"]
```

```python
import math
from contextlib import ExitStack

import concourse.bass as bass
from concourse import mybir

F32 = mybir.dt.float32
BF16 = mybir.dt.bfloat16
I32 = mybir.dt.int32
ALU = mybir.AluOpType
ACT = mybir.ActivationFunctionType
AX = mybir.AxisListType

P = 128
D = 1024
KC = D // P
SEQ = 256
N_META = 16
T = N_META + SEQ
C0 = (N_META, N_META + P, 0)
ROWS = (P, P, N_META)
HEADS = 4
WINDOWS = (2, 4, 8, 16)
QK_DIM = 64
ATT_SCALE = QK_DIM ** -0.5
SLOPES = [2.0 ** (-8.0 * (h + 1) / HEADS) for h in range(HEADS)]
LAMBDA_INIT = 0.8 - 0.6 * math.exp(0.0)
NEG = -1e30
GLA_DV = D // HEADS
GLA_SCALE = float(P) ** -0.5
GLA_TAU = 16.0
GLA_RANK = 16
LEVELS = (64, 32, 16, 8, 4, 2, 1)
DEPTH = 2
ALPHA = (2.0 * DEPTH) ** 0.25
E = 16
GRP = 4
NG = E // GRP
SLOTS = 64
CAP = SLOTS
NR = 6
UNIT = 4096
PAIR_UNITS = 6
GROUP_UNITS = 2 * PAIR_UNITS
BASE_MOE = (6, 6 + NG * GROUP_UNITS + 8)
BASE_ODD = BASE_MOE[0] + NG * GROUP_UNITS


def hybrid_trunk(nc, x, meta, even_w_in, pool_w, pool_scale, diff_lq1, diff_lk1, diff_lq2, diff_lk2,
                 diff_subln, even_w_out, odd_w_in, gla_gate_w2, gla_gate_b, gla_head_norm, odd_w_out,
                 ln_mix_g, ln_mix_b, ln_ffn_g, ln_ffn_b, router_w, router_bias,
                 moe_w_gate, moe_w_up, moe_w_down, out):
    with ExitStack() as ctx:
        def sb(name, shape, dt=F32):
            return ctx.enter_context(nc.sbuf_tensor(name, shape, dt))

        def sem(name):
            return ctx.enter_context(nc.semaphore(name))

        def per_layer(name):
            return [sem(f"{name}{layer}") for layer in range(DEPTH)]

        bank = ctx.enter_context(nc.psum_tensor("bank", [P, 8, 512], F32))

        ring = sb("ring", [P, NR, UNIT])
        htok = sb("htok", [P, 3, D])
        hT = sb("hT", [P, KC, T])
        gain = sb("gain", [P, 2, D])
        ident = sb("ident", [P, P])
        ones_bf = sb("ones_bf", [P, P], BF16)
        before_bf = sb("before_bf", [P, P], BF16)
        dist = sb("dist", [P, 3, T])
        iota_slot = sb("iota_slot", [P, SLOTS])
        iota_g = sb("iota_g", [P, NG])
        earlier = sb("earlier", [P, GRP, GRP])
        iota_i = sb("iota_i", [P, T], I32)
        row_i = sb("row_i", [P, P], I32)
        level_mask = sb("level_mask", [P, len(LEVELS) + 1, P], I32)
        small = sb("small", [P, 32])
        rw = sb("rw", [P, KC, E])
        rbias = sb("rbias", [P, E])
        sub_b = sb("sub_b", [P, P])
        stats = sb("stats", [P, 3, 2, 6])
        mv = sb("mv", [P, 3, 2])
        rstd = sb("rstd", [P, 3, 1])
        lgT = sb("lgT", [E, T])
        lg = sb("lg", [P, 3, E])
        pr = sb("pr", [P, 3, E])
        sel = sb("sel", [P, 3, E])
        above = sb("above", [P, 3 * NG, GRP, GRP])
        equal = sb("equal", [P, 3 * NG, GRP, GRP])
        rank = sb("rank", [P, 3 * NG, GRP])
        gs = sb("gs", [P, 3, NG])
        ghot = sb("ghot", [P, 3, NG])
        r1 = sb("r1", [P, 3, 1])
        r2 = sb("r2", [P, 3, 1])
        t1 = sb("t1", [P, 3, E])
        picked = sb("picked", [P, 3, E])
        picked_bf = sb("picked_bf", [P, 3, E], BF16)
        weight = sb("weight", [P, 3, E])
        late_w = sb("late_w", [P, 3, E])
        slot_of = sb("slot_of", [P, 3, E])
        over = sb("over", [P, 2])
        over_i = sb("over_i", [P, 1], I32)

        SCR = 16000
        scratch = sb("scratch", [P, SCR])

        class Cut:
            def __init__(self):
                self.at = 0

            def __call__(self, *shape):
                n = 1
                for s in shape:
                    n *= s
                v = scratch[:, self.at:self.at + n]
                self.at += n
                assert self.at <= SCR, self.at
                if len(shape) == 2:
                    v = v.rearrange("p (a b) -> p a b", b=shape[1])
                if len(shape) == 3:
                    v = v.rearrange("p (a b c) -> p a b c", b=shape[1], c=shape[2])
                return v

        cut = Cut()
        PADW = N_META + T
        zpool = cut(4, PADW)
        poolA = cut(4, PADW)
        poolB = cut(4, PADW)
        pcount = cut(4, N_META)
        zq = cut(4, T)
        zk = cut(4, T)
        v0 = cut(3, 512)
        yT = cut(8, T)
        s_sb = cut(8, T).rearrange("p (b m) k -> p b m k", b=2)
        pd = cut(2, T)
        pT = cut(2, 3, P)
        o_tok = cut(3, 512)
        pw_sb = cut(4, P)
        sq0 = cut(P)
        lam_v = cut(4, QK_DIM)
        lam_t = cut(2, QK_DIM)
        ss0 = cut(12)
        mx = cut(6, 4)
        sums = cut(6, 4)
        rs = cut(6, 4)
        rstd0 = cut(12)
        cut = Cut()
        qT = cut(4, SEQ)
        kT = cut(4, T)
        bT = cut(4, T)
        la = cut(4, T)
        vt = cut(3, D)
        rt = cut(2, D)
        dec = cut(4, SEQ)
        ql = cut(4, SEQ)
        kl = cut(4, SEQ)
        att = cut(8, P)
        att01 = cut(4, P)
        ss1 = cut(8)
        rstd1 = cut(8)
        glr = cut(T)
        hn_b = cut(GLA_DV)
        g2w = cut(512)
        gb_sb = cut(4)
        glw = cut(KC, GLA_RANK)
        at = Cut()
        og = at(2, D)
        at.at = 1024 + 1088
        attM = at(4, SEQ)
        at.at = 1024 + 3 * 1088
        ogT = at(8, SEQ)
        cut = Cut()
        yacc = cut(3, D)
        xg = cut(KC, GRP * SLOTS)
        onehot = cut(3, GRP * SLOTS)
        whot = cut(3, GRP * SLOTS)
        act_sb = cut(2, 512)
        actT = cut(4, P)
        o_sb = cut(D)
        whotT = cut(2, T)
        ymeta = cut(SEQ)
        extra = scratch[:, cut.at:cut.at + UNIT]
        late_act = cut(T)
        meta_row = scratch[:, cut.at:cut.at + D]
        late_g = cut(KC, P)
        late_u = cut(KC, P)
        late_d = cut(D)

        eps_ln, eps_rms, lam1, lam2, nlam, one = (small[:, i:i + 1] for i in range(6))

        ring_in = [sem(f"ring_in{i}") for i in range(NR)]
        x_in, meta_in, par_in, par1_in, gain_in = (sem(n) for n in ("x_in", "meta_in", "par_in", "par1_in", "gain_in"))
        dve_c, act_c, pool_c = sem("dve_c"), sem("act_c"), sem("pool_c")
        const_ok, lvl_ok = sem("const_ok"), sem("lvl_ok")
        hT_pe, hT_act = sem("hT_pe"), sem("hT_act")
        h_left, h_right = sem("h_left"), sem("h_right")
        pj0_pe, pj0_dve, pj0_act = sem("pj0_pe"), sem("pj0_dve"), sem("pj0_act")
        pj1_pe, pj1_dve, pj1_act = sem("pj1_pe"), sem("pj1_dve"), sem("pj1_act")
        out0, out1 = (pj0_dve, pj0_act), (pj1_dve, pj1_act)
        pooled, poolmm, poolev = sem("pooled"), sem("poolmm"), sem("poolev")
        lam_e, lam_s = sem("lam_e"), sem("lam_s")
        at_s, at_b, at_m, at_e, at_pd = sem("at_s"), sem("at_b"), sem("at_m"), sem("at_e"), sem("at_pd")
        at_t, at_te, at_o, at_oe = sem("at_t"), sem("at_te"), sem("at_o"), sem("at_oe")
        o_ss, o_rs, o_n = sem("o_ss"), sem("o_rs"), sem("o_n")
        yt_pe, yt_dve, yt_act = sem("yt_pe"), sem("yt_dve"), sem("yt_act")
        mix_pe, mix_dve = sem("mix_pe"), sem("mix_dve")
        var_ok, sd_ok = sem("var_ok"), sem("sd_ok")
        ym_zero, ym_out = sem("ym_zero"), sem("ym_out")
        lgt_pe, lgt_ev, lg_pe, lg_ev = sem("lgt_pe"), sem("lgt_ev"), sem("lg_pe"), sem("lg_ev")
        lg_max, lg_exp, pick_ok, pos_pe, route_ok = (sem(n) for n in ("lg_max", "lg_exp", "pick_ok", "pos_pe", "route_ok"))
        eq_ok, slot_ok, flag_ok = sem("eq_ok"), sem("slot_ok"), sem("flag_ok")
        yinit = sem("yinit")
        s_ready, sw_ready = per_layer("s_ready"), per_layer("sw_ready")
        gth_pe, gth_ev = per_layer("gth_pe"), per_layer("gth_ev")
        gate_pe, up_pe, silu_ok, act_ok = per_layer("gate_pe"), per_layer("up_pe"), per_layer("silu_ok"), per_layer("act_ok")
        t_pe, t_ev, w_pe, w_ev = per_layer("t_pe"), per_layer("t_ev"), per_layer("w_pe"), per_layer("w_ev")
        d_pe, d_ev, sc_pe, sc_ev = per_layer("d_pe"), per_layer("d_ev"), per_layer("sc_pe"), per_layer("sc_ev")
        gla_ga, gla_ab, gla_e, gla_ln, gla_b = (sem(n) for n in ("gla_ga", "gla_ab", "gla_e", "gla_ln", "gla_b"))
        lv_d, lv_e, lv_q, lv_k, lv_pe, lv_ev, lv_act = (sem(n) for n in ("lv_d", "lv_e", "lv_q", "lv_k", "lv_pe", "lv_ev", "lv_act"))
        go_pe, go_ev, rg_s, rg_ok, ogt_ok, ogt_pe, ogt_ev = (sem(n) for n in (
            "go_pe", "go_ev", "rg_s", "rg_ok", "ogt_ok", "ogt_pe", "ogt_ev"))
        stored = sem("stored")
        st_ok = sem("st_ok")
        first_half = sem("first_half")
        extra_in, extra_again = sem("extra_in"), per_layer("extra_again")
        late_in = per_layer("late_in")
        lt_g, lt_u, lt_s, lt_m, lt_pe, lt_ev = (per_layer(n) for n in ("lt_g", "lt_u", "lt_s", "lt_m", "lt_pe", "lt_ev"))

        block = ctx.enter_context(nc.Block())

        def in_unit(w, n):
            return w[0][:, 512 * n:512 * (n + 1)].rearrange("(kc p) n -> p kc n", p=P)

        def unit(n):
            return ring[:, n % NR, :].rearrange("p (kc n) -> p kc n", kc=KC)

        def normed(eng, n):
            eng.wait_ge(h_left, n)
            eng.wait_ge(h_right, n)

        def arrived(eng, n):
            eng.wait_ge(ring_in[n % NR], 16 * (n // NR + 1))


        J0 = ([("Q", h, "da"[h % 2]) for h in range(4)] + [("K", h, "da"[h % 2]) for h in range(4)]
              + [("V", tt, "a") for tt in (2, 0, 1)] + [("U", g, "a") for g in (3, 2, 1, 0)])
        def bank0(n):
            return n if n < 8 else (4, 5)[n - 8] if n < 10 else 7

        J1 = ([("V", (n, 0), "a", 4 + n) for n in range(2)] + [("M", 0, "a", 6), ("G", 0, "d", 7)]
              + [("A", h, "g", h) for h in range(4)] + [("Q", h, "da"[h % 2], 4 + h) for h in range(4)]
              + [("K", h, "da"[h % 2], h) for h in range(4)] + [("V", (n, 1), "da"[n], 4 + n) for n in range(2)]
              + [("R", (n, tt), "da"[tt], (6, 7, 4, 5)[2 * tt + n]) for tt in range(2) for n in range(2)])
        NLV = 16

        def job_out(eng, jobs, sems, n):
            by = jobs[n][2]
            sem_of = {"d": sems[0], "a": sems[1], "g": gla_ga}[by]
            eng.wait_ge(sem_of, len([m for m in range(n + 1) if jobs[m][2] == by]))

        def meta_quarters(pe, dst, src, w):
            for kc in range(KC):
                for q in range(4):
                    wq = w(kc, q)
                    mm = pe.matmul(dst[32 * q:32 * q + N_META, 0:wq.shape[-1]], src[:, kc, 0:N_META], wq,
                                   start=(kc == 0), stop=(kc == KC - 1), skip_group_check=True)
            return mm

        def halves(v, w):
            return v.rearrange("p h (m t) -> p h m t", t=2 * w)

        def key_factors(eng, lv):
            w = LEVELS[lv]
            eng.wait_ge(lv_e, lv + 1)
            if lv == 0:
                job_out(eng, J1, out1, NLV - 2)
                job_out(eng, J1, out1, NLV - 1)
                eng.wait_ge(lv_k, 1)
            else:
                eng.wait_ge(lv_pe, 2 * lv)
            eng.tensor_tensor(halves(kl, w)[:, :, :, 0:w], halves(kT[:, :, N_META:T], w)[:, :, :, 0:w],
                              halves(dec, w)[:, :, :, 0:w], ALU.mult).then_inc(lv_k, 1)

        STEPS = [(0, 0), (0, 1), (1, 0), (1, 1), (2, 0), (2, 1)]
        KEYS = ([2, 0], [2, 0, 1], [2])

        FFN_ORDER = (0, 2, 1)
        TURN_BANK = (6, 0, 2)

        def scatter_order(layer, last):
            if last:
                return [(0, 0), (0, 1)] + [(2, 2)] * (layer == 0) + [(1, 0), (1, 1)]
            return [(0, 0), (1, 0), (0, 1), (1, 1)] + [(2, 2)] * (layer == 0)

        def late(eng, layer):
            L = layer
            tiles = ((2, 0, 1), (0, 1))[layer]
            nt = len(tiles)
            c = 0 if layer == 0 else N_META
            eng.wait_ge(flag_ok, layer + 1)
            flag = eng.value_load(over_i[0:1, 0:1], min_val=0, max_val=1)
            with eng.If(flag > 0):
                if eng is nc.scalar:
                    eng.wait_ge(extra_in, 16 * (L + 1))
                if eng is nc.vector:
                    dve_prime = nc.vector.memset(small[:, 31:32], 0.0)
                    dve_prime.then_inc(lt_ev[L], 1)
                with eng.Fori(0, E) as e:
                    for fc in range(4):
                        (late_pe if eng is nc.tensor else late_act_part if eng is nc.scalar else late_dve)(eng, L, tiles, nt, c, e, fc)
                eng.wait_ge(lt_ev[L], 1 + 8 * nt * E)
                if eng is nc.scalar:
                    eng.dma_start(extra.rearrange("p (kc n) -> p kc n", kc=KC), extra_src(layer)).then_inc(extra_again[L], 16)
                if eng is nc.vector:
                    eng.wait_ge(extra_again[L], 16)

        def late_pe(pe, L, tiles, nt, c, e, fc):
            pe.wait_ge(gth_ev[L], 2)
            pe.wait_ge(late_in[L], e * 192 + 48 * (fc + 1))
            pe.wait_ge(lt_ev[L], e * (8 * nt) + (2 * nt * fc + 1))
            for b, (w, done) in enumerate(((late_g, lt_g), (late_u, lt_u))):
                for kc in range(KC):
                    mm = pe.matmul(bank[:, b, c:T], w[:, kc, :], hT[:, kc, c:T], start=(kc == 0), stop=(kc == KC - 1))
                mm.then_inc(done[L], 1)
            pe.wait_ge(lt_m[L], e * 4 + fc + 1)
            for i, tt in enumerate(tiles):
                for n in range(2):
                    pe.matmul(bank[0:ROWS[tt], 2 + 2 * i + n, :], late_act[:, C0[tt]:C0[tt] + ROWS[tt]],
                              late_d[:, 512 * n:512 * (n + 1)], start=True, stop=True).then_inc(lt_pe[L], 1)

        def late_act_part(act, L, tiles, nt, c, e, fc):
            act.wait_ge(lt_ev[L], e * (8 * nt) + (2 * nt * fc + 1))
            cols = slice(P * fc, P * (fc + 1))
            for dst, w in ((late_g, moe_w_gate), (late_u, moe_w_up)):
                act.dma_start(dst, w[L][bass.ds(e, 1)].rearrange("e (kc p) n -> p (e kc) n", p=P)[:, :, cols]).then_inc(late_in[L], 16)
            act.dma_start(late_d, moe_w_down[L][bass.ds(e, 1)].rearrange("e (fc p) n -> p (e fc) n", p=P)[:, fc, :]).then_inc(late_in[L], 16)
            act.wait_ge(lt_g[L], e * 4 + fc + 1)
            act.activation(late_act[:, c:T], bank[:, 0, c:T], ACT.Silu).then_inc(lt_s[L], 1)

        def late_dve(dve, L, tiles, nt, c, e, fc):
            dve.wait_ge(lt_s[L], e * 4 + fc + 1)
            dve.wait_ge(lt_u[L], e * 4 + fc + 1)
            dve.tensor_tensor(late_act[:, c:T], late_act[:, c:T], bank[:, 1, c:T], ALU.mult).then_inc(lt_m[L], 1)
            for i, tt in enumerate(tiles):
                for n in range(2):
                    r = ROWS[tt]
                    dve.wait_ge(lt_pe[L], e * (8 * nt) + (2 * nt * fc + 2 * i + n + 1))
                    y = yacc[0:r, tt, 512 * n:512 * (n + 1)]
                    dve.scalar_tensor_tensor(y, bank[0:r, 2 + 2 * i + n, :], late_w[0:r, tt, bass.ds(e, 1)], y,
                                             ALU.mult, ALU.add).then_inc(lt_ev[L], 1)

        def exponents(dve, lv, link):
            if lv <= len(LEVELS):
                w = (LEVELS + (P,))[lv] if lv else LEVELS[0]
                if lv == len(LEVELS):
                    w = P
                b = halves(bT[:, :, N_META:T], w)
                m = SEQ // (2 * w)
                end = b[:, :, :, w - 1:w].to_broadcast([P, HEADS, m, w])
                link(dve.tensor_tensor(halves(dec, w)[:, :, :, 0:w], end, b[:, :, :, 0:w], ALU.subtract))
                dve.tensor_tensor(halves(dec, w)[:, :, :, w:2 * w], b[:, :, :, w:2 * w], end, ALU.subtract).then_inc(lv_d, 1)
            else:
                end = bT[:, :, N_META - 1:N_META]
                dve.tensor_tensor(la[:, :, 0:N_META], end.to_broadcast([P, HEADS, N_META]), bT[:, :, 0:N_META],
                                  ALU.subtract).then_inc(gla_b, 1)
                dve.tensor_tensor(dec, bT[:, :, N_META:T], end.to_broadcast([P, HEADS, SEQ]), ALU.subtract).then_inc(lv_d, 1)

        def attend(dve, lv):
            for tt in range(2):
                dve.wait_ge(lv_pe, 2 * lv + tt + 1)
                if lv:
                    dve.wait_ge(lv_ev, 2 * lv + tt - 1)
                dve.copy_predicated(att[:, HEADS * tt:HEADS * (tt + 1), :],
                                    level_mask[:, lv, :].unsqueeze(1).to_broadcast([P, HEADS, P]),
                                    bank[:, 2 * (lv % 2) + tt, :].rearrange("p (h t) -> p h t", h=HEADS)).then_inc(lv_ev, 1)

        def extra_src(layer):
            return moe_w_gate[layer][2].rearrange("(kc p) n -> p kc n", p=P)

        @block.sync
        def _(sp):
            def used(n):
                if n < 6:
                    return [(pj0_pe, 4), (pj0_pe, 8), (pj0_pe, 11), (pj0_pe, 15), (mix_pe, 5), (mix_pe, 5)][n]
                m = n - BASE_ODD
                if m < 0:
                    return used_expert(0, NG - 1, m + GROUP_UNITS)
                return [(pj1_pe, 12), (pj1_pe, 16), (pj1_pe, 17), (pj1_pe, 18), (pj1_pe, 21), (pj1_pe, 22),
                        (mix_pe, 9), (mix_pe, 9)][m]

            def used_expert(layer, g, i):
                p, j = i // PAIR_UNITS, i % PAIR_UNITS
                if j < 4:
                    return (gate_pe, up_pe)[j // 2][layer], g * 2 + p + 1
                return d_pe[layer], g * 4 + 2 * p + j - 3

            def load(n, src):
                if n >= NR:
                    sp.wait_ge(*used(n - NR))
                sp.dma_start(unit(n), src).then_inc(ring_in[n % NR], 16)

            def experts(layer):
                base = BASE_MOE[layer]

                def group(g):
                    order = [(k, m) for p in range(2) for k in "gud" for m in (2 * p, 2 * p + 1)]
                    for i, (kind, m) in enumerate(order):
                        dst = ring[:, (base + i) % NR, :]
                        if kind == "d":
                            pair, n = m // 2, m % 2
                            src = moe_w_down[layer][bass.ds(g * GRP + 2 * pair, 2)][:, :, 512 * n:512 * (n + 1)]
                            src = src.rearrange("e (fc p) n -> p (e fc) n", p=P)
                        else:
                            src = {"g": moe_w_gate, "u": moe_w_up}[kind][layer][bass.ds(g * GRP + m, 1)]
                            src = src.rearrange("e (kc p) n -> p (e kc) n", p=P)
                        dst = dst.rearrange("p (kc n) -> p kc n", kc=KC)
                        if isinstance(g, int) and i == NR:
                            continue
                        if isinstance(g, int) and i == 4:
                            sp.wait_ge(*((yt_pe, 3), (ogt_ok, 2 * HEADS))[layer])
                            sp.dma_start(extra.rearrange("p (kc n) -> p kc n", kc=KC), extra_src(layer)).then_inc(extra_in, 16)
                        if i >= NR:
                            sp.wait_ge(*used_expert(layer, g, i - NR))
                        elif isinstance(g, int):
                            sp.wait_ge(*used(base + i - NR))
                        else:
                            sp.wait_ge(*used_expert(layer, g - 1, i - NR + GROUP_UNITS))
                        sp.dma_start(dst, src).then_inc(ring_in[(base + i) % NR], 16)

                group(0)
                with sp.Fori(1, NG) as g:
                    group(g)

            sp.dma_start(htok[0:N_META, 2, :], meta[:, :]).then_inc(meta_in, 16)
            for tt in range(2):
                sp.dma_start(htok[:, tt, :], x[0, P * tt:P * (tt + 1), :]).then_inc(x_in, 16)
            sp.dma_start(unit(0)[:, :, 0:256], in_unit(even_w_in, 1)[:, :, 0:256]).then_inc(first_half, 16)
            sp.dma_start(unit(0)[:, :, 256:512], in_unit(even_w_in, 1)[:, :, 256:512]).then_inc(ring_in[0], 16)
            for n, block_of_w in ((1, 2), (2, 3), (3, 0)):
                load(n, in_unit(even_w_in, block_of_w))
            for n in range(2):
                load(4 + n, in_unit(even_w_out, n))
            experts(0)
            for n in range(6):
                load(BASE_ODD + n, in_unit(odd_w_in, n))
            for n in range(2):
                load(BASE_ODD + 6 + n, in_unit(odd_w_out, n))
            experts(1)
            for tt in range(2):
                for half, done in enumerate((h_left, h_right)):
                    c = slice(512 * half, 512 * (half + 1))
                    sp.wait_ge(done, 3 + 3 + 2 + tt + 1)
                    sp.dma_start(out[0, P * tt:P * (tt + 1), c], htok[:, tt, c]).then_inc(stored, 16)
            sp.wait_ge(stored, 64)

        @block.gpsimd
        def _(pool):
            count = [0]

            def link(ins):
                count[0] += 1
                ins.then_inc(pool_c, 1)
                pool.wait_ge(pool_c, count[0])

            def load_gain(k):
                g, b = ((ln_mix_g, ln_mix_b), (ln_ffn_g, ln_ffn_b))[k % 2]
                if k:
                    normed(pool, (0, 3, 6, 8)[k])
                pool.dma_start(gain[:, 0, :], g[k // 2].partition_broadcast(P)).then_inc(gain_in, 16)
                pool.dma_start(gain[:, 1, :], b[k // 2].partition_broadcast(P)).then_inc(gain_in, 16)

            link(pool.memset(ident[:, :], 0.0))
            pool.affine_select(out=ident[:, :], in_=ident[:, :], compare_op=ALU.not_equal, fill=1.0, base=0,
                               pattern=[[-1, P]], channel_multiplier=1).then_inc(const_ok, 1)
            pool.memset(ones_bf[:, :], 1.0).then_inc(const_ok, 1)
            link(pool.memset(before_bf[:, :], 1.0))
            pool.affine_select(out=before_bf[:, :], in_=before_bf[:, :], compare_op=ALU.is_ge, fill=0.0, base=-1,
                               pattern=[[1, P]], channel_multiplier=-1).then_inc(const_ok, 1)
            pool.iota(iota_slot[:, :], pattern=[[1, SLOTS]], base=1 + CAP - SLOTS, channel_multiplier=0,
                      allow_small_or_imprecise_dtypes=True).then_inc(const_ok, 1)
            pool.iota(iota_g[:, :], pattern=[[-1, NG]], base=NG, channel_multiplier=0,
                      allow_small_or_imprecise_dtypes=True).then_inc(const_ok, 1)
            link(pool.memset(earlier[:, :, :], 1.0))
            link(pool.affine_select(out=earlier[:, :, :], in_=earlier[:, :, :], compare_op=ALU.is_ge, fill=0.0, base=-1,
                                    pattern=[[1, GRP], [-1, GRP]], channel_multiplier=0))
            link(pool.memset(zpool[:, :, 0:N_META], 0.0))
            link(pool.memset(poolA[:, :, 0:N_META], 0.0))
            pool.memset(poolB[:, :, 0:N_META], 0.0).then_inc(const_ok, 1)
            for tt in range(3):
                link(pool.iota(dist[:, tt, :], pattern=[[1, T]], base=-C0[tt], channel_multiplier=-1,
                               allow_small_or_imprecise_dtypes=True))
                pool.affine_select(out=dist[:, tt, :], in_=dist[:, tt, :], compare_op=ALU.is_ge, fill=NEG, base=C0[tt],
                                   pattern=[[-1, T]], channel_multiplier=1).then_inc(const_ok, 1)
                if tt == 1:
                    load_gain(0)
            for g, w in enumerate(WINDOWS):
                link(pool.iota(pcount[:, g, :], pattern=[[1, N_META]], base=1, channel_multiplier=0,
                               allow_small_or_imprecise_dtypes=True))
                pool.tensor_scalar(pcount[:, g, :], pcount[:, g, :], float(w), None, ALU.min).then_inc(const_ok, 1)
            pool.iota(iota_i[:, 0:P], pattern=[[1, P]], base=0, channel_multiplier=0).then_inc(const_ok, 1)
            pool.iota(row_i[:, :], pattern=[[0, P]], base=0, channel_multiplier=1).then_inc(const_ok, 1)

            pool.wait_ge(lam_s, 4)
            for i, g in enumerate((3, 2, 1, 0)):
                job_out(pool, J0, out0, 11 + i)
                src = zpool
                for k in range(g + 1):
                    dst = (poolA, poolB)[k % 2]
                    link(pool.tensor_tensor(dst[:, g, N_META:PADW], src[:, g, N_META:PADW],
                                            src[:, g, N_META - 2 ** k:PADW - 2 ** k], ALU.add))
                    src = dst
                link(pool.tensor_scalar(src[:, g, 2 * N_META:PADW], src[:, g, 2 * N_META:PADW], 1.0 / WINDOWS[g], None, ALU.mult))
                link(pool.tensor_tensor(src[:, g, N_META:2 * N_META], src[:, g, N_META:2 * N_META], pcount[:, g, :], ALU.mult))
                pool.tensor_tensor(src[:, g, N_META:PADW], src[:, g, N_META:PADW], zpool[:, g, N_META:PADW],
                                   ALU.subtract).then_inc(pooled, 1)
            load_gain(1)
            normed(pool, 3)
            pool.dma_start(glw, odd_w_in[0][:, 3072:3072 + GLA_RANK].rearrange("(kc p) n -> p kc n", p=P)).then_inc(par1_in, 16)
            pool.dma_start(g2w[0:GLA_RANK, :], gla_gate_w2[0]).then_inc(par1_in, 16)
            pool.dma_start(gb_sb, gla_gate_b[0].rearrange("(h k) -> k h", k=P),
                           allow_slow_non_contiguous=True).then_inc(par1_in, 16)
            pool.dma_start(hn_b, gla_head_norm[0].partition_broadcast(P)).then_inc(par1_in, 16)
            load_gain(2)
            for lv in range(len(LEVELS)):
                key_factors(pool, lv)
            for tt in range(2):
                pool.wait_ge(rg_s, tt + 1)
                pool.tensor_tensor(rt[:, tt, :].rearrange("p (h v) -> p h v", h=HEADS),
                                   rt[:, tt, :].rearrange("p (h v) -> p h v", h=HEADS),
                                   hn_b.unsqueeze(1).to_broadcast([P, HEADS, GLA_DV]), ALU.mult).then_inc(rg_ok, 1)
            load_gain(3)

        @block.tensor
        def _(pe):
            def turn_tile(k, i, tt):
                if k == 0:
                    pe.wait_ge(meta_in if tt == 2 else x_in, 16 if tt == 2 else 32)
                    if i == 0:
                        pe.wait_ge(const_ok, 1)
                else:
                    pe.wait_ge(h_left, (0, 0, 3, 6)[k] + i + 1)
                for kc in range(KC):
                    if k and kc == KC // 2:
                        pe.wait_ge(h_right, (0, 0, 3, 6)[k] + i + 1)
                    c = P * (kc % 4)
                    mm = pe.transpose(bank[:, TURN_BANK[i] + kc // 4, c:c + ROWS[tt]],
                                      htok[0:ROWS[tt], tt, P * kc:P * (kc + 1)], ident[0:ROWS[tt], 0:ROWS[tt]])
                    if kc % 4 == 3:
                        mm.then_inc(hT_pe, 1)

            def hT_out(k, i, half=1):
                pe.wait_ge(hT_act, 2 * (3 * k + i) + half + 1)

            def keep_clock(n):
                for _ in range(n):
                    pe.matmul(bank[:, 0, 0:P], ident[:, :], ident[:, :], start=True, stop=True)

            def by_token(dst, src, cols, rows, w, kcs=range(KC)):
                for kc in kcs:
                    mm = pe.matmul(dst, src[:, kc, cols:cols + rows], w[:, kc, :], start=(kc == 0), stop=(kc == KC - 1),
                                   skip_group_check=len(kcs) < KC)
                return mm

            def by_channel(dst, w, src, kcs=KC):
                for kc in range(kcs):
                    mm = pe.matmul(dst, w(kc), src(kc), start=(kc == 0), stop=(kc == kcs - 1))
                return mm

            def mix_out(src, first_unit, tiles, base_col, kcs, halves=(0, 1)):
                for tt in tiles:
                    for n in halves:
                        u = unit(first_unit + n)
                        for kc in kcs:
                            mm = pe.matmul(bank[:, 2 * tt + n, :], src[:, kc, C0[tt] - base_col:C0[tt] - base_col + P], u[:, kc, :],
                                           start=(kc == 0), stop=(kc == KC - 1), skip_group_check=True)
                        if kcs[-1] == KC - 1:
                            mm.then_inc(mix_pe, 1)

            def router(layer, tiles):
                k = 1 + 2 * layer
                if layer == 0:
                    pe.wait_ge(par_in, 9 * 16)
                for i, tt in enumerate(tiles):
                    turn_tile(k, i, tt)
                    c = slice(C0[tt], C0[tt] + ROWS[tt])
                    for kc in range(KC):
                        if kc % 4 == 0:
                            hT_out(k, i, kc // 4)
                        mm = pe.matmul(bank[0:E, 6, c], rw[:, kc, :], hT[:, kc, c], start=(kc == 0), stop=(kc == KC - 1))
                mm.then_inc(lgt_pe, 1)
                pe.wait_ge(lgt_ev, layer + 1)
                for tt in tiles:
                    mm = pe.transpose(bank[0:ROWS[tt], 7, E * tt:E * tt + E], lgT[:, C0[tt]:C0[tt] + ROWS[tt]], ident[0:E, 0:E])
                mm.then_inc(lg_pe, 1)
                keep_clock((24, 16)[layer])
                pe.wait_ge(pick_ok, layer + 1)
                if layer == 0:
                    pe.wait_ge(const_ok, 3)
                order = sorted(tiles)
                for tt in order + [3]:
                    rows = P if tt == 3 else ROWS[tt]
                    prev = [t for t in order if t < tt]
                    terms = [(ones_bf[0:ROWS[t], 0:rows], t) for t in prev]
                    if tt < 3:
                        terms.append((before_bf[0:ROWS[tt], 0:rows], tt))
                    for i, (lhs, t) in enumerate(terms):
                        mm = pe.matmul(bank[0:rows, 7 if tt == 3 else 5, E * tt:E * tt + E], lhs, picked_bf[0:ROWS[t], t, :],
                                       start=(i == 0), stop=(i == len(terms) - 1))
                mm.then_inc(pos_pe, 1)

            def experts(layer, tiles):
                base = BASE_MOE[layer]
                nt = len(tiles)
                ns = len(scatter_order(layer, False))
                L = layer

                def gather(g, p, half):
                    if half == 0:
                        pe.wait_ge(s_ready[L], nt * (2 * g + p + 1))
                    for c in range(4):
                        kc = 4 * half + c
                        for i, tt in enumerate(tiles):
                            mm = pe.matmul(bank[:, 4 + half, P * c:P * (c + 1)], htok[0:ROWS[tt], tt, P * kc:P * (kc + 1)],
                                           onehot[0:ROWS[tt], tt, P * p:P * (p + 1)], start=(i == 0), stop=(i == nt - 1))
                    mm.then_inc(gth_pe[L], 1)

                def ring_wait(g, i):
                    n = base + i
                    pe.wait_ge(ring_in[n % NR], g * (16 * GROUP_UNITS // NR) + 16 * (n // NR + 1))

                def group(g, last):
                    def gate_up(p):
                        pe.wait_ge(gth_ev[L], g * 4 + 2 * p + 2)
                        for k in range(2):
                            for e in range(2):
                                ring_wait(g, PAIR_UNITS * p + 2 * k + e)
                            for kc in range(KC):
                                for e in range(2):
                                    s0 = SLOTS * (2 * p + e)
                                    mm = pe.matmul(bank[SLOTS * e:SLOTS * (e + 1), 2 * p + k, :], xg[:, kc, s0:s0 + SLOTS],
                                                   unit(base + PAIR_UNITS * p + 2 * k + e)[:, kc, :],
                                                   start=(kc == 0), stop=(kc == KC - 1))
                            mm.then_inc((gate_pe, up_pe)[k][L], 1)

                    def turn_pair(p):
                        pe.wait_ge(act_ok[L], g * 2 + p + 1)
                        for fc in range(4):
                            mm = pe.transpose(bank[:, 2 * p, P * fc:P * (fc + 1)], act_sb[:, p, P * fc:P * (fc + 1)], ident[:, :])
                        mm.then_inc(t_pe[L], 1)
                        pe.wait_ge(sw_ready[L], nt * (2 * g + p + 1))
                        for tt in sorted(tiles):
                            mm = pe.transpose(bank[:, 2 * p + 1, C0[tt]:C0[tt] + ROWS[tt]],
                                              whot[0:ROWS[tt], tt, P * p:P * (p + 1)], ident[0:ROWS[tt], 0:ROWS[tt]])
                        mm.then_inc(w_pe[L], 1)

                    def down(p):
                        pe.wait_ge(t_ev[L], g * 2 + p + 1)
                        for n in range(2):
                            i = PAIR_UNITS * p + 4 + n
                            ring_wait(g, i)
                            for fc in range(4):
                                for e in range(2):
                                    mm = pe.matmul(bank[SLOTS * e:SLOTS * (e + 1), 6 + n, :], actT[:, fc, SLOTS * e:SLOTS * (e + 1)],
                                                   unit(base + i)[:, 4 * e + fc, :], start=(fc == 0), stop=(fc == 3))
                            mm.then_inc(d_pe[L], 1)

                    def scatter(p):
                        pe.wait_ge(w_ev[L], g * 2 + p + 1)
                        for i, (tt, n) in enumerate(scatter_order(L, last and p == 1)):
                            s = ns * p + i
                            if i == 0 and not (last and p == 1):
                                pe.wait_ge(gth_ev[L], g * 4 + 2 * p + 4)
                            if s >= 2:
                                pe.wait_ge(sc_ev[L], g * (2 * ns) + s)
                            pe.wait_ge(d_ev[L], g * 4 + 2 * p + min(n, 1) + 1)
                            if tt == 2:
                                for q in range(4):
                                    mm = pe.matmul(bank[32 * q:32 * (q + 1), 4 + s % 2, 0:SEQ], whotT[:, p, 0:32],
                                                   o_sb[:, SEQ * q:SEQ * (q + 1)], start=True, stop=True, skip_group_check=True)
                            else:
                                mm = pe.matmul(bank[:, 4 + s % 2, :], whotT[:, p, C0[tt]:C0[tt] + P],
                                               o_sb[:, 512 * n:512 * (n + 1)], start=True, stop=True)
                            mm.then_inc(sc_pe[L], 1)

                    for p in range(2):
                        gate_up(p)
                        following = (g, 1) if p == 0 else (g + 1, 0)
                        if p == 0 or not last:
                            pe.wait_ge(sc_ev[L], (2 * g + p) * ns + 1)
                            gather(*following, 0)
                        turn_pair(p)
                        if p == 0 or not last:
                            gather(*following, 1)
                        down(p)
                        scatter(p)

                keep_clock(7)
                gather(0, 0, 0)
                gather(0, 0, 1)
                late(pe, L)
                with pe.Fori(0, NG - 1) as g:
                    group(g, False)
                group(NG - 1, True)

            for i, tt in enumerate((2, 0, 1)):
                turn_tile(0, i, tt)
            hT_out(0, 2)

            def job0(n):
                kind, m, _ = J0[n]
                if n >= 8:
                    job_out(pe, J0, out0, (4, 5, 7)[n - 8] if n < 11 else n - 1)
                u = unit("QKVU".index(kind))
                if n < 2:
                    pe.wait_ge(first_half, 16)
                else:
                    arrived(pe, "QKVU".index(kind))
                b = bank0(n)
                if kind != "V":
                    mm = by_channel(bank[:, b, 0:T], lambda kc: u[:, kc, P * m:P * (m + 1)], lambda kc: hT[:, kc, :])
                elif m == 2:
                    mm = meta_quarters(pe, bank[:, b, :], hT, lambda kc, q: u[:, kc, P * q:P * (q + 1)])
                else:
                    mm = by_token(bank[:, b, :], hT, C0[m], P, u)
                mm.then_inc(pj0_pe, 1)

            def scores(i):
                tt, hp = STEPS[i]
                nk = C0[tt] + ROWS[tt]
                if i == 0:
                    job_out(pe, J0, out0, 6)
                    job_out(pe, J0, out0, 7)
                else:
                    pe.wait_ge(at_b, 2 * i)
                for j in range(4):
                    h, m = 2 * hp + j // 2, j % 2
                    mm = pe.matmul(bank[0:ROWS[tt], j, 0:nk], zq[64 * m:64 * (m + 1), h, C0[tt]:C0[tt] + ROWS[tt]],
                                   zk[64 * m:64 * (m + 1), h, 0:nk], start=True, stop=True)
                mm.then_inc(at_s, 1)

            def turn_probs(i):
                tt, hp = STEPS[i]
                rows = ROWS[tt]
                if i == 0:
                    job_out(pe, J0, out0, 9)
                pe.wait_ge(at_pd, 2 * i + 2)
                for j in range(2):
                    for kt in KEYS[tt]:
                        mm = pe.transpose(bank[0:ROWS[kt], 4 + j, P * kt:P * kt + rows],
                                          pd[0:rows, j, C0[kt]:C0[kt] + ROWS[kt]], ident[0:rows, 0:rows])
                mm.then_inc(at_t, 1)

            def heads(i):
                tt, hp = STEPS[i]
                rows = ROWS[tt]
                ks = KEYS[tt]
                if i == 0:
                    job_out(pe, J0, out0, 10)
                pe.wait_ge(at_te, i + 1)
                if i >= 1:
                    pe.wait_ge(at_oe, i)
                for j in range(2):
                    h = 2 * hp + j
                    for a, kt in enumerate(ks):
                        mm = pe.matmul(bank[0:rows, 6, P * j:P * (j + 1)], pT[0:ROWS[kt], j, kt, 0:rows],
                                       v0[0:ROWS[kt], kt, P * h:P * (h + 1)], start=(a == 0), stop=(a == len(ks) - 1))
                mm.then_inc(at_o, 1)

            for n in range(8):
                job0(n)
            scores(0)
            job0(8)
            job0(9)
            scores(1)
            turn_probs(0)
            job0(10)
            for i in range(2, 6):
                scores(i)
                heads(i - 2)
                turn_probs(i - 1)
                job0(9 + i)
            heads(4)
            turn_probs(5)
            for i, g in enumerate((3, 2, 1, 0)):
                pe.wait_ge(pooled, i + 1)
                if i == 0:
                    job_out(pe, J0, out0, 14)
                else:
                    pe.wait_ge(poolev, i)
                pe.matmul(bank[:, 7, 0:T], pw_sb[:, g, :], (poolA, poolB)[g % 2][:, g, N_META:PADW],
                          start=True, stop=True).then_inc(poolmm, 1)
                if i == 1:
                    heads(5)
            pe.wait_ge(poolev, 4)
            for n in range(2):
                arrived(pe, 4 + n)
            mix_out(yT, 4, (0, 1), 0, range(4))
            for i, tt in enumerate((2, 0, 1)):
                pe.wait_ge(o_n, i + 1)
                for h in range(HEADS):
                    mm = pe.transpose(bank[:, 5 + i, P * h:P * h + ROWS[tt]], o_tok[0:ROWS[tt], tt, P * h:P * (h + 1)],
                                      ident[0:ROWS[tt], 0:ROWS[tt]])
                mm.then_inc(yt_pe, 1)
            pe.wait_ge(yt_act, 2)
            meta_quarters(pe, bank[:, 4, :], yT, lambda kc, q: unit(4 + q // 2)[:, kc, SEQ * (q % 2):SEQ * (q % 2 + 1)]).then_inc(mix_pe, 1)
            mix_out(yT, 4, (0,), 0, range(4, KC))
            pe.wait_ge(yt_dve, 1)
            mix_out(yT, 4, (1,), 0, range(4, KC))
            router(0, (2, 0, 1))
            experts(0, (2, 0, 1))

            def job1(n, kcs=range(KC)):
                kind, m, _, b = J1[n]
                before = [i for i in range(n) if J1[i][3] == b]
                if before and kcs[0] == 0:
                    job_out(pe, J1, out1, before[-1])
                if kind == "G":
                    mm = by_channel(bank[0:GLA_RANK, b, 0:T], lambda kc: glw[:, kc, :], lambda kc: hT[:, kc, :])
                if kind == "A":
                    job_out(pe, J1, out1, 3)
                    mm = pe.matmul(bank[:, b, 0:T], g2w[0:GLA_RANK, P * m:P * (m + 1)], glr[0:GLA_RANK, :], start=True, stop=True)
                if kind in "QK":
                    u = BASE_ODD + (kind == "K")
                    arrived(pe, u)
                    c = N_META if kind == "Q" else 0
                    mm = by_channel(bank[:, b, 0:T - c], lambda kc: unit(u)[:, kc, P * m:P * (m + 1)], lambda kc: hT[:, kc, c:T])
                if kind in "VR":
                    half, tt = m
                    u = BASE_ODD + (2 if kind == "V" else 4) + half
                    arrived(pe, u)
                    mm = by_token(bank[:, b, :], hT, C0[tt], P, unit(u), kcs)
                if kind == "M":
                    mm = meta_quarters(pe, bank[:, b, :], hT,
                                       lambda kc, q: unit(BASE_ODD + 2 + q // 2)[:, kc, SEQ * (q % 2):SEQ * (q % 2 + 1)])
                if kcs[-1] == KC - 1:
                    mm.then_inc(pj1_pe, 1)

            nl = len(LEVELS)

            def level(st):
                b = 2 * (st % 2)
                if st >= 2:
                    pe.wait_ge(lv_ev, 2 * min(st - 1, nl + 1))
                if st < nl:
                    pe.wait_ge(lv_q, st + 1)
                    pe.wait_ge(lv_k, st + 2)
                if st <= nl:
                    for tt in range(2):
                        for h in range(HEADS):
                            if st < nl:
                                a, c = kl[:, h, P * tt:P * (tt + 1)], ql[:, h, P * tt:P * (tt + 1)]
                            else:
                                a, c = kT[:, h, C0[tt]:C0[tt] + P], qT[:, h, P * tt:P * (tt + 1)]
                            mm = pe.matmul(bank[:, b + tt, P * h:P * (h + 1)], a, c, start=True, stop=True)
                        mm.then_inc(lv_pe, 1)
                if st == nl + 1:
                    pe.wait_ge(lv_q, nl + 1)
                    for h in range(HEADS):
                        mm = pe.matmul(bank[:, b, P * h:P * (h + 1)], kl[:, h, 0:P], ql[:, h, P:SEQ], start=True, stop=True)
                    mm.then_inc(lv_pe, 1)
                if st == nl + 2:
                    pe.wait_ge(lv_q, nl + 2)
                    for h in range(HEADS):
                        mm = pe.matmul(bank[0:N_META, b + h // 2, SEQ * (h % 2):SEQ * (h % 2 + 1)], kl[:, h, 0:N_META],
                                       ql[:, h, :], start=True, stop=True)
                    mm.then_inc(lv_pe, 1)

            keep_clock(2)
            turn_tile(2, 0, FFN_ORDER[0])
            hT_out(2, 0)
            pe.wait_ge(sc_ev[0], 1 + 2 * 5 * NG)
            job1(0)
            job1(1)
            turn_tile(2, 1, FFN_ORDER[1])
            hT_out(2, 1)
            job1(2)
            turn_tile(2, 2, FFN_ORDER[2])
            hT_out(2, 2)
            pe.wait_ge(par1_in, 4 * 16)
            for n in range(3, NLV):
                job1(n)
            for st in range(nl + 3):
                if st < 2:
                    job1(NLV + st)
                else:
                    job1(NLV + 1 + st // 2, range(4) if st % 2 == 0 else range(4, KC))
                level(st)
            pe.wait_ge(lv_ev, 2 * (nl + 1))
            pe.wait_ge(lv_act, 3)
            for n in (2, NLV, NLV + 1):
                job_out(pe, J1, out1, n)
            for tt in range(2):
                for c in range(2):
                    for h in (2 * c, 2 * c + 1):
                        dst = bank[:, 2 * tt + c, GLA_DV * (h % 2):GLA_DV * (h % 2 + 1)]
                        vh = vt[:, :, GLA_DV * h:GLA_DV * (h + 1)]
                        pe.matmul(dst, attM[0:N_META, h, P * tt:P * (tt + 1)], vh[0:N_META, 2, :], start=True, stop=False)
                        if tt == 1:
                            pe.matmul(dst, att01[:, h, :], vh[:, 0, :], start=False, stop=False)
                        mm = pe.matmul(dst, att[:, HEADS * tt + h, :], vh[:, tt, :], start=False, stop=True)
                    mm.then_inc(go_pe, 1)
            for n in range(len(J1) - 4, len(J1)):
                job_out(pe, J1, out1, n)

            def turn_gated(tt):
                pe.wait_ge(ogt_ok, HEADS * (tt + 1))
                for c in range(KC):
                    mm = pe.transpose(bank[:, 4 + 2 * tt + c // 4, P * (c % 4):P * (c % 4 + 1)], og[:, tt, P * c:P * (c + 1)],
                                      ident[:, :])
                mm.then_inc(ogt_pe, 1)

            turn_gated(0)
            for n in range(2):
                arrived(pe, BASE_ODD + 6 + n)
            pe.wait_ge(ogt_ev, 1)
            pe.wait_ge(go_ev, 2)
            mix_out(ogT, BASE_ODD + 6, (0,), N_META, range(KC), (0,))
            turn_gated(1)
            mix_out(ogT, BASE_ODD + 6, (0,), N_META, range(KC), (1,))
            pe.wait_ge(ogt_ev, 2)
            pe.wait_ge(go_ev, 4)
            mix_out(ogT, BASE_ODD + 6, (1,), N_META, range(KC))
            router(1, (0, 1))
            experts(1, (0, 1))

        @block.scalar
        def _(act):
            count = [0]

            def link(ins):
                count[0] += 1
                ins.then_inc(act_c, 1)
                act.wait_ge(act_c, count[0])

            act.dma_start(pw_sb, pool_w[0].rearrange("g c d -> c g d")).then_inc(par_in, 16)
            act.dma_start(small[:, 8:12], pool_scale[0].rearrange("(g c) -> c g", c=P),
                          allow_slow_non_contiguous=True).then_inc(par_in, 16)
            for i, v in enumerate((diff_lq1, diff_lk1, diff_lq2, diff_lk2)):
                act.dma_start(lam_v[:, i, :], v[0].partition_broadcast(P)).then_inc(par_in, 16)
            act.dma_start(sub_b[:, :], diff_subln[0].partition_broadcast(P)).then_inc(par_in, 16)
            act.dma_start(rw[:, :, :], router_w.rearrange("(kc p) e -> p kc e", p=P)).then_inc(par_in, 16)
            act.dma_start(rbias[:, :], router_bias.partition_broadcast(P)).then_inc(par_in, 16)

            def turn_tile(k, i, tt):
                for half in range(2):
                    act.wait_ge(hT_pe, 2 * (3 * k + i) + half + 1)
                    act.copy(hT[:, 4 * half:4 * (half + 1), C0[tt]:C0[tt] + ROWS[tt]],
                             bank[:, TURN_BANK[i] + half, :].rearrange("p (c t) -> p c t", c=4)[:, :, 0:ROWS[tt]]).then_inc(hT_act, 1)

            def norm_tile(k, i, tt):
                r = ROWS[tt]
                act.wait_ge(var_ok, (0, 3, 6, 8)[k] + i + 1)
                act.activation(rstd[0:r, tt, :], mv[0:r, tt, 1:2], ACT.Sqrt, bias=eps_ln[0:r, :]).then_inc(sd_ok, 1)

            def router(layer, tiles):
                k = 1 + 2 * layer
                for i, tt in enumerate(tiles):
                    if i == len(tiles) - 1:
                        norm_tile(k - 1, i, tt)
                    turn_tile(k, i, tt)
                act.activation(small[:, 30:31], one, ACT.Exp)
                c = 0 if layer == 0 else N_META
                act.wait_ge(lgt_pe, layer + 1)
                act.copy(lgT[:, c:T], bank[0:E, 6, c:T]).then_inc(lgt_ev, 1)
                act.wait_ge(lg_max, layer + 1)
                act.activation(pr[:, 0:len(tiles), :], lg[:, 0:len(tiles), :], ACT.Exp).then_inc(lg_exp, 1)
                for tt in range(2):
                    act.mul(yacc[:, tt, :], htok[:, tt, :], ALPHA).then_inc(yinit, 1)
                if layer == 0:
                    act.wait_ge(ym_zero, 1)
                    for q in range(4):
                        act.mul(ymeta[32 * q:32 * q + N_META, :], htok[0:N_META, 2, SEQ * q:SEQ * (q + 1)], ALPHA).then_inc(yinit, 1)
            def experts(layer, tiles):
                L = layer

                def gather_out(g, p, halves=(0, 1)):
                    for f in halves:
                        act.wait_ge(gth_pe[L], g * 4 + 2 * p + f + 1)
                        act.copy(xg[:, 4 * f:4 * (f + 1), P * p:P * (p + 1)],
                                 bank[:, 4 + f, :].rearrange("p (a b) -> p a b", a=4)).then_inc(gth_ev[L], 1)

                def group(g, last):
                    for p in range(2):
                        act.wait_ge(gate_pe[L], g * 2 + p + 1)
                        act.activation(act_sb[:, p, :], bank[:, 2 * p, :], ACT.Silu).then_inc(silu_ok[L], 1)
                        following = (g, 1) if p == 0 else (g + 1, 0)
                        if p == 0 or not last:
                            gather_out(*following, (0,))
                        act.wait_ge(t_pe[L], g * 2 + p + 1)
                        act.copy(actT, bank[:, 2 * p, :].rearrange("p (a b) -> p a b", a=4)).then_inc(t_ev[L], 1)
                        if p == 0 or not last:
                            gather_out(*following, (1,))
                        for n in range(2):
                            act.wait_ge(d_pe[L], g * 4 + 2 * p + n + 1)
                            act.copy(o_sb[:, 512 * n:512 * (n + 1)], bank[:, 6 + n, :]).then_inc(d_ev[L], 1)

                gather_out(0, 0)
                late(act, L)
                with act.Fori(0, NG - 1) as g:
                    group(g, False)
                group(NG - 1, True)

            for i, tt in enumerate((2, 0, 1)):
                turn_tile(0, i, tt)

            def job0(n):
                kind, m, _ = J0[n]
                act.wait_ge(pj0_pe, n + 1)
                b = bank0(n)
                if kind in "QK":
                    act.copy((zq, zk)[kind == "K"][:, m, :], bank[:, b, 0:T]).then_inc(pj0_act, 1)
                elif kind == "U":
                    act.copy(zpool[:, m, N_META:PADW], bank[:, b, 0:T]).then_inc(pj0_act, 1)
                elif m == 2:
                    for q in range(4):
                        cp = act.copy(v0[0:N_META, 2, P * q:P * (q + 1)], bank[32 * q:32 * q + N_META, b, 0:P])
                        if q < 3:
                            link(cp)
                    cp.then_inc(pj0_act, 1)
                else:
                    act.copy(v0[:, m, :], bank[:, b, :]).then_inc(pj0_act, 1)

            def exps(i):
                tt, hp = STEPS[i]
                r, nk = ROWS[tt], C0[tt] + ROWS[tt]
                act.wait_ge(at_m, i + 1)
                for j in range(4):
                    sv = s_sb[0:r, i % 2, j, 0:nk]
                    act.activation(sv, sv, ACT.Exp, bias=mx[0:r, i, j:j + 1], scale=ATT_SCALE,
                                   accum_out=sums[0:r, i, j:j + 1]).then_inc(at_e, 1)

            def probs_copy(i):
                tt, hp = STEPS[i]
                rows = ROWS[tt]
                act.wait_ge(at_t, i + 1)
                n = (1, 2, 0)[tt]
                if n:
                    link(act.copy(pT[:, :, 0:n, :], bank[:, 4:6, 0:P * n].rearrange("p b (a c) -> p b a c", c=P)))
                act.copy(pT[0:N_META, :, 2, 0:rows], bank[0:N_META, 4:6, 2 * P:2 * P + rows]).then_inc(at_te, 1)

            for n in range(1, 8, 2):
                job0(n)
            act.wait_ge(lam_e, 2)
            link(act.activation(lam1, lam1, ACT.Exp))
            link(act.activation(lam2, lam2, ACT.Exp))
            exps(0)
            job0(8)
            job0(9)
            for i in range(1, 6):
                probs_copy(i - 1)
                exps(i)
                job0(9 + i)
            probs_copy(5)
            for i, g in enumerate((3, 2, 1, 0)):
                act.wait_ge(poolmm, i + 1)
                act.mul(yT[:, g, :], bank[:, 7, 0:T], small[:, 8 + g:9 + g]).then_inc(poolev, 1)
            act.wait_ge(o_ss, 12)
            act.activation(rstd0, ss0, ACT.Sqrt, bias=eps_rms, scale=1.0 / P).then_inc(o_rs, 1)
            for i, tt in enumerate((2, 0)):
                act.wait_ge(yt_pe, i + 1)
                act.copy(yT[:, 4:8, C0[tt]:C0[tt] + ROWS[tt]],
                         bank[:, 5 + i, :].rearrange("p (h t) -> p h t", h=HEADS)[:, :, 0:ROWS[tt]]).then_inc(yt_act, 1)
            norm_tile(0, 0, 2)
            norm_tile(0, 1, 0)
            router(0, (2, 0, 1))
            experts(0, (2, 0, 1))

            def job1(n):
                kind, m, by, b = J1[n]
                if by != "a":
                    return
                act.wait_ge(pj1_pe, n + 1)
                if kind == "Q":
                    act.mul(qT[:, m, :], bank[:, b, 0:SEQ], GLA_SCALE).then_inc(pj1_act, 1)
                if kind == "K":
                    act.copy(kT[:, m, :], bank[:, b, 0:T]).then_inc(pj1_act, 1)
                if kind in "VR":
                    half, tt = m
                    act.copy((vt if kind == "V" else rt)[:, tt, 512 * half:512 * (half + 1)], bank[:, b, :]).then_inc(pj1_act, 1)
                if kind == "M":
                    for q in range(4):
                        cp = act.copy(vt[0:N_META, 2, SEQ * q:SEQ * (q + 1)], bank[32 * q:32 * q + N_META, b, 0:SEQ])
                        if q < 3:
                            link(cp)
                    cp.then_inc(pj1_act, 1)

            norm_tile(1, 0, FFN_ORDER[0])
            turn_tile(2, 0, FFN_ORDER[0])
            act.wait_ge(sc_ev[0], 10 * NG - 1)
            for q in range(4):
                act.copy(meta_row[0:N_META, SEQ * q:SEQ * (q + 1)], ymeta[32 * q:32 * q + N_META, :]).then_inc(ym_out, 1)
            norm_tile(1, 1, FFN_ORDER[1])
            norm_tile(1, 2, FFN_ORDER[2])
            job1(0)
            job1(1)
            turn_tile(2, 1, FFN_ORDER[1])
            job1(2)
            turn_tile(2, 2, FFN_ORDER[2])
            for h in range(HEADS):
                act.wait_ge(gla_ab, h + 1)
                act.activation(la[:, h, :], la[:, h, :], ACT.Exp, scale=-1.0).then_inc(gla_e, 1)
            act.wait_ge(gla_e, 4)
            for h in range(HEADS):
                act.activation(la[:, h, :], la[:, h, :], ACT.Ln, bias=one).then_inc(gla_ln, 1)

            for n in range(3, NLV):
                job1(n)
            nl = len(LEVELS)
            for st in range(nl + 3):
                if st != nl:
                    d = st if st < nl else st - 1
                    act.wait_ge(lv_d, d + 1)
                    act.activation(dec, dec, ACT.Exp).then_inc(lv_e, 1)
                if st == nl + 2:
                    act.wait_ge(gla_b, 5)
                    act.activation(la[:, :, 0:N_META], la[:, :, 0:N_META], ACT.Exp).then_inc(lv_e, 1)
                    job_out(act, J1, out1, len(J1) - 4)
                    job_out(act, J1, out1, len(J1) - 3)
                    act.activation(rt[:, 0, :], rt[:, 0, :], ACT.Silu).then_inc(rg_s, 1)
                if st < 2 or st % 2:
                    job1(NLV + (st if st < 2 else 1 + st // 2))
                if st == nl + 2:
                    act.wait_ge(lv_pe, 2 * (nl + 1) + 1)
                    act.copy(att01, bank[:, 2 * ((nl + 1) % 2), :].rearrange("p (h t) -> p h t", h=HEADS)).then_inc(lv_act, 1)
            act.wait_ge(lv_pe, 2 * (nl + 1) + 2)
            for c in range(2):
                act.copy(attM[0:N_META, 2 * c:2 * c + 2, :],
                         bank[0:N_META, 2 * (nl % 2) + c, :].rearrange("p (h t) -> p h t", h=2)).then_inc(lv_act, 1)
            job_out(act, J1, out1, len(J1) - 1)
            act.activation(rt[:, 1, :], rt[:, 1, :], ACT.Silu).then_inc(rg_s, 1)
            for tt in range(2):
                heads = slice(HEADS * tt, HEADS * (tt + 1))
                act.wait_ge(o_ss, 12 + HEADS * (tt + 1))
                act.activation(rstd1[:, heads], ss1[:, heads], ACT.Sqrt, bias=eps_rms, scale=1.0 / GLA_DV).then_inc(o_rs, 1)
                act.wait_ge(ogt_pe, tt + 1)
                b = 4 + 2 * tt
                act.copy(ogT[:, :, P * tt:P * (tt + 1)],
                         bank[:, b:b + 2, :].rearrange("p b (c t) -> p (b c) t", c=4)).then_inc(ogt_ev, 1)
            norm_tile(2, 0, 0)
            router(1, (0, 1))
            experts(1, (0, 1))
            norm_tile(3, 0, 0)
            norm_tile(3, 1, 1)

        @block.vector
        def _(dve):
            count = [0]

            def link(ins):
                count[0] += 1
                ins.then_inc(dve_c, 1)
                dve.wait_ge(dve_c, count[0])

            def norm_centre(k, i, tt):
                r = ROWS[tt]
                n = (0, 3, 6, 8)[k] + i + 1
                src = (htok if k % 2 == 0 else yacc)[0:r, tt, :]
                if tt < 2:
                    dve.wait_ge(st_ok, 4 * k + 2 * tt + 2)
                else:
                    for half in range(2):
                        link(dve.bn_stats(stats[0:r, tt, half, :], src[:, 512 * half:512 * (half + 1)]))
                dve.bn_aggr(mv[0:r, tt, :], stats[0:r, tt, :, :]).then_inc(var_ok, 1)
                dve.wait_ge(var_ok, n)
                if i == 0:
                    dve.wait_ge(gain_in, 32 * (k + 1))
                link(dve.scalar_tensor_tensor(htok[0:r, tt, :], src, mv[0:r, tt, 0:1], gain[0:r, 0, :], ALU.subtract, ALU.mult))

            def norm_scale(k, i, tt):
                r = ROWS[tt]
                dve.wait_ge(sd_ok, (0, 3, 6, 8)[k] + i + 1)
                link(dve.reciprocal(rstd[0:r, tt, :], rstd[0:r, tt, :]))
                for half, done in enumerate((h_left, h_right)):
                    h = htok[0:r, tt, 512 * half:512 * (half + 1)]
                    dve.scalar_tensor_tensor(h, h, rstd[0:r, tt, :], gain[0:r, 1, 512 * half:512 * (half + 1)],
                                             ALU.mult, ALU.add).then_inc(done, 1)

            def norm_tile(k, i, tt):
                norm_centre(k, i, tt)
                norm_scale(k, i, tt)

            def mix_tile(done, tt):
                if tt == 2:
                    dve.wait_ge(mix_pe, done + 1)
                    for q in range(4):
                        c = slice(SEQ * q, SEQ * (q + 1))
                        link(dve.scalar_tensor_tensor(htok[0:N_META, 2, c], htok[0:N_META, 2, c], ALPHA,
                                                      bank[32 * q:32 * q + N_META, 4, 0:SEQ], ALU.mult, ALU.add))
                    return
                for n in range(2):
                    dve.wait_ge(mix_pe, done + n + 1)
                    c = slice(512 * n, 512 * (n + 1))
                    link(dve.scalar_tensor_tensor(htok[:, tt, c], htok[:, tt, c], ALPHA, bank[:, 2 * tt + n, :], ALU.mult, ALU.add))
                    dve.bn_stats(stats[:, tt, n, :], htok[:, tt, c]).then_inc(st_ok, 1)

            def router(layer, tiles):
                nt = len(tiles)
                a = slice(0, nt)
                dve.wait_ge(lg_pe, layer + 1)
                if nt == 3:
                    link(dve.tensor_copy(lg[0:N_META, 2, :], bank[0:N_META, 7, 2 * E:3 * E]))
                link(dve.tensor_copy(lg[:, 0:2, :], bank[:, 7, 0:2 * E].rearrange("p (t e) -> p t e", t=2)))
                link(dve.tensor_reduce(r1[:, a, :], lg[:, a, :], AX.X, ALU.max))
                dve.tensor_tensor(lg[:, a, :], lg[:, a, :], r1[:, a, :].to_broadcast([P, nt, E]), ALU.subtract).then_inc(lg_max, 1)
                dve.wait_ge(lg_exp, layer + 1)
                link(dve.tensor_reduce(r1[:, a, :], pr[:, a, :], AX.X, ALU.add))
                link(dve.reciprocal(r1[:, a, :], r1[:, a, :]))
                link(dve.tensor_tensor(pr[:, a, :], pr[:, a, :], r1[:, a, :].to_broadcast([P, nt, E]), ALU.mult))
                link(dve.tensor_tensor(sel[:, a, :], pr[:, a, :], rbias[:, :].unsqueeze(1).to_broadcast([P, nt, E]), ALU.add))
                n = nt * NG
                s4 = sel[:, a, :].rearrange("p t (g c) -> p (t g) c", c=GRP)
                shape = [P, n, GRP, GRP]
                ab, eq, rk = above[:, 0:n, :, :], equal[:, 0:n, :, :], rank[:, 0:n, :]
                j_side, i_side = s4.unsqueeze(2).to_broadcast(shape), s4.unsqueeze(3).to_broadcast(shape)
                dve.tensor_tensor(eq, j_side, i_side, ALU.is_equal).then_inc(eq_ok, 1)
                link(dve.tensor_tensor(ab, j_side, i_side, ALU.is_gt))
                dve.wait_ge(eq_ok, layer + 1)
                link(dve.tensor_tensor(eq, eq, earlier[:, :, :].unsqueeze(1).to_broadcast(shape), ALU.mult))
                link(dve.tensor_tensor(ab, ab, eq, ALU.add))
                link(dve.tensor_reduce(rk, ab, AX.X, ALU.add))
                t4 = t1[:, a, :].rearrange("p t (g c) -> p (t g) c", c=GRP)
                link(dve.scalar_tensor_tensor(t4, rk, 1.5, s4, ALU.is_lt, ALU.mult))
                gv = gs[:, a, :].rearrange("p t g -> p (t g)")
                link(dve.tensor_reduce(gv, t4, AX.X, ALU.add))
                g3 = gs[:, a, :]
                link(dve.tensor_reduce(r1[:, a, :], g3, AX.X, ALU.max))
                link(dve.tensor_tensor(g3, g3, r1[:, a, :].to_broadcast([P, nt, NG]), ALU.is_equal))
                link(dve.tensor_tensor(g3, g3, iota_g[:, :].unsqueeze(1).to_broadcast([P, nt, NG]), ALU.mult))
                link(dve.tensor_reduce(r2[:, a, :], g3, AX.X, ALU.max))
                link(dve.tensor_tensor(ghot[:, a, :], g3, r2[:, a, :].to_broadcast([P, nt, NG]), ALU.is_equal))
                hot = ghot[:, a, :].rearrange("p t g -> p (t g)").unsqueeze(2).to_broadcast([P, n, GRP])
                dve.scalar_tensor_tensor(picked_bf[:, a, :].rearrange("p t (g c) -> p (t g) c", c=GRP), rk, 1.5, hot,
                                         ALU.is_lt, ALU.mult).then_inc(pick_ok, 1)
                dve.wait_ge(pick_ok, layer + 1)
                link(dve.tensor_tensor(weight[:, a, :], pr[:, a, :], picked_bf[:, a, :], ALU.mult))
                link(dve.tensor_reduce(r1[:, a, :], weight[:, a, :], AX.X, ALU.add))
                link(dve.reciprocal(r1[:, a, :], r1[:, a, :]))
                link(dve.tensor_tensor(weight[:, a, :], weight[:, a, :], r1[:, a, :].to_broadcast([P, nt, E]), ALU.mult))
                dve.wait_ge(pos_pe, layer + 1)
                if nt == 3:
                    dve.scalar_tensor_tensor(slot_of[0:N_META, 2, :], bank[0:N_META, 5, 2 * E:3 * E], 1.0,
                                             picked_bf[0:N_META, 2, :], ALU.add, ALU.mult).then_inc(slot_ok, 1)
                dve.scalar_tensor_tensor(slot_of[:, 0:2, :], bank[:, 5, 0:2 * E].rearrange("p (t e) -> p t e", t=2), 1.0,
                                         picked_bf[:, 0:2, :], ALU.add, ALU.mult).then_inc(slot_ok, 1)
                dve.wait_ge(slot_ok, (2, 3)[layer])

            def overflow(layer, nt):
                a = slice(0, nt)
                link(dve.tensor_reduce(over[:, 0:1], bank[:, 7, 3 * E:4 * E], AX.X, ALU.max))
                link(dve.tensor_scalar(over[:, 1:2], over[:, 0:1], float(CAP), None, ALU.is_gt))
                dve.tensor_copy(over_i[:, :], over[:, 1:2]).then_inc(flag_ok, 1)
                dve.memset(small[:, 29:30], 0.0).then_inc(sc_ev[layer], 1)
                link(dve.scalar_tensor_tensor(late_w[:, a, :], slot_of[:, a, :], float(CAP), weight[:, a, :], ALU.is_gt, ALU.mult))

            def experts(layer, tiles):
                L = layer
                nt = len(tiles)
                ns = len(scatter_order(L, False))

                def experts_of(v, r, tt, g, p):
                    cols = bass.ds(g * GRP + 2 * p, 2) if not isinstance(g, int) else slice(g * GRP + 2 * p, g * GRP + 2 * p + 2)
                    return v[0:r, tt, cols].unsqueeze(2).to_broadcast([r, 2, SLOTS])

                def build(g, p):
                    for tt in tiles:
                        r = ROWS[tt]
                        dve.tensor_tensor(onehot[0:r, tt, P * p:P * (p + 1)].rearrange("p (e s) -> p e s", e=2),
                                          iota_slot[0:r, :].unsqueeze(1).to_broadcast([r, 2, SLOTS]),
                                          experts_of(slot_of, r, tt, g, p), ALU.is_equal).then_inc(s_ready[L], 1)

                def slot_weights(g, p):
                    dve.wait_ge(s_ready[L], nt * (2 * g + p + 1))
                    for tt in tiles:
                        r = ROWS[tt]
                        c = slice(P * p, P * (p + 1))
                        dve.tensor_tensor(whot[0:r, tt, c].rearrange("p (e s) -> p e s", e=2),
                                          onehot[0:r, tt, c].rearrange("p (e s) -> p e s", e=2),
                                          experts_of(weight, r, tt, g, p), ALU.mult).then_inc(sw_ready[L], 1)

                def group(g, last):
                    for p in range(2):
                        slot_weights(g, p)
                        if p == 0 and not last:
                            dve.wait_ge(sw_ready[L], nt * (2 * g + 1))
                            dve.wait_ge(gth_pe[L], g * 4 + 2)
                            build(g + 1, 0)
                        dve.wait_ge(silu_ok[L], g * 2 + p + 1)
                        dve.wait_ge(up_pe[L], g * 2 + p + 1)
                        dve.tensor_tensor(act_sb[:, p, :], act_sb[:, p, :], bank[:, 2 * p + 1, :], ALU.mult).then_inc(act_ok[L], 1)
                        dve.wait_ge(w_pe[L], g * 2 + p + 1)
                        c = 0 if nt == 3 else N_META
                        dve.tensor_copy(whotT[:, p, c:T], bank[:, 2 * p + 1, c:T]).then_inc(w_ev[L], 1)
                        if p == 1 and not last:
                            dve.wait_ge(sw_ready[L], nt * (2 * g + 2))
                            dve.wait_ge(gth_pe[L], g * 4 + 4)
                            build(g + 1, 1)
                        for i, (tt, n) in enumerate(scatter_order(L, last and p == 1)):
                            s = ns * p + i
                            dve.wait_ge(sc_pe[L], g * (2 * ns) + s + 1)
                            if tt == 2:
                                dve.tensor_tensor(ymeta, ymeta, bank[:, 4 + s % 2, 0:SEQ], ALU.add).then_inc(sc_ev[L], 1)
                            else:
                                y = yacc[:, tt, 512 * n:512 * (n + 1)]
                                dve.tensor_tensor(y, y, bank[:, 4 + s % 2, :], ALU.add).then_inc(sc_ev[L], 1)
                                if last and p == 1:
                                    dve.wait_ge(sc_ev[L], g * (2 * ns) + s + 2)
                                    dve.bn_stats(stats[:, tt, n, :], y).then_inc(st_ok, 1)
                                    if (tt, n) == (0, 1):
                                        norm_tile(2 * L + 1, 0, 0)

                build(0, 0)
                build(0, 1)
                overflow(L, nt)
                dve.wait_ge(yinit, (6, 8)[layer])
                late(dve, L)
                n = BASE_MOE[L] + NR
                dve.wait_ge(extra_in, 16 * (L + 1))
                dve.wait_ge(gate_pe[L], 1)
                dve.tensor_copy(ring[:, n % NR, :], extra).then_inc(ring_in[n % NR], 16)
                with dve.Fori(0, NG - 1) as g:
                    group(g, False)
                group(NG - 1, True)

            dve.memset(eps_ln, 1e-5)
            dve.memset(eps_rms, 1e-6)
            dve.memset(one, 1.0)
            dve.memset(lg[:, :, :], 0.0)
            dve.memset(slot_of[:, :, :], 0.0)
            link(dve.memset(ss0, 1.0))

            def level_masks():
                ge, xf = rt[:, 0, 0:P], rt[:, 0, P:2 * P]
                link(dve.tensor_tensor(ge, iota_i[:, 0:P], row_i[:, :], ALU.is_ge))
                link(dve.tensor_tensor(row_i[:, :], row_i[:, :], iota_i[:, 0:P], ALU.bitwise_xor))
                link(dve.tensor_scalar(xf, row_i[:, :], -4096.0, None, ALU.add))
                link(dve.tensor_tensor(xf, xf, ge, ALU.mult))
                link(dve.tensor_scalar(row_i[:, :], xf, 4096.0, None, ALU.add))
                for lv, w in enumerate(LEVELS):
                    link(dve.tensor_scalar(level_mask[:, lv, :], row_i[:, :], w.bit_length() - 1, None, ALU.logical_shift_right))
                    link(dve.tensor_scalar(level_mask[:, lv, :], level_mask[:, lv, :], 1.0, None, ALU.is_equal))
                link(dve.tensor_scalar(level_mask[:, len(LEVELS), :], row_i[:, :], 0.0, None, ALU.is_equal))

            for n in range(0, 8, 2):
                kind, m, _ = J0[n]
                if n == 4:
                    dve.wait_ge(const_ok, 6 + 3 + 4 + 2)
                    level_masks()
                dve.wait_ge(pj0_pe, n + 1)
                dve.tensor_copy((zq, zk)[kind == "K"][:, m, :], bank[:, n, 0:T]).then_inc(pj0_dve, 1)
            for g in range(4):
                dve.reciprocal(pcount[:, g, :], pcount[:, g, :]).then_inc(lam_s, 1)
            dve.wait_ge(par_in, 9 * 16)
            for k in range(2):
                link(dve.tensor_tensor(lam_t[:, k, :], lam_v[:, 2 * k, :], lam_v[:, 2 * k + 1, :], ALU.mult))
                dve.tensor_reduce((lam1, lam2)[k], lam_t[:, k, :], AX.X, ALU.add).then_inc(lam_e, 1)
            link(dve.tensor_scalar(sub_b[:, :], sub_b[:, :], 1.0 - LAMBDA_INIT, None, ALU.mult))

            def biased(i):
                tt, hp = STEPS[i]
                r, nk = ROWS[tt], C0[tt] + ROWS[tt]
                dve.wait_ge(at_s, i + 1)
                for j in range(2):
                    dve.scalar_tensor_tensor(s_sb[0:r, i % 2, 2 * j:2 * j + 2, 0:nk],
                                             dist[0:r, tt, 0:nk].unsqueeze(1).to_broadcast([r, 2, nk]),
                                             SLOPES[2 * hp + j] / ATT_SCALE,
                                             bank[0:r, 2 * j:2 * j + 2, 0:nk], ALU.mult, ALU.add).then_inc(at_b, 1)
                dve.wait_ge(at_b, 2 * i + 2)
                link(dve.tensor_reduce(mx[0:r, i, :], s_sb[0:r, i % 2, :, 0:nk], AX.X, ALU.max))
                dve.tensor_scalar(mx[0:r, i, :], mx[0:r, i, :], -ATT_SCALE, None, ALU.mult).then_inc(at_m, 1)

            def difference(i):
                tt, hp = STEPS[i]
                r, nk = ROWS[tt], C0[tt] + ROWS[tt]
                dve.wait_ge(at_e, 4 * i + 4)
                link(dve.reciprocal(rs[0:r, i, :], sums[0:r, i, :]))
                odd = rs[0:r, i, :].rearrange("p (j m) -> p j m", m=2)[:, :, 1]
                link(dve.tensor_scalar(odd, odd, nlam[0:r, :], None, ALU.mult))
                for j in range(2):
                    p1 = s_sb[0:r, i % 2, 2 * j + 1, 0:nk]
                    link(dve.tensor_scalar(p1, p1, rs[0:r, i, 2 * j + 1:2 * j + 2], None, ALU.mult))
                if i >= 1:
                    dve.wait_ge(at_t, i)
                for j in range(2):
                    dve.scalar_tensor_tensor(pd[0:r, j, 0:nk], s_sb[0:r, i % 2, 2 * j, 0:nk], rs[0:r, i, 2 * j:2 * j + 1],
                                             s_sb[0:r, i % 2, 2 * j + 1, 0:nk], ALU.mult, ALU.add).then_inc(at_pd, 1)

            def heads_out(i):
                tt, hp = STEPS[i]
                r = ROWS[tt]
                dve.wait_ge(at_o, i + 1)
                dve.tensor_copy(o_tok[0:r, tt, 2 * P * hp:2 * P * (hp + 1)], bank[0:r, 6, 0:2 * P]).then_inc(at_oe, 1)
                dve.wait_ge(at_oe, i + 1)
                for j in range(2):
                    h = 2 * hp + j
                    o = o_tok[0:r, tt, P * h:P * (h + 1)]
                    c = HEADS * tt + h
                    dve.tensor_tensor_reduce(out=sq0[0:r, :], in0=o, in1=o, scale=1.0, scalar=0.0, op0=ALU.mult,
                                             op1=ALU.add, accum_out=ss0[0:r, c:c + 1]).then_inc(o_ss, 1)
                    dve.wait_ge(o_ss, 2 * i + j + 1)

            biased(0)
            dve.wait_ge(act_c, 2)
            link(dve.tensor_tensor(nlam, lam2, lam1, ALU.subtract))
            link(dve.tensor_scalar(nlam, nlam, -LAMBDA_INIT, None, ALU.add))
            difference(0)
            for i in range(1, 6):
                biased(i)
                if i >= 2:
                    heads_out(i - 2)
                difference(i)
            heads_out(4)
            heads_out(5)
            dve.wait_ge(o_rs, 1)
            link(dve.reciprocal(rstd0, rstd0))
            for tt in (2, 0, 1):
                r = ROWS[tt]
                o = o_tok[0:r, tt, :].rearrange("p (h v) -> p h v", h=HEADS)
                link(dve.tensor_tensor(o, o, rstd0[0:r, HEADS * tt:HEADS * (tt + 1)].unsqueeze(2).to_broadcast([r, HEADS, P]), ALU.mult))
                dve.tensor_tensor(o, o, sub_b[0:r, :].unsqueeze(1).to_broadcast([r, HEADS, P]), ALU.mult).then_inc(o_n, 1)
            dve.wait_ge(yt_pe, 3)
            dve.tensor_copy(yT[:, 4:8, C0[1]:T], bank[:, 7, :].rearrange("p (h t) -> p h t", h=HEADS)).then_inc(yt_dve, 1)
            for i, tt in enumerate((2, 0, 1)):
                mix_tile((0, 1, 3)[i], tt)
                norm_tile(0, i, tt)
            dve.memset(ymeta, 0.0).then_inc(ym_zero, 1)
            link(dve.memset(yacc[0:N_META, 2, :], 0.0))
            router(0, (2, 0, 1))
            experts(0, (2, 0, 1))
            dve.wait_ge(ym_out, 4)
            link(dve.tensor_tensor(yacc[0:N_META, 2, :], yacc[0:N_META, 2, :], meta_row[0:N_META, :], ALU.add))
            norm_tile(1, 1, 2)
            norm_tile(1, 2, 1)

            dve.wait_ge(par1_in, 64)

            def job1(n):
                kind, m, by, b = J1[n]
                if by == "a":
                    return
                dve.wait_ge(pj1_pe, n + 1)
                if kind == "G":
                    dve.tensor_copy(glr[0:GLA_RANK, :], bank[0:GLA_RANK, b, 0:T]).then_inc(pj1_dve, 1)
                if kind == "A":
                    dve.tensor_scalar(bT[:, m, :], bank[:, b, 0:T], gb_sb[:, m:m + 1], None, ALU.add).then_inc(gla_ga, 1)
                    dve.wait_ge(gla_ga, m + 1)
                    dve.scalar_tensor_tensor(la[:, m, :], bT[:, m, :], -1.0, bT[:, m, :], ALU.mult, ALU.max).then_inc(gla_ab, 1)
                if kind == "Q":
                    dve.tensor_scalar(qT[:, m, :], bank[:, b, 0:SEQ], GLA_SCALE, None, ALU.mult).then_inc(pj1_dve, 1)
                if kind == "K":
                    dve.tensor_copy(kT[:, m, :], bank[:, b, 0:T]).then_inc(pj1_dve, 1)
                if kind in "VR":
                    half, tt = m
                    dve.tensor_copy((vt if kind == "V" else rt)[:, tt, 512 * half:512 * (half + 1)], bank[:, b, :]).then_inc(pj1_dve, 1)

            nl = len(LEVELS)
            for n in range(3, NLV):
                job1(n)
                if n == 11:
                    dve.wait_ge(gla_ln, 4)
                    link(dve.tensor_scalar(bT, bT, 0.0, None, ALU.min))
                    link(dve.tensor_tensor(la, bT, la, ALU.subtract))
                    link(dve.tensor_scalar(la, la, 1.0 / GLA_TAU, None, ALU.mult))
                    link(dve.memset(ql, 1.0))
                    for h in range(HEADS):
                        dve.tensor_tensor_scan(bT[:, h, :], ql.rearrange("p a b -> p (a b)")[:, 0:T], la[:, h, :], 0.0,
                                               ALU.mult, ALU.add).then_inc(gla_b, 1)
                    dve.wait_ge(gla_b, 4)
                    exponents(dve, 0, link)
                    link(dve.memset(att, 0.0))
                    dve.memset(kl, 0.0).then_inc(lv_k, 1)
            for st in range(nl + 3):
                if st < nl:
                    w = LEVELS[st]
                    dve.wait_ge(lv_e, st + 1)
                    if st:
                        dve.wait_ge(lv_pe, 2 * st)
                    dve.tensor_tensor(halves(ql, w)[:, :, :, w:2 * w], halves(qT, w)[:, :, :, w:2 * w],
                                      halves(dec, w)[:, :, :, w:2 * w], ALU.mult).then_inc(lv_q, 1)
                    dve.wait_ge(lv_q, st + 1)
                    dve.wait_ge(lv_k, st + 2)
                    exponents(dve, st + 1, link)
                if st == nl + 1:
                    dve.wait_ge(lv_e, nl + 1)
                    dve.wait_ge(lv_pe, 2 * nl)
                    link(dve.tensor_tensor(kl[:, :, 0:P], kT[:, :, N_META:N_META + P], dec[:, :, 0:P], ALU.mult))
                    dve.tensor_tensor(ql[:, :, P:SEQ], qT[:, :, P:SEQ], dec[:, :, P:SEQ], ALU.mult).then_inc(lv_q, 1)
                    dve.wait_ge(lv_q, nl + 1)
                    exponents(dve, nl + 1, link)
                if st < 2 or st % 2:
                    job1(NLV + (st if st < 2 else 1 + st // 2))
                if st <= nl:
                    attend(dve, st)
                if st == nl + 2:
                    dve.wait_ge(lv_e, nl + 3)
                    dve.wait_ge(lv_pe, 2 * (nl + 1) + 1)
                    link(dve.tensor_tensor(kl[:, :, 0:N_META], kT[:, :, 0:N_META], la[:, :, 0:N_META], ALU.mult))
                    dve.tensor_tensor(ql, qT, dec, ALU.mult).then_inc(lv_q, 1)
            for tt in range(2):
                for c in range(2):
                    dve.wait_ge(go_pe, 2 * tt + c + 1)
                    o = og[:, tt, 512 * c:512 * (c + 1)]
                    dve.tensor_copy(o, bank[:, 2 * tt + c, :]).then_inc(go_ev, 1)
                    dve.wait_ge(go_ev, 2 * tt + c + 1)
                    for h in (2 * c, 2 * c + 1):
                        oh = og[:, tt, GLA_DV * h:GLA_DV * (h + 1)]
                        j = HEADS * tt + h
                        dve.tensor_tensor_reduce(out=att[:, 0:2, :].rearrange("p a b -> p (a b)"), in0=oh, in1=oh, scale=1.0,
                                                 scalar=0.0, op0=ALU.mult, op1=ALU.add, accum_out=ss1[:, j:j + 1]).then_inc(o_ss, 1)
                        dve.wait_ge(o_ss, 12 + j + 1)
                heads = slice(HEADS * tt, HEADS * (tt + 1))
                dve.wait_ge(o_rs, tt + 2)
                link(dve.reciprocal(rstd1[:, heads], rstd1[:, heads]))
                dve.wait_ge(rg_ok, tt + 1)
                for h in range(HEADS):
                    c = slice(GLA_DV * h, GLA_DV * (h + 1))
                    j = HEADS * tt + h
                    dve.scalar_tensor_tensor(og[:, tt, c], og[:, tt, c], rstd1[:, j:j + 1], rt[:, tt, c],
                                             ALU.mult, ALU.mult).then_inc(ogt_ok, 1)
            for i in range(2):
                mix_tile(5 + 2 * i, i)
                norm_tile(2, i, i)
            router(1, (0, 1))
            experts(1, (0, 1))
            norm_tile(3, 1, 1)


_INS = ['x', 'meta', 'even_w_in', 'pool_w', 'pool_scale', 'diff_lq1', 'diff_lk1', 'diff_lq2', 'diff_lk2',
        'diff_subln', 'even_w_out', 'odd_w_in', 'gla_gate_w2', 'gla_gate_b', 'gla_head_norm', 'odd_w_out',
        'ln_mix_g', 'ln_mix_b', 'ln_ffn_g', 'ln_ffn_b', 'router_w', 'router_bias',
        'moe_w_gate', 'moe_w_up', 'moe_w_down']


def kernel(**inputs):
    import numpy as _np
    import concourse.bacc as _bacc
    from concourse import mybir as _mybir
    from concourse.bass_utils import run_bass_kernel_spmd as _run

    nc = _bacc.Bacc("TRN2", target_bir_lowering=False, num_devices=1)
    arrays, args = {}, []
    for name in _INS:
        a = _np.ascontiguousarray(inputs[name])
        arrays[f"in_{name}_dram"] = a
        args.append(nc.dram_tensor(f"in_{name}_dram", a.shape, _mybir.dt.from_np(a.dtype), kind="ExternalInput").ap())
    out = nc.dram_tensor("out_0_dram", (1, SEQ, D), _mybir.dt.float32, kind="ExternalOutput").ap()
    hybrid_trunk(nc, *args, out)
    r = _run(nc, [arrays], core_ids=[0])
    return r.results[0]["out_0_dram"]
```
